# Optimizing a Trainium2 kernel written in Bass

```python
import jax, jax.numpy as jnp
from jax import lax
import numpy as np

D_MODEL = 1024
BATCH = 1
SEQ = 2048
DEPTH = 2
DEC_BATCH = 8
DEC_SEQ = 8
PAST_LEN = 4096
PAGE_SIZE = 128

N_A = DEPTH // 2
N_B = DEPTH - N_A
D_CONV = D_MODEL
CONV_WIDTH = 31
CONV_STATE = CONV_WIDTH - 1
N_HEADS = 16
N_KV_HEADS = 4
HEAD_DIM = 64
GROUP = N_HEADS // N_KV_HEADS
D_ATTN = N_HEADS * HEAD_DIM
D_KV = N_KV_HEADS * HEAD_DIM
WINDOW = 128
Q_BLOCK = 128
RMS_EPS = 1e-6
LN_EPS = 1e-5

kernel_name = "yoco_conformer_conv_swa_sink_decoder_step"

def rms_norm(x, g):
    xf = x.astype(jnp.float32)
    y = xf * lax.rsqrt(jnp.mean(xf * xf, axis=-1, keepdims=True) + RMS_EPS)
    return (y * g.astype(jnp.float32)).astype(x.dtype)

def layer_norm(x, g, b):
    xf = x.astype(jnp.float32)
    mu = jnp.mean(xf, axis=-1, keepdims=True)
    xc = xf - mu
    var = jnp.mean(xc * xc, axis=-1, keepdims=True)
    return (xc * lax.rsqrt(var + LN_EPS) * g.astype(jnp.float32) + b.astype(jnp.float32)).astype(x.dtype)

def alibi_slopes():
    s = 2.0 ** (-8.0 * np.arange(1, N_HEADS + 1) / N_HEADS)
    return jnp.asarray(s, jnp.float32).reshape(N_KV_HEADS, GROUP)

def conv_mixer(x, prefix, g_norm, w_in, w_dw, b_dw, ln_g, ln_b, w_out):
    h = rms_norm(x, g_norm)
    u = jnp.einsum('btd,de->bte', h, w_in)
    a, gl, z = jnp.split(u, 3, axis=-1)
    v = a * jax.nn.sigmoid(gl)
    if prefix is None:
        prefix = jnp.zeros((x.shape[0], CONV_STATE, D_CONV), v.dtype)
    vfull = jnp.concatenate([prefix.astype(v.dtype), v], axis=1)
    c = lax.conv_general_dilated(
        vfull, w_dw[:, None, :].astype(v.dtype), window_strides=(1,), padding='VALID',
        dimension_numbers=('NWC', 'WIO', 'NWC'), feature_group_count=D_CONV)
    c = c + b_dw
    c = jax.nn.silu(layer_norm(c, ln_g, ln_b)) * jax.nn.silu(z)
    out = jnp.einsum('btc,cd->btd', c, w_out)
    return x + out, vfull[:, -CONV_STATE:]

def shared_kv(x, g_kv, w_kv, k_norm_g):
    b, t, _ = x.shape
    h = rms_norm(x, g_kv)
    kv = jnp.einsum('btd,de->bte', h, w_kv)
    k, v = jnp.split(kv, 2, axis=-1)
    k = rms_norm(k.reshape(b, t, N_KV_HEADS, HEAD_DIM), k_norm_g)
    return k, v.reshape(b, t, N_KV_HEADS, HEAD_DIM)

def query_side(x, g_norm, w_in, q_norm_g):
    b, t, _ = x.shape
    h = rms_norm(x, g_norm)
    u = jnp.einsum('btd,de->bte', h, w_in)
    q, z = jnp.split(u, 2, axis=-1)
    q = rms_norm(q.reshape(b, t, N_HEADS, HEAD_DIM), q_norm_g)
    return q, z

def band_attention(q, k_ctx, v_ctx, key_valid, sinks):
    b, tq = q.shape[:2]
    tk = k_ctx.shape[1]
    qg = q.reshape(b, tq, N_KV_HEADS, GROUP, HEAD_DIM)
    s = jnp.einsum('bqkgd,bskd->bkgqs', qg, k_ctx,
                   preferred_element_type=jnp.float32) * (HEAD_DIM ** -0.5)
    dist = jnp.arange(tq)[:, None] + WINDOW - jnp.arange(tk)[None, :]
    allowed = (dist >= 0) & (dist < WINDOW) & key_valid[None, :]
    s = s - alibi_slopes()[..., None, None] * dist.astype(jnp.float32)
    s = jnp.where(allowed, s, -jnp.inf)
    sink = sinks.astype(jnp.float32).reshape(N_KV_HEADS, GROUP)[..., None, None]
    m = jnp.maximum(jnp.max(s, axis=-1, keepdims=True), sink)
    p = jnp.exp(s - m)
    denom = jnp.sum(p, axis=-1, keepdims=True) + jnp.exp(sink - m)
    p = (p / denom).astype(v_ctx.dtype)
    o = jnp.einsum('bkgqs,bskd->bqkgd', p, v_ctx)
    return o.reshape(b, tq, D_ATTN)

def prompt_attention(q, k, v, sinks):
    b, t = q.shape[:2]
    nb = t // Q_BLOCK
    span = WINDOW + Q_BLOCK
    pad = ((0, 0), (WINDOW, 0), (0, 0), (0, 0))
    kp = jnp.pad(k, pad)
    vp = jnp.pad(v, pad)

    def block(i):
        start = i * Q_BLOCK
        qb = lax.dynamic_slice_in_dim(q, start, Q_BLOCK, axis=1)
        kb = lax.dynamic_slice_in_dim(kp, start, span, axis=1)
        vb = lax.dynamic_slice_in_dim(vp, start, span, axis=1)
        valid = (start - WINDOW + jnp.arange(span)) >= 0
        return band_attention(qb, kb, vb, valid, sinks)

    o = lax.map(block, jnp.arange(nb))
    return jnp.moveaxis(o, 0, 1).reshape(b, t, D_ATTN)

def attn_output(x, o, z, w_out):
    return x + jnp.einsum('bte,ed->btd', o * jax.nn.silu(z), w_out)

def setup_inputs(seed: int = 0) -> dict:
    key = jax.random.key(seed)
    ks = jax.random.split(key, 24)
    f32 = jnp.float32

    def nrm(k, shape, scale):
        return jax.random.normal(k, shape, f32) * scale

    def gain(k, shape):
        return 1.0 + 0.01 * jax.random.normal(k, shape, f32)

    return {
        "x_prompt": nrm(ks[0], (BATCH, SEQ, D_MODEL), 1.0),
        "x_sample": nrm(ks[1], (DEC_BATCH, DEC_SEQ, D_MODEL), 1.0),
        "state_conv": nrm(ks[2], (N_A, DEC_BATCH, CONV_STATE, D_CONV), 0.5),
        "cache_k": nrm(ks[3], (DEC_BATCH, WINDOW, N_KV_HEADS, HEAD_DIM), 1.0),
        "cache_v": nrm(ks[4], (DEC_BATCH, WINDOW, N_KV_HEADS, HEAD_DIM), 1.0),
        "norm_a": gain(ks[5], (N_A, D_MODEL)),
        "w_in_a": nrm(ks[6], (N_A, D_MODEL, 3 * D_CONV), D_MODEL ** -0.5),
        "w_dw_a": nrm(ks[7], (N_A, CONV_WIDTH, D_CONV), CONV_WIDTH ** -0.5),
        "b_dw_a": nrm(ks[8], (N_A, D_CONV), 0.01),
        "ln_g_a": gain(ks[9], (N_A, D_CONV)),
        "ln_b_a": nrm(ks[10], (N_A, D_CONV), 0.01),
        "w_out_a": nrm(ks[11], (N_A, D_CONV, D_MODEL), D_CONV ** -0.5),
        "norm_kv": gain(ks[12], (D_MODEL,)),
        "w_kv": nrm(ks[13], (D_MODEL, 2 * D_KV), D_MODEL ** -0.5),
        "k_norm": gain(ks[14], (HEAD_DIM,)),
        "norm_b": gain(ks[15], (N_B, D_MODEL)),
        "w_in_b": nrm(ks[16], (N_B, D_MODEL, 2 * D_ATTN), D_MODEL ** -0.5),
        "q_norm": gain(ks[17], (N_B, HEAD_DIM)),
        "sinks_b": nrm(ks[18], (N_B, N_HEADS), 1.0),
        "w_out_b": nrm(ks[19], (N_B, D_ATTN, D_MODEL), D_ATTN ** -0.5),
    }

def reference(x_prompt, x_sample, state_conv, cache_k, cache_v,
              norm_a, w_in_a, w_dw_a, b_dw_a, ln_g_a, ln_b_a, w_out_a,
              norm_kv, w_kv, k_norm,
              norm_b, w_in_b, q_norm, sinks_b, w_out_b):
    xp, xs = x_prompt, x_sample
    conv_p, conv_s = [], []
    kp = vp = kctx_s = vctx_s = None
    for layer in range(DEPTH):
        if layer < N_A:
            i = layer
            args = (norm_a[i], w_in_a[i], w_dw_a[i], b_dw_a[i], ln_g_a[i], ln_b_a[i], w_out_a[i])
            xp, st_p = conv_mixer(xp, None, *args)
            xs, st_s = conv_mixer(xs, state_conv[i], *args)
            conv_p.append(st_p)
            conv_s.append(st_s)
        else:
            j = layer - N_A
            if j == 0:
                kp, vp = shared_kv(xp, norm_kv, w_kv, k_norm)
                kn, vn = shared_kv(xs, norm_kv, w_kv, k_norm)
                kctx_s = jnp.concatenate([cache_k.astype(kn.dtype), kn], axis=1)
                vctx_s = jnp.concatenate([cache_v.astype(vn.dtype), vn], axis=1)
            qp, zp = query_side(xp, norm_b[j], w_in_b[j], q_norm[j])
            op = prompt_attention(qp, kp, vp, sinks_b[j])
            xp = attn_output(xp, op, zp, w_out_b[j])
            qs, zs = query_side(xs, norm_b[j], w_in_b[j], q_norm[j])
            valid_s = jnp.ones((kctx_s.shape[1],), bool)
            os_ = band_attention(qs, kctx_s, vctx_s, valid_s, sinks_b[j])
            xs = attn_output(xs, os_, zs, w_out_b[j])
    new_conv_prompt = jnp.stack(conv_p, axis=0)
    new_conv_sample = jnp.stack(conv_s, axis=0)
    new_k_prompt = kp[:, -WINDOW:]
    new_v_prompt = vp[:, -WINDOW:]
    new_k_sample = kctx_s[:, -WINDOW:]
    new_v_sample = vctx_s[:, -WINDOW:]
    return (xp, xs, new_conv_prompt, new_conv_sample, new_k_prompt, new_v_prompt, new_k_sample, new_v_sample)


_drawn_inputs = setup_inputs


def setup_inputs(seed=0):
    import zlib

    import numpy as np

    out = dict(_drawn_inputs(seed))
    spreads = {}
    factors = {'norm_a': 4.985,
     'b_dw_a': 8.0,
     'ln_g_a': 8.0,
     'ln_b_a': 8.0,
     'norm_kv': 5.759,
     'k_norm': 5.874,
     'norm_b': 8.0,
     'q_norm': 8.0,
     'sinks_b': 8.0}
    for name, (base, spread) in spreads.items():
        noise = np.random.default_rng([zlib.crc32(name.encode()), seed]).standard_normal(out[name].shape)
        drawn = base * np.exp(spread * noise) if base else spread * noise
        out[name] = __import__('jax').numpy.asarray(drawn.astype(out[name].dtype))
    for name, factor in factors.items():
        out[name] = (out[name] * factor).astype(out[name].dtype)
    return out
```

```python
from contextlib import ExitStack

import numpy as np

import concourse.bass as bass
from concourse import mybir

F32 = mybir.dt.float32
F32R = mybir.dt.float32r
ALU = mybir.AluOpType
ACT = mybir.ActivationFunctionType
AX_X = mybir.AxisListType.X

P = 128
D = 1024
KT = D // P
SEQ = 2048
TILES = SEQ // P
DB, DS = 8, 8
DEC = DB * DS
TOK = SEQ + DEC
ALL = TILES + 1
TAPS = 31
VECS = 6
HIST = TAPS - 1
HALF = 512
CT = HALF // P
CHUNK = 4
CTOK = CHUNK * P
NCHUNK = TILES // CHUNK
HEADS, KVH, HD = 16, 4, 64
GROUP = HEADS // KVH
KV = KVH * HD
RMS_EPS = 1e-6
LN_EPS = 1e-5


class Names:
    pass


def after(eng, sem, count):
    if isinstance(count, int) and count <= 0:
        return
    eng.wait_ge(sem, count)


def rows_of(tile):
    return DEC if isinstance(tile, int) and tile % ALL == TILES else P


def f32(ap):
    return ap.bitcast(F32)


def token_rows(dram, t, n):
    return dram[bass.ds(t * P, n), :] if not isinstance(t, int) else dram[t * P:t * P + n, :]


STAGES = 4


def split_weights_dma(sp, weights, g, n0):
    for k in range(KT):
        piece = KT * n0 + k
        after(sp, g.w_lo, piece - STAGES + 1)
        sp.dma_start(g.stage[:, piece % STAGES], weights[k * P:(k + 1) * P, :]).then_inc(g.w_in[piece % STAGES], 16)


def split_weights_hi(act, m, gain, g, n0, free=None):
    if free is not None:
        act.wait_ge(*free)
    for k in range(KT):
        piece = KT * n0 + k
        act.wait_ge(g.w_in[piece % STAGES], 16 * (piece // STAGES + 1))
        scale = 1.0 if gain is None else gain[:, k:k + 1]
        act.activation(g.wslot[m][:, 0, k], g.stage[:, piece % STAGES], ACT.Copy, scale=scale).then_inc(g.w_hi, 1)


def split_weights_lo(dve, m, gain, g, n0):
    for k in range(KT):
        piece = KT * n0 + k
        dve.wait_ge(g.w_hi, piece + 1)
        dve.scalar_tensor_tensor(g.wslot[m][:, 1, k], g.stage[:, piece % STAGES],
                                 1.0 if gain is None else gain[:, k:k + 1], f32(g.wslot[m][:, 0, k]),
                                 ALU.mult, ALU.subtract).then_inc(g.w_lo, 1)


def project(pe, out, xt, w, n, lo_gate=None):
    for k in range(KT):
        if lo_gate is not None:
            pe.wait_ge(lo_gate[0], lo_gate[1] + k + 1)
        for a, b in ((0, 0), (1, 0), (0, 1)):
            last = pe.matmul(out, xt[:, a, k, 0:n], w[:, b, k], start=(k == 0 and a == 0 and b == 0),
                             stop=(k == KT - 1 and b == 1))
    return last


def phase_a(nc, io, g):
    with ExitStack() as ctx:
        sb = lambda name, shape, dt=F32: ctx.enter_context(nc.sbuf_tensor(name, shape, dt))
        pb = lambda name, shape: ctx.enter_context(nc.psum_tensor(name, shape, F32))
        sem = lambda name: ctx.enter_context(nc.semaphore(name))

        g.wslot = [sb(f"a_w{m}", [P, 2, KT, HALF], F32R) for m in range(3)]
        g.stage = sb("a_stage", [P, STAGES, HALF])
        x = sb("a_x", [P, 2, D])
        xs = sb("a_xs", [P, D])
        xt = [sb(f"a_xt{p}", [P, 2, KT, P], F32R) for p in range(2)]
        sig = sb("a_sig", [P, HALF])
        v = sb("a_v", [P, 2, HALF])
        zo = sb("a_zo", [P, 2, HALF])
        vbuf = sb("a_vbuf", [P, CT, HIST + SEQ])
        vdec = sb("a_vdec", [P, KT, DB, HIST + DS])
        acc = sb("a_acc", [P, CT, CTOK])
        dacc = sb("a_dacc", [P, CT, DEC])
        raw = sb("a_raw", [P, 3, P])
        ss = sb("a_ss", [P, 2])
        ms = sb("a_ms", [P, 2])
        rstd = sb("a_rstd", [P, 2])

        ps_t = pb("a_pst", [P, KT, P])
        ps_g, ps_a, ps_z = (pb(f"a_ps{n}", [P, HALF]) for n in "gaz")
        ps_v = pb("a_psv", [P, CT, P])

        g.w_in = [sem(f"a_w_in{b}") for b in range(STAGES)]
        g.w_hi, g.w_lo = sem("a_w_hi"), sem("a_w_lo")
        x_in = [sem("a_x_in0"), sem("a_x_in1")]
        v_out = [sem("a_v_out0"), sem("a_v_out1")]
        z_out = [sem("a_z_out0"), sem("a_z_out1")]
        (raw_in, st_in, eps_made, ident_made, cols_t, cols_ready, hist_zero, st_t, st_copied, ss_ready, ms_ready, rstd_ready,
         xs_ready, xt_done, hi_ready, lo_ready, g_mm, a_mm, z_mm, sig_ready, v_ready, z_copied, vt_done, vt_copied,
         conv_step, dec_step, c_out, d_out, copy_out) = (sem("a_" + s) for s in (
             "raw_in st_in eps_made ident_made cols_t cols_ready hist_zero st_t st_copied ss_ready ms_ready rstd_ready "
             "xs_ready xt_done hi_ready lo_ready g_mm a_mm z_mm sig_ready v_ready z_copied vt_done vt_copied "
             "conv_step dec_step c_out d_out copy_out").split())

        w_in = io.w_in_a
        GATE, VALUE, ZGATE = 0, 1, 2
        col = lambda s, m: ((D, 0, 2 * D)[m]) + s * HALF
        na = g.cols[:, 0:KT]
        wcol = lambda k, ch: g.taps[:, k * KT + ch:k * KT + ch + 1]
        bcol = lambda ch: g.cols[:, 3 * KT + ch:3 * KT + ch + 1]
        block = ctx.enter_context(nc.Block())

        @block.sync
        def _(sp):
            taps = io.w_dw_a.rearrange("w (j p) -> (w j) p", p=P)
            sp.dma_start(raw[:, 0], taps[0:P, :]).then_inc(raw_in, 16)
            sp.dma_start(raw[0:TAPS * KT - P, 1], taps[P:TAPS * KT, :]).then_inc(raw_in, 16)
            for n, vec in enumerate((io.norm_a, io.norm_kv, io.norm_b, io.b_dw_a, io.ln_g_a, io.ln_b_a)):
                sp.dma_start(raw[n * KT:(n + 1) * KT, 2], vec.rearrange("(j p) -> j p", p=P)).then_inc(raw_in, 16)
            for h in range(2):
                sp.dma_start(g.qgain[h * HD:(h + 1) * HD, :], io.q_norm.rearrange("(p a) -> p a", a=1)).then_inc(raw_in, 16)
            state = io.state.rearrange("b w c -> (b w) c")
            for h in range(2):
                sp.dma_start(x[0:DB * HIST // 2, h], state[h * DB * HIST // 2:(h + 1) * DB * HIST // 2, :]).then_inc(st_in, 16)
            sp.dma_start(io.conv_s[:, 0:HIST - DS, :], io.state[:, DS:HIST, :]).then_inc(copy_out, 16)

            def load_x(T, t, p):
                if isinstance(T, int) and T < 2:
                    sp.wait_ge(st_t, T + 1)
                after(sp, xs_ready, T - 1)
                n = rows_of(t)
                src = io.x_sample if n == DEC else token_rows(io.x_prompt, t, n)
                sp.dma_start(x[0:n, p], src).then_inc(x_in[p], 16)

            def store(T, t, p, s):
                n = rows_of(t)
                sp.wait_ge(z_copied, T + 1)
                sp.dma_start(token_rows(g.z_d, t, n)[:, s * HALF:(s + 1) * HALF], zo[0:n, p]).then_inc(z_out[p], 16)

            def store_state(T, t, p, s):
                sp.wait_ge(v_ready, T + 1)
                cols = slice(s * HALF, (s + 1) * HALF)
                if t == TILES:
                    for b in range(DB):
                        sp.dma_start(io.conv_s[b, HIST - DS:HIST, cols], v[b * DS:(b + 1) * DS, p]).then_inc(v_out[p], 16)
                else:
                    sp.dma_start(io.conv_p[:, cols], v[P - HIST:P, p]).then_inc(v_out[p], 16)

            def store_c(gc, c, s):
                for j in range(CT):
                    sp.wait_ge(conv_step, gc * TAPS * CT + (TAPS - 1) * CT + j + 1)
                    dst = g.c_d[(s * CT + j) * P:(s * CT + j + 1) * P, :]
                    dst = dst[:, bass.ds(c * CTOK, CTOK)] if not isinstance(c, int) else dst[:, c * CTOK:(c + 1) * CTOK]
                    sp.dma_start(dst, acc[:, j]).then_inc(c_out, 16)

            def store_dec(s):
                for j in range(CT):
                    sp.wait_ge(dec_step, s * TAPS * CT + (TAPS - 1) * CT + j + 1)
                    sp.dma_start(g.c_d[(s * CT + j) * P:(s * CT + j + 1) * P, SEQ:TOK], dacc[:, j]).then_inc(d_out, 16)

            load_x(0, 0, 0)
            load_x(1, 1, 1)
            for s in range(2):
                for m in range(3):
                    split_weights_dma(sp, w_in[:, col(s, m):col(s, m) + HALF], g, 3 * s + m)
                B = s * ALL
                for t in range(CHUNK):
                    load_x(B + t + 2, t + 2, (B + t) % 2)
                    store(B + t, t, (B + t) % 2, s)
                if s:
                    store_c(NCHUNK - 1, NCHUNK - 1, 0)
                    store_dec(0)
                with sp.Fori(1, NCHUNK - 1) as c:
                    for q in range(CHUNK):
                        load_x(B + c * CHUNK + q + 2, c * CHUNK + q + 2, (B + q) % 2)
                        store(B + c * CHUNK + q, c * CHUNK + q, (B + q) % 2, s)
                    store_c(s * NCHUNK + c - 1, c - 1, s)
                for t in range(TILES - CHUNK, TILES):
                    if B + t + 2 < 2 * ALL:
                        load_x(B + t + 2, (t + 2) % ALL, (B + t) % 2)
                    store(B + t, t, (B + t) % 2, s)
                store_state(B + TILES - 1, TILES - 1, (B + TILES - 1) % 2, s)
                store_c(s * NCHUNK + NCHUNK - 2, NCHUNK - 2, s)
                if s == 0:
                    load_x(ALL + 1, 1, (ALL + 1) % 2)
                store(B + TILES, TILES, (B + TILES) % 2, s)
                store_state(B + TILES, TILES, (B + TILES) % 2, s)
            store_c(2 * NCHUNK - 1, NCHUNK - 1, 1)
            store_dec(1)
            sp.wait_ge(c_out, 16 * 2 * NCHUNK * CT)
            sp.wait_ge(d_out, 16 * 2 * CT)
            for p in range(2):
                sp.wait_ge(z_out[p], 16 * ALL)
                sp.wait_ge(v_out[p], 16 * (1 + DB))
            sp.wait_ge(copy_out, 16)

        @block.gpsimd
        def _(pool):
            pool.memset(g.half[:, :], -0.5).then_inc(ident_made, 1)
            pool.memset(g.rms_eps[:, :], RMS_EPS)
            pool.memset(g.ln_eps[:, :], LN_EPS).then_inc(eps_made, 1)
            pool.wait_ge(eps_made, 1)
            pool.memset(g.ident[:, :], 0.0).then_inc(ident_made, 1)
            pool.wait_ge(ident_made, 2)
            pool.affine_select(out=g.ident[:, :], in_=g.ident[:, :], compare_op=ALU.not_equal, fill=1.0, base=0,
                               pattern=[[-1, P]], channel_multiplier=1).then_inc(ident_made, 1)
            pool.memset(vbuf[:, :, 0:HIST], 0.0).then_inc(hist_zero, 1)

            def rms(T, t, p):
                n = rows_of(t)
                pool.wait_ge(ss_ready, T + 1)
                after(pool, xs_ready, T - 1)
                pool.tensor_tensor(ms[0:n, p:p + 1], ss[0:n, p:p + 1], g.rms_eps[0:n, 0:1], ALU.add).then_inc(ms_ready, 1)
                pool.wait_ge(ms_ready, T + 1)
                pool.tensor_tensor(rstd[0:n, p:p + 1], ms[0:n, p:p + 1], g.half[0:n, 0:1], ALU.pow).then_inc(rstd_ready, 1)

            for s in range(2):
                B = s * ALL
                for q in range(2):
                    rms(B + q, q, (B + q) % 2)
                with pool.Fori(1, TILES // 2) as i:
                    for q in range(2):
                        rms(B + i * 2 + q, i * 2 + q, (B + q) % 2)
                rms(B + TILES, TILES, (B + TILES) % 2)

        def scale_x(act, T, t, p):
            n = rows_of(t)
            act.wait_ge(x_in[p], 16 * (T // 2 + 1) if isinstance(T, int) else p_uses(T, p))
            after(act, xt_done, T)
            act.activation(xs[0:n], x[0:n, p], ACT.Square, scale=D ** -0.5, accum_out=ss[0:n, p:p + 1]).then_inc(ss_ready, 1)
            act.wait_ge(rstd_ready, T + 1)
            act.activation(xs[0:n], x[0:n, p], ACT.Copy, scale=rstd[0:n, p:p + 1]).then_inc(xs_ready, 1)

        def p_uses(T, p):
            return T * 8 + (16 if p == 0 else 8)

        def cut_hi(act, T, t, p):
            n = rows_of(t)
            act.wait_ge(xt_done, T + 1)
            after(act, z_mm, T - 1)
            act.activation(xt[p][:, 0, :, 0:n], ps_t[:, :, 0:n], ACT.Copy).then_inc(hi_ready, 1)

        @block.scalar
        def _(act):
            act.wait_ge(cols_t, 1)
            act.activation(g.taps[:, :], ps_g[:, 0:TAPS * KT], ACT.Copy).then_inc(cols_ready, 1)
            act.activation(g.cols[:, :], ps_g[:, 256:256 + VECS * KT], ACT.Copy).then_inc(cols_ready, 1)
            for h in range(2):
                act.wait_ge(st_t, h + 1)
                dst = vdec[:, :, h * DB // 2:(h + 1) * DB // 2, 0:HIST]
                src = ps_t[:, :, 0:DB * HIST // 2].rearrange("p k (b w) -> p k b w", w=HIST)
                for j in range(KT):
                    last = act.activation(dst[:, j], src[:, j], ACT.Copy)
                last.then_inc(st_copied, 1)
            scale_x(act, 0, 0, 0)
            cut_hi(act, 0, 0, 0)

            def body(T, t, p, s):
                last = isinstance(T, int) and T == 2 * ALL - 1
                n = rows_of(t)
                if not last:
                    tn = (t + 1) % ALL if isinstance(t, int) else t + 1
                    scale_x(act, T + 1, tn, 1 - p)
                act.wait_ge(g_mm, T + 1)
                after(act, v_ready, T)
                act.activation(sig[0:n], ps_g[0:n], ACT.Sigmoid).then_inc(sig_ready, 1)
                if not last:
                    cut_hi(act, T + 1, tn, 1 - p)
                act.wait_ge(z_mm, T + 1)
                if not (isinstance(T, int) and T < 2):
                    act.wait_ge(z_out[p], p_uses(T - 2, p) if not isinstance(T, int) else 16 * (T // 2))
                act.activation(zo[0:n, p], ps_z[0:n], ACT.Copy).then_inc(z_copied, 1)
                act.wait_ge(vt_done, T + 1)
                if n == DEC:
                    for j in range(CT):
                        ins = act.activation(vdec[:, s * CT + j, :, HIST:], ps_v[:, j, 0:DEC].rearrange("p (b w) -> p b w", w=DS), ACT.Copy)
                else:
                    if s:
                        done = NCHUNK - 1 if isinstance(t, int) and t < CHUNK else NCHUNK
                        act.wait_ge(conv_step, done * TAPS * CT)
                    dst = vbuf[:, :, HIST + t * P:HIST + (t + 1) * P] if isinstance(t, int) else vbuf[:, :, bass.ds(t * P + HIST, P)]
                    ins = act.activation(dst, ps_v[:, :, :], ACT.Copy)
                ins.then_inc(vt_copied, 1)

            for s in range(2):
                B = s * ALL
                for m in range(3):
                    split_weights_hi(act, m, na, g, 3 * s + m, free=((g_mm, a_mm, z_mm)[m], ALL) if s else None)
                for t in range(CHUNK):
                    body(B + t, t, (B + t) % 2, s)
                with act.Fori(CHUNK // 2, TILES // 2) as i:
                    for q in range(2):
                        body(B + i * 2 + q, i * 2 + q, (B + q) % 2, s)
                body(B + TILES, TILES, (B + TILES) % 2, s)

        @block.vector
        def _(dve):
            dve.wait_ge(cols_ready, 2)

            def cut_lo(T, t, p):
                n = rows_of(t)
                dve.wait_ge(hi_ready, T + 1)
                dve.tensor_tensor(xt[p][:, 1, :, 0:n], ps_t[:, :, 0:n], f32(xt[p][:, 0, :, 0:n]), ALU.subtract).then_inc(lo_ready, 1)

            def gate(T, t, p):
                n = rows_of(t)
                dve.wait_ge(sig_ready, T + 1)
                dve.wait_ge(a_mm, T + 1)
                after(dve, vt_done, T - 1)
                if isinstance(T, int) and T % ALL < 2 and T >= ALL:
                    dve.wait_ge(v_out[0], 16 * DB)
                    dve.wait_ge(v_out[1], 16)
                dve.tensor_tensor(v[0:n, p], ps_a[0:n], sig[0:n], ALU.mult).then_inc(v_ready, 1)

            def conv(gc, c, s, k0, k1):
                for k in range(k0, k1):
                    for j in range(CT):
                        win = vbuf[:, j, c * CTOK + k:c * CTOK + k + CTOK] if isinstance(c, int) else vbuf[:, j, bass.ds(c * CTOK + k, CTOK)]
                        if k == 0:
                            after(dve, c_out, gc * 16 * CT)
                            dve.tensor_scalar(acc[:, j], win, wcol(k, s * CT + j), bcol(s * CT + j), ALU.mult, ALU.add).then_inc(conv_step, 1)
                        else:
                            dve.wait_ge(conv_step, gc * TAPS * CT + (k - 1) * CT + j + 1)
                            dve.scalar_tensor_tensor(acc[:, j], win, wcol(k, s * CT + j), acc[:, j], ALU.mult, ALU.add).then_inc(conv_step, 1)

            def dec_conv(s, k0, k1):
                for k in range(k0, k1):
                    for j in range(CT):
                        win = vdec[:, s * CT + j, :, k:k + DS]
                        out = dacc[:, j].rearrange("p (b w) -> p b w", w=DS)
                        if k == 0:
                            after(dve, d_out, 16 * s * CT)
                            dve.tensor_scalar(out, win, wcol(k, s * CT + j), bcol(s * CT + j), ALU.mult, ALU.add).then_inc(dec_step, 1)
                        else:
                            dve.wait_ge(dec_step, (s * TAPS + k - 1) * CT + j + 1)
                            dve.scalar_tensor_tensor(out, win, wcol(k, s * CT + j), out, ALU.mult, ALU.add).then_inc(dec_step, 1)

            cut_lo(0, 0, 0)
            for s in range(2):
                B = s * ALL
                for m in range(3):
                    split_weights_lo(dve, m, na, g, 3 * s + m)

                def step(T, t, p, q, gc, c, cs, dec=False):
                    gate(T, t, p)
                    if gc is not None:
                        conv(gc, c, cs, 8 * q, 8 * q + 4)
                        if dec:
                            dec_conv(0, 8 * q, 8 * q + 4)
                    cut_lo(T + 1, (t + 1) % ALL if isinstance(t, int) else t + 1, 1 - p)
                    if gc is not None:
                        conv(gc, c, cs, 8 * q + 4, min(8 * q + 8, TAPS))
                        if dec:
                            dec_conv(0, 8 * q + 4, min(8 * q + 8, TAPS))

                if s:
                    dve.wait_ge(vt_copied, ALL)
                else:
                    dve.wait_ge(hist_zero, 1)
                for q in range(CHUNK):
                    if s:
                        step(B + q, q, (B + q) % 2, q, NCHUNK - 1, NCHUNK - 1, 0, dec=True)
                    else:
                        step(B + q, q, (B + q) % 2, q, None, None, None)

                def chunk(c):
                    dve.wait_ge(vt_copied, B + c * CHUNK)
                    for q in range(CHUNK):
                        step(B + c * CHUNK + q, c * CHUNK + q, (B + q) % 2, q, s * NCHUNK + c - 1, c - 1, s)

                chunk(1)
                with dve.Fori(2, NCHUNK) as c:
                    chunk(c)
                gate(B + TILES, TILES, (B + TILES) % 2)
                if s == 0:
                    cut_lo(ALL, 0, ALL % 2)
            dve.wait_ge(vt_copied, 2 * ALL)
            conv(2 * NCHUNK - 1, NCHUNK - 1, 1, 0, TAPS)
            dec_conv(1, 0, TAPS)

        @block.tensor
        def _(pe):
            pe.wait_ge(ident_made, 3)
            pe.wait_ge(raw_in, 16 * (2 + VECS + 2))
            pe.transpose(ps_g[:, 0:P], raw[:, 0], g.ident[:, :])
            pe.transpose(ps_g[:, P:TAPS * KT], raw[0:TAPS * KT - P, 1], g.ident[0:TAPS * KT - P, 0:TAPS * KT - P])
            pe.transpose(ps_g[:, 256:256 + VECS * KT], raw[0:VECS * KT, 2], g.ident[0:VECS * KT, 0:VECS * KT]).then_inc(cols_t, 1)
            pe.wait_ge(st_in, 32)
            n = DB * HIST // 2
            for h in range(2):
                after(pe, st_copied, h)
                for k in range(KT):
                    last = pe.transpose(ps_t[:, k, 0:n], x[0:n, h, k * P:(k + 1) * P], g.ident[0:n, 0:n])
                last.then_inc(st_t, 1)
            pe.wait_ge(st_copied, 2)

            def turn_x(T, t, p):
                n = rows_of(t)
                pe.wait_ge(xs_ready, T + 1)
                after(pe, lo_ready, T)
                for k in range(KT):
                    last = pe.transpose(ps_t[:, k, 0:n], xs[0:n, k * P:(k + 1) * P], g.ident[0:n, 0:n])
                last.then_inc(xt_done, 1)

            def body(T, t, p, s):
                n = rows_of(t)
                first = isinstance(t, int) and t == 0
                gate_of = lambda m: (g.w_lo, KT * (3 * s + m)) if first else None
                pe.wait_ge(lo_ready, T + 1)
                after(pe, sig_ready, T)
                if isinstance(T, int) and T == 0:
                    pe.wait_ge(cols_ready, 2)
                project(pe, ps_g[0:n], xt[p], g.wslot[GATE], n, gate_of(GATE)).then_inc(g_mm, 1)
                after(pe, v_ready, T)
                project(pe, ps_a[0:n], xt[p], g.wslot[VALUE], n, gate_of(VALUE)).then_inc(a_mm, 1)
                if not (isinstance(T, int) and T == 2 * ALL - 1):
                    turn_x(T + 1, (t + 1) % ALL if isinstance(t, int) else t + 1, 1 - p)
                after(pe, z_copied, T)
                project(pe, ps_z[0:n], xt[p], g.wslot[ZGATE], n, gate_of(ZGATE)).then_inc(z_mm, 1)
                pe.wait_ge(v_ready, T + 1)
                after(pe, vt_copied, T)
                for j in range(CT):
                    last = pe.transpose(ps_v[:, j, 0:n], v[0:n, p, j * P:(j + 1) * P], g.ident[0:n, 0:n])
                last.then_inc(vt_done, 1)

            turn_x(0, 0, 0)
            for s in range(2):
                B = s * ALL
                for t in range(2):
                    body(B + t, t, (B + t) % 2, s)
                with pe.Fori(1, TILES // 2 - 1) as i:
                    for q in range(2):
                        body(B + i * 2 + q, i * 2 + q, (B + q) % 2, s)
                for t in range(TILES - 2, ALL):
                    body(B + t, t, (B + t) % 2, s)


def phase_b(nc, io, g):
    with ExitStack() as ctx:
        sb = lambda name, shape, dt=F32: ctx.enter_context(nc.sbuf_tensor(name, shape, dt))
        pb = lambda name, shape: ctx.enter_context(nc.psum_tensor(name, shape, F32))
        sem = lambda name: ctx.enter_context(nc.semaphore(name))

        OUT0, OUT1, KVS, Q0, Q1 = range(5)
        g.wslot = [sb(f"b_w{m}", [P, 2, KT, HALF], F32R) for m in range(5)]
        c = sb("b_c", [P, KT, P])
        z = sb("b_z", [P, D])
        x = sb("b_x", [P, D])
        y = sb("b_y", [P, D])
        yc = y[:, :].rearrange("p (k n) -> p k n", k=KT)
        yt = sb("b_yt", [P, 2, KT, P], F32R)
        ht = sb("b_ht", [P, 2, KT, P], F32R)
        hq = sb("b_hq", [P, 2 * D])
        g.stage = hq[:, :].rearrange("p (s n) -> p s n", s=STAGES)
        h, qo = hq[:, 0:D], hq[:, D:2 * D]
        kvo = sb("b_kvo", [P, 2 * KV])
        kgain = sb("b_kgain", [P, HD])
        stats = sb("b_stats", [P, 2, 6])
        mv = sb("b_mv", [P, 2])
        pause = sb("b_pause", [P, 1])
        lms = sb("b_lms", [P, 1])
        lrs = sb("b_lrs", [P, 1])
        ss = sb("b_ss", [P, 1])
        ms = sb("b_ms", [P, 1])
        hss = sb("b_hss", [P, HEADS + KVH])
        hms = sb("b_hms", [P, HEADS + KVH])
        hrs = sb("b_hrs", [P, HEADS + KVH])

        ps_c = pb("b_psc", [P, D])
        ps_cc = ps_c[:, :].rearrange("p (k n) -> p k n", k=KT)
        ps_t = pb("b_pst", [P, KT, P])
        ps_o = pb("b_pso", [P, D])
        ps_q = pb("b_psq", [P, D])

        g.w_in = [sem(f"b_w_in{b}") for b in range(STAGES)]
        g.w_hi, g.w_lo = sem("b_w_hi"), sem("b_w_lo")
        (kg_in, c_in, z_in, x_in, x1_out, q_out, kv_out, copy_out, tc_done, tz_done, ty_done, th_done, out_mm, kv_mm,
         q_mm, stat_step, lms_ready, lrs_ready, yn_ready, sz_ready, y2_ready, prod_ready, yhi_ready, ylo_ready,
         x1_ready, ss_ready, ms_ready, rstd_ready, h_ready, hhi_ready, hlo_ready, ksq_ready, qsq_ready, v_ready,
         kss_ready, qss_ready, kms_ready, qms_ready, krs_ready, qrs_ready, kn_ready, k_ready, q_ready) = (
             sem("b_" + s) for s in (
                 "kg_in c_in z_in x_in x1_out q_out kv_out copy_out tc_done tz_done ty_done th_done out_mm kv_mm "
                 "q_mm stat_step lms_ready lrs_ready yn_ready sz_ready y2_ready prod_ready yhi_ready ylo_ready "
                 "x1_ready ss_ready ms_ready rstd_ready h_ready hhi_ready hlo_ready ksq_ready qsq_ready v_ready "
                 "kss_ready qss_ready kms_ready qms_ready krs_ready qrs_ready kn_ready k_ready q_ready").split())
        heads = lambda ap, m: ap.rearrange("p (h d) -> p h d", h=m)
        block = ctx.enter_context(nc.Block())

        def steady(eng, body):
            body(0)
            body(1)
            with eng.Fori(1, TILES // 2 - 1) as i:
                for q in range(2):
                    body(i * 2 + q)
            for t in range(TILES - 2, ALL):
                body(t)

        @block.sync
        def _(sp):
            sp.dma_start(kgain[:, :], io.k_norm.rearrange("(a d) -> a d", a=1).broadcast_to([P, HD])).then_inc(kg_in, 16)
            sp.dma_start(io.k_s[:, 0:P - DS, :], io.cache_k[:, DS:P, :]).then_inc(copy_out, 16)
            sp.dma_start(io.v_s[:, 0:P - DS, :], io.cache_v[:, DS:P, :]).then_inc(copy_out, 16)

            def load_c(t):
                after(sp, tc_done, t)
                n = rows_of(t)
                cols = slice(t * P, t * P + n) if isinstance(t, int) else bass.ds(t * P, P)
                sp.dma_start(c[:, :, 0:n], g.c_d.rearrange("(k p) n -> p k n", p=P)[:, :, cols]).then_inc(c_in, 16)

            def load_z(t):
                after(sp, tz_done, t)
                n = rows_of(t)
                sp.dma_start(z[0:n], token_rows(g.z_d, t, n)).then_inc(z_in, 16)

            def load_x(t):
                after(sp, x1_out, 16 * t)
                after(sp, h_ready, t)
                n = rows_of(t)
                sp.dma_start(x[0:n], io.x_sample if n == DEC else token_rows(io.x_prompt, t, n)).then_inc(x_in, 16)

            def store_x1(t):
                n = rows_of(t)
                sp.wait_ge(x1_ready, t + 1)
                sp.dma_start(token_rows(g.x1_d, t, n), x[0:n]).then_inc(x1_out, 16)

            def store_qkv(t):
                n = rows_of(t)
                sp.wait_ge(k_ready, t + 1)
                sp.wait_ge(v_ready, t + 1)
                sp.dma_start(token_rows(g.kv_d, t, n), kvo[0:n]).then_inc(kv_out, 16)
                if isinstance(t, int) and t == TILES - 1:
                    sp.dma_start(io.k_p, kvo[:, 0:KV]).then_inc(copy_out, 16)
                    sp.dma_start(io.v_p, kvo[:, KV:2 * KV]).then_inc(copy_out, 16)
                if n == DEC:
                    for b in range(DB):
                        rows = slice(b * DS, (b + 1) * DS)
                        sp.dma_start(io.k_s[b, P - DS:P, :], kvo[rows, 0:KV]).then_inc(copy_out, 16)
                        sp.dma_start(io.v_s[b, P - DS:P, :], kvo[rows, KV:2 * KV]).then_inc(copy_out, 16)
                sp.wait_ge(q_ready, t + 1)
                sp.dma_start(token_rows(g.q_d, t, n), qo[0:n]).then_inc(q_out, 16)

            load_c(0)
            load_z(0)
            load_x(0)
            for n, w in enumerate((io.w_out_a[:, 0:HALF], io.w_out_a[:, HALF:D], io.w_kv, io.w_in_b[:, 0:HALF],
                                   io.w_in_b[:, HALF:D])):
                split_weights_dma(sp, w, g, n)
            load_c(1)
            load_z(1)

            def body(t):
                store_x1(t)
                if not isinstance(t, int) or t + 1 < ALL:
                    load_x(t + 1)
                if not isinstance(t, int) or t + 2 < ALL:
                    load_c(t + 2)
                    load_z(t + 2)
                if not (isinstance(t, int) and t == 0):
                    store_qkv(t - 1)
            steady(sp, body)
            store_qkv(ALL - 1)
            sp.wait_ge(x1_out, 16 * ALL)
            sp.wait_ge(q_out, 16 * ALL)
            sp.wait_ge(kv_out, 16 * ALL)
            sp.wait_ge(copy_out, 16 * (2 + 2 + 2 * DB))

        @block.gpsimd
        def _(pool):
            def power(out, mid, src, n, eps, mid_ready, ready, t):
                after(pool, ready, t)
                pool.tensor_tensor(mid[0:n], src[0:n], eps[0:n, 0:out.shape[1]], ALU.add).then_inc(mid_ready, 1)
                pool.wait_ge(mid_ready, t + 1)
                pool.tensor_tensor(out[0:n], mid[0:n], g.half[0:n, 0:out.shape[1]], ALU.pow).then_inc(ready, 1)

            def layer(t):
                pool.wait_ge(stat_step, 3 * t + 3)
                after(pool, yn_ready, t)
                power(lrs[:, :], lms[:, :], mv[:, 1:2], rows_of(t), g.ln_eps, lms_ready, lrs_ready, t)

            def body(t):
                if not isinstance(t, int) or t + 1 < ALL:
                    layer(t + 1)
                pool.wait_ge(ss_ready, t + 1)
                after(pool, h_ready, t)
                power(g.rstd_b[:, t:t + 1] if isinstance(t, int) else g.rstd_b[:, bass.ds(t, 1)], ms[:, :], ss[:, :], rows_of(t), g.rms_eps,
                      ms_ready, rstd_ready, t)
                if isinstance(t, int) and t == 0:
                    return
                qk(t - 1)

            def qk(t):
                pool.wait_ge(kss_ready, t + 1)
                after(pool, k_ready, t)
                power(hrs[:, HEADS:], hms[:, HEADS:], hss[:, HEADS:], rows_of(t), g.rms_eps, kms_ready, krs_ready, t)
                pool.wait_ge(qss_ready, t + 1)
                after(pool, q_ready, t)
                power(hrs[:, 0:HEADS], hms[:, 0:HEADS], hss[:, 0:HEADS], rows_of(t), g.rms_eps, qms_ready, qrs_ready, t)

            layer(0)
            steady(pool, body)
            qk(ALL - 1)

        lng = g.cols[:, 4 * KT:5 * KT]
        lnb = g.cols[:, 5 * KT:6 * KT]

        @block.scalar
        def _(act):
            def silu_z(t):
                n = rows_of(t)
                act.wait_ge(z_in, 16 * (t + 1))
                act.activation(z[0:n], z[0:n], ACT.Silu).then_inc(sz_ready, 1)

            def silu_y(t):
                n = rows_of(t)
                act.wait_ge(ty_done, t + 1)
                for k in range(KT):
                    ins = act.activation(yc[:, k, 0:n], ps_t[:, k, 0:n], ACT.Silu, scale=lng[:, k:k + 1], bias=lnb[:, k:k + 1])
                ins.then_inc(y2_ready, 1)

            def cut_y(t):
                n = rows_of(t)
                act.wait_ge(prod_ready, t + 1)
                after(act, out_mm, t)
                act.activation(yt[:, 0, :, 0:n], yc[:, :, 0:n], ACT.Copy).then_inc(yhi_ready, 1)

            def square_x1(t):
                n = rows_of(t)
                act.wait_ge(x1_ready, t + 1)
                after(act, th_done, t)
                act.activation(h[0:n], x[0:n], ACT.Square, scale=D ** -0.5, accum_out=ss[0:n]).then_inc(ss_ready, 1)

            def scale_h(t):
                n = rows_of(t)
                act.wait_ge(rstd_ready, t + 1)
                rs = g.rstd_b[0:n, t:t + 1] if isinstance(t, int) else g.rstd_b[0:n, bass.ds(t, 1)]
                act.activation(h[0:n], x[0:n], ACT.Copy, scale=rs).then_inc(h_ready, 1)

            def cut_h(t):
                n = rows_of(t)
                act.wait_ge(th_done, t + 1)
                after(act, q_mm, t)
                act.activation(ht[:, 0, :, 0:n], ps_t[:, :, 0:n], ACT.Copy).then_inc(hhi_ready, 1)

            def qkv(t):
                n = rows_of(t)
                act.wait_ge(kv_mm, t + 1)
                after(act, kv_out, 16 * t)
                if isinstance(t, int) and t == TILES:
                    act.wait_ge(copy_out, 16 * 4)
                act.activation(kvo[0:n, 0:KV], ps_o[0:n, 0:KV], ACT.Square, scale=HD ** -0.5).then_inc(ksq_ready, 1)
                act.activation(kvo[0:n, KV:], ps_o[0:n, KV:2 * KV], ACT.Copy).then_inc(v_ready, 1)
                act.wait_ge(q_mm, t + 1)
                after(act, q_out, 16 * t)
                act.activation(qo[0:n], ps_q[0:n], ACT.Square, scale=HD ** -0.5).then_inc(qsq_ready, 1)

            def body(t):
                if not (isinstance(t, int) and t == 0):
                    cut_h(t - 1)
                more = not isinstance(t, int) or t + 1 < ALL
                if more:
                    silu_z(t + 1)
                square_x1(t)
                if more:
                    silu_y(t + 1)
                scale_h(t)
                if more:
                    cut_y(t + 1)
                if not (isinstance(t, int) and t == 0):
                    qkv(t - 1)

            silu_z(0)
            for m, gain in ((OUT0, None), (OUT1, None), (KVS, g.cols[:, KT:2 * KT]), (Q0, g.cols[:, 2 * KT:3 * KT]),
                            (Q1, g.cols[:, 2 * KT:3 * KT])):
                split_weights_hi(act, m, gain, g, m)
                if m == OUT0:
                    silu_y(0)
                    cut_y(0)
            act.wait_ge(g.w_lo, 5 * KT)
            steady(act, body)
            cut_h(ALL - 1)
            qkv(ALL - 1)

        @block.vector
        def _(dve):
            dve.wait_ge(kg_in, 16)

            def normalize(t):
                n = rows_of(t)
                dve.wait_ge(tc_done, t + 1)
                after(dve, lms_ready, t)
                for b in range(2):
                    dve.bn_stats(stats[0:n, b], ps_c[0:n, b * HALF:(b + 1) * HALF]).then_inc(stat_step, 1)
                dve.wait_ge(stat_step, 3 * t + 2)
                dve.memset(pause[:, :], 0.0)
                dve.bn_aggr(mv[0:n], stats[0:n].rearrange("p a b -> p (a b)")).then_inc(stat_step, 1)
                dve.wait_ge(stat_step, 3 * t + 3)
                dve.wait_ge(lrs_ready, t + 1)
                after(dve, ylo_ready, t)
                dve.tensor_scalar(y[0:n], ps_c[0:n], mv[0:n, 0:1], lrs[0:n, 0:1], ALU.subtract, ALU.mult).then_inc(yn_ready, 1)

            def gate(t):
                n = rows_of(t)
                dve.wait_ge(y2_ready, t + 1)
                dve.wait_ge(tz_done, t + 1)
                dve.tensor_tensor(yc[:, :, 0:n], yc[:, :, 0:n], ps_cc[:, :, 0:n], ALU.mult).then_inc(prod_ready, 1)
                dve.wait_ge(yhi_ready, t + 1)
                dve.tensor_tensor(yt[:, 1, :, 0:n], yc[:, :, 0:n], f32(yt[:, 0, :, 0:n]), ALU.subtract).then_inc(ylo_ready, 1)

            def residual(t):
                n = rows_of(t)
                dve.wait_ge(out_mm, t + 1)
                dve.wait_ge(x_in, 16 * (t + 1))
                dve.tensor_tensor(x[0:n], ps_o[0:n], x[0:n], ALU.add).then_inc(x1_ready, 1)

            def cut_h(t):
                n = rows_of(t)
                dve.wait_ge(hhi_ready, t + 1)
                dve.tensor_tensor(ht[:, 1, :, 0:n], ps_t[:, :, 0:n], f32(ht[:, 0, :, 0:n]), ALU.subtract).then_inc(hlo_ready, 1)

            def keys(t):
                n = rows_of(t)
                dve.wait_ge(ksq_ready, t + 1)
                after(dve, kms_ready, t)
                dve.tensor_reduce(hss[0:n, HEADS:], heads(kvo[0:n, 0:KV], KVH), AX_X, ALU.add).then_inc(kss_ready, 1)
                dve.wait_ge(krs_ready, t + 1)
                dve.wait_ge(v_ready, t + 1)
                rs = hrs[0:n, HEADS:].rearrange("p (h a) -> p h a", a=1).broadcast_to([n, KVH, HD])
                dve.tensor_tensor(heads(kvo[0:n, 0:KV], KVH), heads(ps_o[0:n, 0:KV], KVH), rs, ALU.mult).then_inc(kn_ready, 1)
                dve.wait_ge(kn_ready, t + 1)
                kg = kgain[0:n, :].rearrange("p (a d) -> p a d", a=1).broadcast_to([n, KVH, HD])
                dve.tensor_tensor(heads(kvo[0:n, 0:KV], KVH), heads(kvo[0:n, 0:KV], KVH), kg, ALU.mult).then_inc(k_ready, 1)

            def query_sums(t):
                n = rows_of(t)
                dve.wait_ge(qsq_ready, t + 1)
                after(dve, qms_ready, t)
                dve.tensor_reduce(hss[0:n, 0:HEADS], heads(qo[0:n], HEADS), AX_X, ALU.add).then_inc(qss_ready, 1)

            def queries(t):
                n = rows_of(t)
                dve.wait_ge(qrs_ready, t + 1)
                rs = hrs[0:n, 0:HEADS].rearrange("p (h a) -> p h a", a=1).broadcast_to([n, HEADS, HD])
                dve.tensor_tensor(heads(qo[0:n], HEADS), heads(ps_q[0:n], HEADS), rs, ALU.mult).then_inc(q_ready, 1)

            def body(t):
                if not (isinstance(t, int) and t == 0):
                    cut_h(t - 1)
                if not (isinstance(t, int) and t < 2):
                    queries(t - 2)
                more = not isinstance(t, int) or t + 1 < ALL
                if more:
                    normalize(t + 1)
                residual(t)
                if more:
                    gate(t + 1)
                if not (isinstance(t, int) and t == 0):
                    keys(t - 1)
                    query_sums(t - 1)

            normalize(0)
            for m, gain in ((OUT0, None), (OUT1, None), (KVS, g.cols[:, KT:2 * KT]), (Q0, g.cols[:, 2 * KT:3 * KT]),
                            (Q1, g.cols[:, 2 * KT:3 * KT])):
                split_weights_lo(dve, m, gain, g, m)
                if m == OUT0:
                    gate(0)
            steady(dve, body)
            queries(ALL - 2)
            cut_h(ALL - 1)
            keys(ALL - 1)
            query_sums(ALL - 1)
            queries(ALL - 1)

        @block.tensor
        def _(pe):
            def turn_c(t):
                n = rows_of(t)
                pe.wait_ge(c_in, 16 * (t + 1))
                after(pe, prod_ready, t)
                for k in range(KT):
                    ins = pe.transpose(ps_c[0:n, k * P:(k + 1) * P], c[:, k, 0:n], g.ident[:, :])
                ins.then_inc(tc_done, 1)

            def turn(out, src, t, done):
                n = rows_of(t)
                for k in range(KT):
                    ins = pe.transpose(out[:, k, 0:n], src[0:n, k * P:(k + 1) * P], g.ident[0:n, 0:n])
                ins.then_inc(done, 1)

            def turn_y(t):
                pe.wait_ge(yn_ready, t + 1)
                after(pe, hlo_ready, t - 1)
                turn(ps_t, y, t, ty_done)

            def turn_z(t):
                pe.wait_ge(sz_ready, t + 1)
                turn(ps_cc, z, t, tz_done)

            def turn_h(t):
                pe.wait_ge(h_ready, t + 1)
                after(pe, y2_ready, t + 2 if not isinstance(t, int) else min(t + 2, ALL))
                turn(ps_t, h, t, th_done)

            def out(t, gate=False):
                n = rows_of(t)
                pe.wait_ge(ylo_ready, t + 1)
                after(pe, k_ready, t - 1)
                after(pe, v_ready, t - 1)
                for b in range(2):
                    ins = project(pe, ps_o[0:n, b * HALF:(b + 1) * HALF], yt, g.wslot[OUT0 + b], n,
                                  (g.w_lo, KT * b) if gate else None)
                ins.then_inc(out_mm, 1)

            def qkv(t, gate=False):
                n = rows_of(t)
                pe.wait_ge(hlo_ready, t + 1)
                after(pe, x1_ready, t + 2 if not isinstance(t, int) else min(t + 2, ALL))
                project(pe, ps_o[0:n, 0:HALF], ht, g.wslot[KVS], n, (g.w_lo, KT * KVS) if gate else None).then_inc(kv_mm, 1)
                after(pe, q_ready, t)
                for b in range(2):
                    ins = project(pe, ps_q[0:n, b * HALF:(b + 1) * HALF], ht, g.wslot[Q0 + b], n,
                                  (g.w_lo, KT * (Q0 + b)) if gate else None)
                ins.then_inc(q_mm, 1)

            def body(t):
                more = not isinstance(t, int) or t + 1 < ALL
                if more:
                    turn_c(t + 1)
                out(t, gate=isinstance(t, int) and t == 0)
                if more:
                    turn_y(t + 1)
                    turn_z(t + 1)
                if not (isinstance(t, int) and t == 0):
                    qkv(t - 1, gate=isinstance(t, int) and t == 1)
                turn_h(t)

            turn_c(0)
            turn_y(0)
            turn_z(0)
            steady(pe, body)
            qkv(ALL - 1)


def phase_c(nc, io, g):
    with ExitStack() as ctx:
        sb = lambda name, shape, dt=F32: ctx.enter_context(nc.sbuf_tensor(name, shape, dt))
        pb = lambda name, shape: ctx.enter_context(nc.psum_tensor(name, shape, F32))
        sem = lambda name: ctx.enter_context(nc.semaphore(name))

        Z0, Z1, OUT0, OUT1 = range(4)
        g.wslot = [sb(f"c_w{m}", [P, 2, KT, HALF], F32R) for m in range(4)]
        hx = sb("c_hx", [P, D])
        xr = sb("c_xr", [P, D])
        ht = sb("c_ht", [P, 2, KT, P], F32R)
        ot = sb("c_ot", [P, 2, KT, P], F32R)
        q = sb("c_q", [P, D])
        qt = sb("c_qt", [P, KT, P])
        kd = sb("c_kd", [P, KVH, 2, HD])
        kt = sb("c_kt", [P, 2, KVH, P])
        v = sb("c_v", [P, 2, KV])
        bias = sb("c_bias", [P, HEADS, 2 * P])
        s = sb("c_s", [P, 2, GROUP, 2 * P])
        g.stage = s[:, :].rearrange("p b (a j) k -> p (b a) (j k)", a=2)
        pt = sb("c_pt", [P, 2, GROUP, P])
        sz = sb("c_sz", [P, D])
        sink0 = sb("c_sink0", [P, HEADS])
        sink = sb("c_sink", [P, HEADS])
        nsink = sb("c_nsink", [P, HEADS])
        sinkd = sb("c_sinkd", [P, 2])
        nm = sb("c_nm", [P, 2, GROUP])
        es = sb("c_es", [P, 2, GROUP])
        den = sb("c_den", [P, 2, GROUP])
        rden = sb("c_rden", [P, 2, GROUP])
        dist = sb("c_dist", [P, 2 * P])
        ddist = sb("c_ddist", [P, P + DS + 1])
        vn = sb("c_vn", [DS, 2, KV])

        acc = pb("c_acc", [P, HALF])
        ps_t = pb("c_pst", [P, KT, P])
        ps_s = pb("c_pss", [P, GROUP, 2 * P])
        ps_p = pb("c_psp", [P, 2, GROUP, P])
        ps_o = pb("c_pso", [P, HALF])

        g.w_in = [sem(f"c_w_in{b}") for b in range(STAGES)]
        g.w_hi, g.w_lo = sem("c_w_hi"), sem("c_w_lo")
        kn_in = [sem("c_kn_in0"), sem("c_kn_in1")]
        v_in = [sem("c_v_in0"), sem("c_v_in1")]
        (tab_in, hx_in, xr_in, q_in, k_in, y_out, bias_made, nsink_made, h_ready, th_done, hhi_ready, hlo_ready,
         tq_done, qt_ready, tk_done, kt_ready, z_mm, zexp_ready, z_step, zg_done, qk_done, s_read, m_ready, nm_ready,
         es_in, es_ready, p_ready, den_ready, rden_ready, pn_ready, tp_done, pt_ready, pv_done, o_done, to_done,
         ohi_ready, olo_ready, out_mm, res_done, szt_done, szt_ready, od_ready) = (sem("c_" + x) for x in (
             "tab_in hx_in xr_in q_in k_in y_out bias_made nsink_made h_ready th_done hhi_ready hlo_ready "
             "tq_done qt_ready tk_done kt_ready z_mm zexp_ready z_step zg_done qk_done s_read m_ready nm_ready "
             "es_in es_ready p_ready den_ready rden_ready pn_ready tp_done pt_ready pv_done o_done to_done "
             "ohi_ready olo_ready out_mm res_done szt_done szt_ready od_ready").split())
        WAVES = DB // GROUP
        GD = TILES * KVH
        DK = P + DS
        slope = [2.0 ** (-8.0 * (h + 1) / HEADS) for h in range(HEADS)]
        SCALE = HD ** -0.5
        place = lambda j: 2 * (j % 2) + j // 2
        szc = sz[:, :].rearrange("p (k n) -> p k n", k=KT)
        qc = q[:, :].rearrange("p (k n) -> p k n", k=KT)
        qd = qt[0:HD, :, :].rearrange("p a b -> p (a b)")
        knt = bias[:, 0:4, 0:DEC]
        block = ctx.enter_context(nc.Block())

        def loop(eng, body):
            body(0, 0)
            body(1, 1)
            with eng.Fori(1, TILES // 2 - 1) as i:
                for r in range(2):
                    body(i * 2 + r, r)
            body(TILES - 2, 0)
            body(TILES - 1, 1)

        halves = lambda t: (1,) if isinstance(t, int) and t == 0 else (0, 1)
        keys_of = lambda t: slice(P, 2 * P) if isinstance(t, int) and t == 0 else slice(0, 2 * P)

        @block.sync
        def _(sp):
            def load_h(t):
                after(sp, th_done, t)
                n = rows_of(t)
                sp.dma_start(hx[0:n], token_rows(g.x1_d, t, n)).then_inc(hx_in, 16)

            def load_q(t):
                after(sp, tq_done, t)
                n = rows_of(t)
                sp.dma_start(q[0:n], token_rows(g.q_d, t, n)).then_inc(q_in, 16)

            def load_k(t, src=None):
                after(sp, tk_done, t)
                n = P if src is not None else rows_of(t)
                src = token_rows(g.kv_d, t, n)[:, 0:KV] if src is None else src
                for e in range(2):
                    sp.dma_start(kd[0:n, :, e], src.rearrange("n (h d) -> n h d", h=KVH)).then_inc(k_in, 16)

            def load_v(t, r):
                if not (isinstance(t, int) and t < 2):
                    sp.wait_ge(pv_done, t * KVH)
                sp.dma_start(v[:, r], token_rows(g.kv_d, t, P)[:, KV:2 * KV]).then_inc(v_in[r], 16)

            def load_res(t):
                after(sp, y_out, 16 * t)
                n = rows_of(t)
                sp.dma_start(xr[0:n], token_rows(g.x1_d, t, n)).then_inc(xr_in, 16)

            def store_y(t):
                n = rows_of(t)
                sp.wait_ge(res_done, 2 * t + 2)
                sp.dma_start(io.y_s if n == DEC else token_rows(io.y_p, t, n), xr[0:n]).then_inc(y_out, 16)

            sp.dma_start(dist[:, :], io.distance).then_inc(tab_in, 16)
            sp.dma_start(ddist[:, :], io.decode_distance).then_inc(tab_in, 16)
            sp.dma_start(sink0[:, :], io.sinks.broadcast_to([P, HEADS])).then_inc(tab_in, 16)
            for h in range(HEADS):
                sp.dma_start(sinkd[h * DS:(h + 1) * DS, 0:1], io.sinks[:, h:h + 1].broadcast_to([DS, 1])).then_inc(tab_in, 16)
            load_h(0)
            load_q(0)
            load_k(0)
            load_v(0, 0)
            for n, w in enumerate((io.w_in_b[:, D:D + HALF], io.w_in_b[:, D + HALF:2 * D], io.w_out_b[:, 0:HALF],
                                   io.w_out_b[:, HALF:D])):
                split_weights_dma(sp, w, g, n)

            def body(t, r):
                first = isinstance(t, int) and t == 0
                load_h(t + 1)
                if not first:
                    load_res(t - 1)
                load_q(t + 1)
                load_k(t + 1)
                if not first:
                    store_y(t - 1)
                if not (isinstance(t, int) and t == TILES - 1):
                    load_v(t + 1, 1 - r)
            loop(sp, body)
            load_res(TILES - 1)

            def load_cache(b):
                after(sp, pv_done, max(GD, GD + b - 1))
                sp.dma_start(v[:, b % 2], io.cache_v[b]).then_inc(v_in[b % 2], 16)
                sp.dma_start(vn[:, b % 2], g.kv_d[SEQ + b * DS:SEQ + (b + 1) * DS, KV:2 * KV]).then_inc(kn_in[b % 2], 16)
            load_cache(0)
            load_cache(1)
            for b in range(GROUP):
                load_k(ALL + b, io.cache_k[b])
            store_y(TILES - 1)
            load_res(TILES)
            for b in range(2, GROUP):
                load_cache(b)
            for b in range(GROUP, DB):
                load_k(ALL + b, io.cache_k[b])
            for b in range(GROUP, DB):
                load_cache(b)
            store_y(TILES)
            sp.wait_ge(y_out, 16 * ALL)

        @block.scalar
        def _(act):
            def scale_h(t):
                n = rows_of(t)
                act.wait_ge(hx_in, 16 * (t + 1))
                rs = g.rstd_b[0:n, t:t + 1] if isinstance(t, int) else g.rstd_b[0:n, bass.ds(t, 1)]
                act.activation(hx[0:n], hx[0:n], ACT.Copy, scale=rs).then_inc(h_ready, 1)

            def cut_h(t):
                n = rows_of(t)
                act.wait_ge(th_done, t + 1)
                after(act, z_mm, 2 * t)
                act.activation(ht[:, 0, :, 0:n], ps_t[:, :, 0:n], ACT.Copy).then_inc(hhi_ready, 1)

            def cut_o(t):
                n = rows_of(t)
                if n == DEC:
                    act.wait_ge(od_ready, 1)
                    src = szc[:, :, 0:n]
                else:
                    act.wait_ge(to_done, t + 1)
                    src = ps_t[:, :, 0:n]
                after(act, out_mm, 2 * t)
                act.activation(ot[:, 0, :, 0:n], src, ACT.Copy).then_inc(ohi_ready, 1)

            def queries(t):
                act.wait_ge(tq_done, t + 1)
                if isinstance(t, int) and t == TILES:
                    after(act, qk_done, GD)
                    act.activation(qd.rearrange("p (b h i) -> p b h i", b=DB, h=HEADS),
                                   ps_t[0:HD, :, :].rearrange("p a c -> p (a c)").rearrange("p (h b i) -> p b h i", h=HEADS, b=DB), ACT.Copy, scale=g.qgain[0:HD]).then_inc(qt_ready, 1)
                else:
                    after(act, qk_done, KVH * t)
                    act.activation(qt[:, :, :], ps_t[:, :, :], ACT.Copy, scale=g.qgain[:, :]).then_inc(qt_ready, 1)

            def keys(t, r):
                act.wait_ge(tk_done, t + 1)
                if isinstance(t, int) and t == TILES:
                    act.activation(knt[:, :, :], acc[:, :].rearrange("p (h k) -> p h k", h=KVH)[:, :, 0:DEC], ACT.Copy).then_inc(kt_ready, 1)
                    return
                act.activation(kt[:, r], acc[:, :].rearrange("p (h k) -> p h k", h=KVH), ACT.Copy).then_inc(kt_ready, 1)

            def gate_exp(t, b):
                n = rows_of(t)
                act.wait_ge(z_mm, 2 * t + b + 1)
                after(act, to_done, t)
                act.activation(sz[0:n, b * HALF:(b + 1) * HALF], acc[0:n], ACT.Exp, scale=-1.0).then_inc(zexp_ready, 1)

            def exps(G, b, ks):
                act.wait_ge(nm_ready, G + 1)
                after(act, rden_ready, G - 1)
                act.wait_ge(es_in, G + 1)
                act.activation(es[:, b], es[:, b], ACT.Exp).then_inc(es_ready, 1)
                for j in range(GROUP):
                    ins = act.activation(s[:, b, j, ks], s[:, b, j, ks], ACT.Exp, bias=nm[:, b, j:j + 1], accum_out=den[:, b, j:j + 1])
                ins.then_inc(p_ready, 1)

            def turn_out(G, ks):
                act.wait_ge(tp_done, G + 1)
                after(act, pv_done, G)
                act.activation(pt[:, ks], ps_p[:, ks], ACT.Copy).then_inc(pt_ready, 1)

            for m in range(4):
                if m == 0:
                    scale_h(0)
                    cut_h(0)
                    queries(0)
                    keys(0, 0)
                split_weights_hi(act, m, g.cols[:, 2 * KT:3 * KT] if m < 2 else None, g, m)

            def body(t, r):
                hs = slice(1, 2) if isinstance(t, int) and t == 0 else slice(0, 2)
                ks = keys_of(t)
                first = isinstance(t, int) and t == 0
                scale_h(t + 1)
                exps(t * KVH, 0, ks)
                if not first:
                    cut_o(t - 1)
                gate_exp(t, 0)
                turn_out(t * KVH, hs)
                exps(t * KVH + 1, 1, ks)
                gate_exp(t, 1)
                turn_out(t * KVH + 1, hs)
                exps(t * KVH + 2, 0, ks)
                cut_h(t + 1)
                turn_out(t * KVH + 2, hs)
                exps(t * KVH + 3, 1, ks)
                queries(t + 1)
                turn_out(t * KVH + 3, hs)
                keys(t + 1, 1 - r)
            loop(act, body)

            gate_exp(TILES, 0)
            cut_o(TILES - 1)
            for b in range(GROUP):
                keys(ALL + b, b % 2)
            gate_exp(TILES, 1)
            for w in range(WAVES):
                G = GD + w
                exps(G, w % 2, slice(0, DK))
                for j in range(GROUP):
                    b = GROUP * w + j
                    act.wait_ge(tp_done, GD + b + 1)
                    after(act, pv_done, GD + b)
                    act.activation(pt[:, 0, 0], ps_p[:, 0, 0], ACT.Copy)
                    act.activation(pt[0:DS, 1, 0], ps_p[0:DS, 1, 0], ACT.Copy).then_inc(pt_ready, 1)
                if w + 1 < WAVES:
                    for b in range(GROUP * (w + 1), GROUP * (w + 2)):
                        keys(ALL + b, b % 2)
            act.wait_ge(szt_done, 1)
            act.activation(qc[:, :, 0:DEC], ps_t[:, :, 0:DEC], ACT.Copy).then_inc(szt_ready, 1)
            cut_o(TILES)

        @block.vector
        def _(dve):
            dve.wait_ge(tab_in, 16 * (3 + HEADS))
            for h in range(HEADS):
                ins = dve.tensor_scalar(bias[:, h - h % GROUP + place(h % GROUP)], dist[:, :], -slope[h], None, ALU.mult)
            ins.then_inc(bias_made, 1)
            ordered = lambda ap: ap.rearrange("p (g b a) -> p g b a", b=2, a=2)
            given = sink0[:, :].rearrange("p (g a b) -> p g b a", b=2, a=2)
            dve.tensor_scalar(ordered(sink[:, :]), given, 1.0, None, ALU.mult).then_inc(nsink_made, 1)
            dve.tensor_scalar(ordered(nsink[:, :]), given, -1.0, None, ALU.mult).then_inc(nsink_made, 1)
            dve.tensor_scalar(sinkd[:, 1:2], sinkd[:, 0:1], -1.0, None, ALU.mult).then_inc(nsink_made, 1)
            dve.tensor_scalar(ddist[:, 0:DK], ddist[:, 0:DK], ddist[:, DK:DK + 1], None, ALU.mult).then_inc(nsink_made, 1)

            def cut_h(t):
                n = rows_of(t)
                dve.wait_ge(hhi_ready, t + 1)
                dve.tensor_tensor(ht[:, 1, :, 0:n], ps_t[:, :, 0:n], f32(ht[:, 0, :, 0:n]), ALU.subtract).then_inc(hlo_ready, 1)

            def cut_o(t):
                n = rows_of(t)
                dve.wait_ge(ohi_ready, t + 1)
                src = szc if n == DEC else ps_t
                dve.tensor_tensor(ot[:, 1, :, 0:n], src[:, :, 0:n], f32(ot[:, 0, :, 0:n]), ALU.subtract).then_inc(olo_ready, 1)

            def gate(t, b):
                n = rows_of(t)
                k = 2 * t + b
                part = sz[0:n, b * HALF:(b + 1) * HALF]
                dve.wait_ge(zexp_ready, k + 1)
                dve.tensor_scalar(part, part, 1.0, None, ALU.add).then_inc(z_step, 1)
                dve.wait_ge(z_step, 2 * k + 1)
                dve.reciprocal(part, part).then_inc(z_step, 1)
                dve.wait_ge(z_step, 2 * k + 2)
                dve.tensor_tensor(part, acc[0:n], part, ALU.mult).then_inc(zg_done, 1)

            def scores(G, t, kv, b):
                ks = keys_of(t)
                dve.wait_ge(qk_done, G + 1)
                after(dve, tp_done, G - 1)
                dve.scalar_tensor_tensor(s[:, b, :, ks], ps_s[:, :, ks], SCALE, bias[:, kv * GROUP:(kv + 1) * GROUP, ks],
                                         ALU.mult, ALU.add).then_inc(s_read, 1)
                dve.wait_ge(s_read, G + 1)
                dve.tensor_reduce(nm[:, b], s[:, b, :, ks], AX_X, ALU.max, negate=True).then_inc(m_ready, 1)
                sinks(G, b, nsink[:, kv * GROUP:(kv + 1) * GROUP], sink[:, kv * GROUP:(kv + 1) * GROUP])

            def sinks(G, b, minus, plus):
                dve.wait_ge(m_ready, G + 1)
                dve.tensor_tensor(nm[:, b], nm[:, b], minus, ALU.min).then_inc(nm_ready, 1)
                dve.wait_ge(nm_ready, G + 1)
                dve.tensor_tensor(es[:, b], plus, nm[:, b], ALU.add).then_inc(es_in, 1)

            def sums(G, b):
                dve.wait_ge(p_ready, G + 1)
                dve.wait_ge(es_ready, G + 1)
                dve.tensor_tensor(den[:, b], den[:, b], es[:, b], ALU.add).then_inc(den_ready, 1)
                dve.wait_ge(den_ready, G + 1)
                dve.reciprocal(rden[:, b], den[:, b]).then_inc(rden_ready, 1)

            def gated(G, kv, b):
                dve.wait_ge(pv_done, G + 1)
                dve.wait_ge(rden_ready, G + 1)
                for j in range(GROUP):
                    part = sz[:, (kv * GROUP + j) * HD:(kv * GROUP + j + 1) * HD]
                    ins = dve.scalar_tensor_tensor(part, ps_o[:, j * HD:(j + 1) * HD], rden[:, b, place(j):place(j) + 1], part, ALU.mult, ALU.mult)
                ins.then_inc(o_done, 1)

            def residual(t, b):
                n = rows_of(t)
                part = xr[0:n, b * HALF:(b + 1) * HALF]
                dve.wait_ge(out_mm, 2 * t + b + 1)
                dve.wait_ge(xr_in, 16 * (t + 1))
                dve.tensor_tensor(part, acc[0:n], part, ALU.add).then_inc(res_done, 1)

            for m in range(4):
                if m == 0:
                    cut_h(0)
                split_weights_lo(dve, m, g.cols[:, 2 * KT:3 * KT] if m < 2 else None, g, m)
            dve.wait_ge(g.w_lo, 4 * KT)
            dve.wait_ge(bias_made, 1)
            dve.wait_ge(nsink_made, 4)

            def body(t, r):
                first = isinstance(t, int) and t == 0
                G = t * KVH
                scores(G, t, 0, 0)
                if not first:
                    cut_o(t - 1)
                sums(G, 0)
                gate(t, 0)
                scores(G + 1, t, 1, 1)
                gated(G, 0, 0)
                sums(G + 1, 1)
                gate(t, 1)
                scores(G + 2, t, 2, 0)
                gated(G + 1, 1, 1)
                sums(G + 2, 0)
                cut_h(t + 1)
                if not first:
                    residual(t - 1, 0)
                scores(G + 3, t, 3, 1)
                gated(G + 2, 2, 0)
                if not first:
                    residual(t - 1, 1)
                sums(G + 3, 1)
                gated(G + 3, 3, 1)
            loop(dve, body)

            gate(TILES, 0)
            cut_o(TILES - 1)
            gate(TILES, 1)
            for w in range(WAVES):
                G, b = GD + w, w % 2
                dve.wait_ge(qk_done, G + 1)
                after(dve, tp_done, GD - 1 + w if w == 0 else GD)
                dd = ddist[:, 0:DK].rearrange("p (a k) -> p a k", a=1).broadcast_to([P, GROUP, DK])
                dve.scalar_tensor_tensor(s[:, b, :, 0:DK], ps_s[:, :, 0:DK], SCALE, dd, ALU.mult, ALU.add).then_inc(s_read, 1)
                dve.wait_ge(s_read, G + 1)
                dve.tensor_reduce(nm[:, b], s[:, b, :, 0:DK], AX_X, ALU.max, negate=True).then_inc(m_ready, 1)
                sinks(G, b, sinkd[:, 1:2].broadcast_to([P, GROUP]), sinkd[:, 0:1].broadcast_to([P, GROUP]))
                if w == 0:
                    residual(TILES - 1, 0)
                    residual(TILES - 1, 1)
                sums(G, b)
                dve.wait_ge(rden_ready, G + 1)
                for j in range(GROUP):
                    ins = dve.tensor_scalar(s[:, b, j, 0:DK], s[:, b, j, 0:DK], rden[:, b, j:j + 1], None, ALU.mult)
                ins.then_inc(pn_ready, 1)
            dve.wait_ge(pv_done, GD + DB)
            dve.wait_ge(szt_ready, 1)
            dve.tensor_tensor(szc[:, :, 0:DEC], ps_o[:, :].rearrange("p (k n) -> p k n", k=KT), qc[:, :, 0:DEC], ALU.mult).then_inc(od_ready, 1)
            dve.wait_ge(od_ready, 1)
            cut_o(TILES)
            residual(TILES, 0)
            residual(TILES, 1)

        @block.tensor
        def _(pe):
            def turn_h(t):
                n = rows_of(t)
                pe.wait_ge(h_ready, t + 1)
                if isinstance(t, int) and t <= 1:
                    after(pe, qt_ready, t)
                else:
                    pe.wait_ge(olo_ready, t - 1)
                for k in range(KT):
                    ins = pe.transpose(ps_t[:, k, 0:n], hx[0:n, k * P:(k + 1) * P], g.ident[0:n, 0:n])
                ins.then_inc(th_done, 1)

            def turn_q(t):
                pe.wait_ge(q_in, 16 * (t + 1))
                pe.wait_ge(hlo_ready, t + 1)
                if isinstance(t, int) and t == TILES:
                    flat = ps_t[0:HD, :, :].rearrange("p a b -> p (a b)")
                    for h in range(HEADS):
                        ins = pe.transpose(flat[:, h * DEC:(h + 1) * DEC], q[0:DEC, h * HD:(h + 1) * HD], g.ident[0:DEC, 0:DEC])
                else:
                    for k in range(KT):
                        ins = pe.transpose(ps_t[:, k], q[:, k * P:(k + 1) * P], g.ident[:, :])
                ins.then_inc(tq_done, 1)

            def turn_k(t):
                n = P if isinstance(t, int) and t >= ALL else rows_of(t)
                pe.wait_ge(k_in, 32 * (t + 1))
                for h in range(KVH):
                    ins = pe.transpose(acc[:, h * P:h * P + n], kd[0:n, h].rearrange("p e d -> p (e d)"), g.ident[0:n, 0:n])
                ins.then_inc(tk_done, 1)

            def qk(t, kv, r):
                G = t * KVH + kv
                pe.wait_ge(qt_ready, t + 1)
                pe.wait_ge(kt_ready, t + 1)
                after(pe, s_read, G)
                for j in range(GROUP):
                    h = kv * GROUP + j
                    e = h % 2
                    for half in halves(t):
                        ins = pe.matmul(ps_s[:, place(j), half * P:(half + 1) * P], qt[e * HD:(e + 1) * HD, h // 2],
                                        kt[e * HD:(e + 1) * HD, r if half else 1 - r, kv], start=True, stop=True)
                ins.then_inc(qk_done, 1)

            def turn_p(t, kv, b):
                G = t * KVH + kv
                pe.wait_ge(p_ready, G + 1)
                after(pe, pt_ready, G)
                for j in range(GROUP):
                    for half in halves(t):
                        ins = pe.transpose(ps_p[:, half, j], s[:, b, j, half * P:(half + 1) * P], g.ident[:, :])
                ins.then_inc(tp_done, 1)

            def pv(t, kv, r, loads):
                G = t * KVH + kv
                pe.wait_ge(pt_ready, G + 1)
                after(pe, o_done, G)
                if kv == 0:
                    pe.wait_ge(v_in[r], loads)
                for j in range(GROUP):
                    hv = halves(t)
                    for half in hv:
                        ins = pe.matmul(ps_o[:, j * HD:(j + 1) * HD], pt[:, half, place(j)], v[:, r if half else 1 - r, kv * HD:(kv + 1) * HD],
                                        start=(half == hv[0]), stop=(half == 1))
                ins.then_inc(pv_done, 1)

            def z(t, b, gate=False):
                n = rows_of(t)
                pe.wait_ge(hlo_ready, t + 1)
                if b == 0:
                    pe.wait_ge(kt_ready, t + 1)
                else:
                    pe.wait_ge(zg_done, 2 * t + 1)
                project(pe, acc[0:n], ht, g.wslot[Z0 + b], n, (g.w_lo, KT * b) if gate else None).then_inc(z_mm, 1)

            def turn_o(t):
                pe.wait_ge(o_done, KVH * (t + 1))
                pe.wait_ge(qt_ready, t + 2)
                for k in range(KT):
                    ins = pe.transpose(ps_t[:, k], sz[:, k * P:(k + 1) * P], g.ident[:, :])
                ins.then_inc(to_done, 1)

            def out(t, b, gate=False):
                n = rows_of(t)
                pe.wait_ge(olo_ready, t + 1)
                if b == 0:
                    pe.wait_ge(zg_done, 2 * t + 4 if n == P else 2 * ALL)
                else:
                    pe.wait_ge(res_done, 2 * t + 1)
                project(pe, acc[0:n], ot, g.wslot[OUT0 + b], n, (g.w_lo, KT * (OUT0 + b)) if gate else None).then_inc(out_mm, 1)

            turn_h(0)
            turn_q(0)
            turn_k(0)

            def body(t, r):
                first = isinstance(t, int) and t == 0
                gate = first
                loads = 16 * (t // 2 + 1) if isinstance(t, int) else (t * 8 + (16 if r == 0 else 8))
                qk(t, 0, r)
                z(t, 0, gate)
                if not first:
                    turn_o(t - 1)
                qk(t, 1, r)
                turn_p(t, 0, 0)
                pv(t, 0, r, loads)
                z(t, 1, gate)
                qk(t, 2, r)
                turn_p(t, 1, 1)
                pv(t, 1, r, loads)
                turn_h(t + 1)
                if not first:
                    out(t - 1, 0, isinstance(t, int) and t == 1)
                qk(t, 3, r)
                turn_p(t, 2, 0)
                pv(t, 2, r, loads)
                if not first:
                    out(t - 1, 1, isinstance(t, int) and t == 1)
                turn_q(t + 1)
                turn_p(t, 3, 1)
                if first:
                    pe.wait_ge(zg_done, 2)
                else:
                    pe.wait_ge(res_done, t * 2)
                turn_k(t + 1)
                pv(t, 3, r, loads)
            loop(pe, body)

            z(TILES, 0)
            turn_o(TILES - 1)
            for w in range(WAVES):
                if w == 0:
                    pe.wait_ge(zg_done, 2 * TILES + 1)
                else:
                    pe.wait_ge(res_done, 2 * TILES)
                for j in range(GROUP):
                    b = GROUP * w + j
                    if j:
                        pe.wait_ge(kt_ready, ALL + b)
                    turn_k(ALL + b)
                    pe.wait_ge(kt_ready, ALL + b + 1)
                    if j == 0:
                        after(pe, s_read, GD + w)
                    for kv in range(KVH):
                        rows = slice(kv * GROUP * DS, (kv + 1) * GROUP * DS)
                        qh = qd[:, b * P + kv * GROUP * DS:b * P + (kv + 1) * GROUP * DS]
                        pe.matmul(ps_s[rows, j, 0:P], qh, kt[0:HD, b % 2, kv], start=True, stop=True)
                        ins = pe.matmul(ps_s[rows, j, P:DK], qh, knt[0:HD, kv, b * DS:(b + 1) * DS], start=True, stop=True)
                ins.then_inc(qk_done, 1)
                if w == 0:
                    z(TILES, 1)
                    out(TILES - 1, 0)
                    out(TILES - 1, 1)
                pe.wait_ge(pn_ready, w + 1)
                for j in range(GROUP):
                    b = GROUP * w + j
                    after(pe, pt_ready, GD + b)
                    pe.transpose(ps_p[:, 0, 0], s[:, w % 2, j, 0:P], g.ident[:, :])
                    pe.transpose(ps_p[0:DS, 1, 0], s[:, w % 2, j, P:DK], g.ident[:, :]).then_inc(tp_done, 1)
                    pe.wait_ge(pt_ready, GD + b + 1)
                    pe.wait_ge(v_in[b % 2], 16 * (TILES // 2 + b // 2 + 1))
                    pe.wait_ge(kn_in[b % 2], 16 * (b // 2 + 1))
                    if b == 0:
                        pe.wait_ge(o_done, GD)
                    for kv in range(KVH):
                        for e in range(2):
                            to = ps_o[e * HD:(e + 1) * HD, :].rearrange("p (k n) -> p k n", k=KT)[:, 2 * kv:2 * kv + 2, b * DS:(b + 1) * DS]
                            col = lambda half, n: pt[0:n, half, 0, kv * 32:(kv + 1) * 32].rearrange("p (j i) -> p j i", i=DS)[:, e::2]
                            pe.matmul(to, v[:, b % 2, kv * HD:(kv + 1) * HD], col(0, P), start=True, stop=False)
                            ins = pe.matmul(to, vn[:, b % 2, kv * HD:(kv + 1) * HD], col(1, DS), start=False, stop=True)
                    ins.then_inc(pv_done, 1)
            pe.wait_ge(zg_done, 2 * ALL)
            pe.wait_ge(olo_ready, TILES)
            for k in range(KT):
                ins = pe.transpose(ps_t[:, k, 0:DEC], sz[0:DEC, k * P:(k + 1) * P], g.ident[0:DEC, 0:DEC])
            ins.then_inc(szt_done, 1)
            out(TILES, 0)
            out(TILES, 1)


def program(nc, io):
    g = Names()
    with ExitStack() as ctx:
        sb = lambda name, shape: ctx.enter_context(nc.sbuf_tensor(name, shape, F32))
        g.ident = sb("ident", [P, P])
        g.half = sb("minus_half", [P, HEADS + KVH])
        g.rms_eps = sb("rms_eps", [P, HEADS + KVH])
        g.ln_eps = sb("ln_eps", [P, 1])
        g.taps = sb("taps", [P, TAPS * KT])
        g.cols = sb("cols", [P, VECS * KT])
        g.qgain = sb("qgain", [P, 1])
        g.rstd_b = sb("rstd_b", [P, ALL])
        scratch = lambda name, *shape: nc.dram_tensor(name, shape, F32, kind=SCRATCH).ap()
        g.c_d = scratch("c_d", D, TOK)
        g.z_d = scratch("z_d", TOK, D)
        g.x1_d = scratch("x1_d", TOK, D)
        g.q_d = scratch("q_d", TOK, D)
        g.kv_d = scratch("kv_d", TOK, 2 * KV)
        phase_a(nc, io, g)
        phase_b(nc, io, g)
        phase_c(nc, io, g)


SCRATCH = "Internal"
INPUTS = ("x_prompt", "x_sample", "state_conv", "cache_k", "cache_v", "norm_a", "w_in_a", "w_dw_a", "b_dw_a", "ln_g_a",
          "ln_b_a", "w_out_a", "norm_kv", "w_kv", "k_norm", "norm_b", "w_in_b", "q_norm", "sinks_b", "w_out_b")
OUTPUTS = (("y_p", (1, SEQ, D)), ("y_s", (DB, DS, D)), ("conv_p", (1, 1, HIST, D)), ("conv_s", (1, DB, HIST, D)),
           ("k_p", (1, P, KVH, HD)), ("v_p", (1, P, KVH, HD)), ("k_s", (DB, P, KVH, HD)), ("v_s", (DB, P, KVH, HD)))


def constants():
    far = 1e30
    i, j = np.arange(P)[:, None], np.arange(2 * P)[None, :]
    dist = (i + P - j).astype(np.float64)
    distance = np.where((dist >= 0) & (dist < P), dist, far).astype(np.float32)
    i, j = (np.arange(P) % DS)[:, None], np.arange(P + DS)[None, :]
    dist = (i + P - j).astype(np.float64)
    decode = np.where((dist >= 0) & (dist < P), dist, far)
    slope = -(2.0 ** (-8.0 * (np.arange(P) // DS + 1) / HEADS))[:, None]
    return {"distance": distance, "decode_distance": np.concatenate([decode, slope], 1).astype(np.float32)}


def build(nc, shapes):
    dram = lambda name, shape, kind: nc.dram_tensor(name, shape, F32, kind=kind).ap()
    a = {name: dram("in_" + name, shape, "ExternalInput") for name, shape in shapes.items()}
    o = {name: dram("out_" + name, shape, "ExternalOutput") for name, shape in OUTPUTS}
    flat = lambda ap: ap.rearrange("b w h d -> b w (h d)")
    io = Names()
    io.x_prompt = a["x_prompt"][0]
    io.x_sample = a["x_sample"].rearrange("b s d -> (b s) d")
    io.state = a["state_conv"][0]
    io.cache_k = flat(a["cache_k"])
    io.cache_v = flat(a["cache_v"])
    io.k_norm = a["k_norm"]
    io.norm_kv = a["norm_kv"]
    io.w_kv = a["w_kv"]
    io.norm_a = a["norm_a"][0]
    io.w_in_a = a["w_in_a"][0]
    io.w_dw_a = a["w_dw_a"][0]
    io.b_dw_a = a["b_dw_a"][0]
    io.ln_g_a = a["ln_g_a"][0]
    io.ln_b_a = a["ln_b_a"][0]
    io.w_out_a = a["w_out_a"][0]
    io.norm_b = a["norm_b"][0]
    io.w_in_b = a["w_in_b"][0]
    io.q_norm = a["q_norm"][0]
    io.sinks = a["sinks_b"]
    io.w_out_b = a["w_out_b"][0]
    io.distance = a["distance"]
    io.decode_distance = a["decode_distance"]
    io.y_p = o["y_p"][0]
    io.y_s = o["y_s"].rearrange("b s d -> (b s) d")
    io.conv_p = o["conv_p"][0, 0]
    io.conv_s = o["conv_s"][0]
    io.k_p = flat(o["k_p"])[0]
    io.v_p = flat(o["v_p"])[0]
    io.k_s = flat(o["k_s"])
    io.v_s = flat(o["v_s"])
    program(nc, io)


def kernel(**inputs):
    import concourse.bacc as bacc
    from concourse.bass_utils import run_bass_kernel_spmd

    nc = bacc.Bacc("TRN2", target_bir_lowering=False, num_devices=1)
    arrays = {name: np.ascontiguousarray(inputs[name]) for name in INPUTS}
    arrays.update(constants())
    build(nc, {name: array.shape for name, array in arrays.items()})
    r = run_bass_kernel_spmd(nc, [{"in_" + name: array for name, array in arrays.items()}], core_ids=[0])
    return tuple(r.results[0]["out_" + name] for name, _ in OUTPUTS)
```

```python
from contextlib import ExitStack

import numpy as np

import concourse.bass as bass
from concourse import mybir

F32 = mybir.dt.float32
F32R = mybir.dt.float32r
ALU = mybir.AluOpType
ACT = mybir.ActivationFunctionType
AX_X = mybir.AxisListType.X

P = 128
D = 1024
KT = D // P
SEQ = 2048
TILES = SEQ // P
DB, DS = 8, 8
DEC = DB * DS
TOK = SEQ + DEC
ALL = TILES + 1
TAPS = 31
VECS = 6
HIST = TAPS - 1
HALF = 512
CT = HALF // P
CHUNK = 4
CTOK = CHUNK * P
NCHUNK = TILES // CHUNK
HEADS, KVH, HD = 16, 4, 64
GROUP = HEADS // KVH
KV = KVH * HD
RMS_EPS = 1e-6
LN_EPS = 1e-5


class Names:
    pass


def after(eng, sem, count):
    if isinstance(count, int) and count <= 0:
        return
    eng.wait_ge(sem, count)


def rows_of(tile):
    return DEC if isinstance(tile, int) and tile % ALL == TILES else P


def f32(ap):
    return ap.bitcast(F32)


def token_rows(dram, t, n):
    return dram[bass.ds(t * P, n), :] if not isinstance(t, int) else dram[t * P:t * P + n, :]


STAGES = 4
PTAPS = 12
DTAPS = TAPS - PTAPS
RING = 4


def split_weights_dma(sp, weights, g, n0, k0=0, k1=KT):
    for k in range(k0, k1):
        piece = KT * n0 + k
        after(sp, g.w_lo, piece - g.stages + 1)
        sp.dma_start(g.stage[:, piece % g.stages], weights[k * P:(k + 1) * P, :]).then_inc(g.w_in[piece % g.stages], 16)


def gain_of(gain, k):
    return gain if isinstance(gain, float) else gain[:, k:k + 1]


def split_weights_hi(act, m, gain, g, n0, free=None, k0=0, k1=KT):
    if free is not None:
        act.wait_ge(*free)
    for k in range(k0, k1):
        piece = KT * n0 + k
        act.wait_ge(g.w_in[piece % g.stages], 16 * (piece // g.stages + 1))
        act.activation(g.wslot[m][:, 0, k], g.stage[:, piece % g.stages], ACT.Copy, scale=gain_of(gain, k)).then_inc(g.w_hi, 1)


def split_weights_lo(dve, m, gain, g, n0, k0=0, k1=KT):
    for k in range(k0, k1):
        piece = KT * n0 + k
        dve.wait_ge(g.w_hi, piece + 1)
        dve.scalar_tensor_tensor(g.wslot[m][:, 1, k], g.stage[:, piece % g.stages],
                                 gain_of(gain, k), f32(g.wslot[m][:, 0, k]),
                                 ALU.mult, ALU.subtract).then_inc(g.w_lo, 1)


def project(pe, out, xt, w, n, lo_gate=None):
    for k in range(KT):
        if lo_gate is not None:
            pe.wait_ge(lo_gate[0], lo_gate[1] + k + 1)
        for a, b in ((0, 0), (1, 0), (0, 1)):
            last = pe.matmul(out, xt[:, a, k, 0:n], w[:, b, k], start=(k == 0 and a == 0 and b == 0),
                             stop=(k == KT - 1 and b == 1))
    return last


def phase_a(nc, io, g):
    with ExitStack() as ctx:
        sb = lambda name, shape, dt=F32: ctx.enter_context(nc.sbuf_tensor(name, shape, dt))
        pb = lambda name, shape: ctx.enter_context(nc.psum_tensor(name, shape, F32))
        sem = lambda name: ctx.enter_context(nc.semaphore(name))

        g.wslot = g.shared_slots + [sb("a_w2", [P, 2, KT, HALF], F32R)]
        g.stages = STAGES
        g.stage = sb("a_stage", [P, STAGES, HALF])
        x = sb("a_x", [P, 2, D])
        xs = sb("a_xs", [P, D])
        xt = [sb(f"a_xt{p}", [P, 2, KT, P], F32R) for p in range(2)]
        sig = sb("a_sig", [P, HALF])
        v = sb("a_v", [P, 2, HALF])
        zo = sb("a_zo", [P, 2, HALF])
        vbuf = sb("a_vbuf", [P, CT, HIST + SEQ])
        vdec = sb("a_vdec", [P, KT, DB, HIST + DS])
        csum = sb("a_csum", [P, CT, CTOK])
        prod = sb("a_prod", [P, RING, CTOK])
        dacc = sb("a_dacc", [P, CT, DEC])
        raw = sb("a_raw", [P, 3, P])
        ss = sb("a_ss", [P, 2])
        ms = sb("a_ms", [P, 2])
        rstd = sb("a_rstd", [P, 2])

        ps_t = pb("a_pst", [P, KT, P])
        ps_g, ps_a, ps_z = (pb(f"a_ps{n}", [P, HALF]) for n in "gaz")
        ps_v = pb("a_psv", [P, CT, P])
        acc = pb("a_acc", [P, 2, CTOK])

        g.w_in = [sem(f"a_w_in{b}") for b in range(STAGES)]
        g.w_hi, g.w_lo = sem("a_w_hi"), sem("a_w_lo")
        x_in = [sem("a_x_in0"), sem("a_x_in1")]
        v_out = [sem("a_v_out0"), sem("a_v_out1")]
        z_out = [sem("a_z_out0"), sem("a_z_out1")]
        (raw_in, st_in, eps_made, ident_made, cols_t, cols_ready, hist_zero, st_t, st_copied, ss_ready, ms_ready, rstd_ready,
         xs_ready, xt_done, hi_ready, lo_ready, g_mm, a_mm, z_mm, sig_ready, v_ready, z_copied, vt_done, vt_copied,
         conv_step, prod_ready, prod_added, dec_step, c_out, d_out, copy_out) = (sem("a_" + s) for s in (
             "raw_in st_in eps_made ident_made cols_t cols_ready hist_zero st_t st_copied ss_ready ms_ready rstd_ready "
             "xs_ready xt_done hi_ready lo_ready g_mm a_mm z_mm sig_ready v_ready z_copied vt_done vt_copied "
             "conv_step prod_ready prod_added dec_step c_out d_out copy_out").split())

        w_in = io.w_in_a
        GATE, VALUE, ZGATE = 0, 1, 2
        col = lambda s, m: ((D, 0, 2 * D)[m]) + s * HALF
        na = g.cols[:, 0:KT]
        wcol = lambda k, ch: g.taps[:, k * KT + ch:k * KT + ch + 1]
        taps_done = lambda gc, pair, k, j: ((gc * 2 + pair) * DTAPS + k) * 2 + j + 1
        turn = (2, 3, 0, 1)
        bcol = lambda ch: g.cols[:, 3 * KT + ch:3 * KT + ch + 1]
        block = ctx.enter_context(nc.Block())

        @block.sync
        def _(sp):
            taps = io.w_dw_a.rearrange("w (j p) -> (w j) p", p=P)
            sp.dma_start(raw[:, 0], taps[0:P, :]).then_inc(raw_in, 16)
            sp.dma_start(raw[0:TAPS * KT - P, 1], taps[P:TAPS * KT, :]).then_inc(raw_in, 16)
            for n, vec in enumerate((io.norm_a, io.norm_kv, io.norm_b, io.b_dw_a, io.ln_g_a, io.ln_b_a)):
                sp.dma_start(raw[n * KT:(n + 1) * KT, 2], vec.rearrange("(j p) -> j p", p=P)).then_inc(raw_in, 16)
            for h in range(2):
                sp.dma_start(g.qgain[h * HD:(h + 1) * HD, :], io.q_norm.rearrange("(p a) -> p a", a=1)).then_inc(raw_in, 16)
            state = io.state.rearrange("b w c -> (b w) c")
            for h in range(2):
                sp.dma_start(x[0:DB * HIST // 2, h], state[h * DB * HIST // 2:(h + 1) * DB * HIST // 2, :]).then_inc(st_in, 16)
            sp.dma_start(io.conv_s[:, 0:HIST - DS, :], io.state[:, DS:HIST, :]).then_inc(copy_out, 16)

            def load_x(T, t, p):
                if isinstance(T, int) and T < 2:
                    sp.wait_ge(st_t, T + 1)
                after(sp, xs_ready, T - 1)
                n = rows_of(t)
                src = io.x_sample if n == DEC else token_rows(io.x_prompt, t, n)
                sp.dma_start(x[0:n, p], src).then_inc(x_in[p], 16)

            def store(T, t, p, s):
                n = rows_of(t)
                sp.wait_ge(z_copied, T + 1)
                sp.dma_start(token_rows(g.z_d, t, n)[:, s * HALF:(s + 1) * HALF], zo[0:n, p]).then_inc(z_out[p], 16)

            def store_state(T, t, p, s):
                sp.wait_ge(v_ready, T + 1)
                cols = slice(s * HALF, (s + 1) * HALF)
                if t == TILES:
                    for b in range(DB):
                        sp.dma_start(io.conv_s[b, HIST - DS:HIST, cols], v[b * DS:(b + 1) * DS, p]).then_inc(v_out[p], 16)
                else:
                    sp.dma_start(io.conv_p[:, cols], v[P - HIST:P, p]).then_inc(v_out[p], 16)

            def store_c(gc, c, s):
                for j in range(CT):
                    if j < 2:
                        sp.wait_ge(prod_added, (gc * CT + j + 3) * PTAPS)
                    else:
                        sp.wait_ge(conv_step, taps_done(gc, 1, DTAPS - 1, j - 2))
                    dst = g.c_d[(s * CT + j) * P:(s * CT + j + 1) * P, :]
                    dst = dst[:, bass.ds(c * CTOK, CTOK)] if not isinstance(c, int) else dst[:, c * CTOK:(c + 1) * CTOK]
                    sp.dma_start(dst, csum[:, j]).then_inc(c_out, 16)

            def store_dec(s):
                for j in range(CT):
                    sp.wait_ge(dec_step, s * TAPS * CT + (TAPS - 1) * CT + j + 1)
                    sp.dma_start(g.c_d[(s * CT + j) * P:(s * CT + j + 1) * P, SEQ:TOK], dacc[:, j]).then_inc(d_out, 16)

            load_x(0, 0, 0)
            load_x(1, 1, 1)
            for s in range(2):
                for m in range(3):
                    split_weights_dma(sp, w_in[:, col(s, m):col(s, m) + HALF], g, 3 * s + m)
                B = s * ALL
                for t in range(CHUNK):
                    load_x(B + t + 2, t + 2, (B + t) % 2)
                    store(B + t, t, (B + t) % 2, s)
                if s:
                    store_c(NCHUNK - 1, NCHUNK - 1, 0)
                    store_dec(0)
                with sp.Fori(1, NCHUNK - 1) as c:
                    for q in range(CHUNK):
                        load_x(B + c * CHUNK + q + 2, c * CHUNK + q + 2, (B + q) % 2)
                        store(B + c * CHUNK + q, c * CHUNK + q, (B + q) % 2, s)
                    store_c(s * NCHUNK + c - 1, c - 1, s)
                for t in range(TILES - CHUNK, TILES):
                    if B + t + 2 < 2 * ALL:
                        load_x(B + t + 2, (t + 2) % ALL, (B + t) % 2)
                    store(B + t, t, (B + t) % 2, s)
                store_state(B + TILES - 1, TILES - 1, (B + TILES - 1) % 2, s)
                store_c(s * NCHUNK + NCHUNK - 2, NCHUNK - 2, s)
                if s == 0:
                    load_x(ALL + 1, 1, (ALL + 1) % 2)
                store(B + TILES, TILES, (B + TILES) % 2, s)
                store_state(B + TILES, TILES, (B + TILES) % 2, s)
            for b in range(2):
                split_weights_dma(sp, io.w_out_a[:, b * HALF:(b + 1) * HALF], g, 6 + b)
            store_c(2 * NCHUNK - 1, NCHUNK - 1, 1)
            store_dec(1)
            sp.wait_ge(c_out, 16 * 2 * NCHUNK * CT)
            sp.wait_ge(d_out, 16 * 2 * CT)
            for p in range(2):
                sp.wait_ge(z_out[p], 16 * ALL)
                sp.wait_ge(v_out[p], 16 * (1 + DB))
            sp.wait_ge(copy_out, 16)

        @block.gpsimd
        def _(pool):
            pool.memset(g.half[:, :], -0.5).then_inc(ident_made, 1)
            pool.memset(g.rms_eps[:, :], RMS_EPS)
            pool.memset(g.ln_eps[:, :], LN_EPS).then_inc(eps_made, 1)
            pool.wait_ge(eps_made, 1)
            pool.memset(g.ident[:, :], 0.0).then_inc(ident_made, 1)
            pool.wait_ge(ident_made, 2)
            pool.affine_select(out=g.ident[:, :], in_=g.ident[:, :], compare_op=ALU.not_equal, fill=1.0, base=0,
                               pattern=[[-1, P]], channel_multiplier=1).then_inc(ident_made, 1)
            pool.memset(vbuf[:, :, 0:HIST], 0.0).then_inc(hist_zero, 1)

            def rms(T, t, p):
                n = rows_of(t)
                pool.wait_ge(ss_ready, T + 1)
                after(pool, xs_ready, T - 1)
                pool.tensor_tensor(ms[0:n, p:p + 1], ss[0:n, p:p + 1], g.rms_eps[0:n, 0:1], ALU.add).then_inc(ms_ready, 1)
                pool.wait_ge(ms_ready, T + 1)
                pool.tensor_tensor(rstd[0:n, p:p + 1], ms[0:n, p:p + 1], g.half[0:n, 0:1], ALU.pow).then_inc(rstd_ready, 1)

            def out_lo(n):
                if n >= 2 * KT:
                    return
                piece = 6 * KT + n
                pool.wait_ge(g.w_hi, piece + 1)
                pool.tensor_tensor(g.wslot[n // KT][:, 1, n % KT], g.stage[:, piece % STAGES], f32(g.wslot[n // KT][:, 0, n % KT]),
                                   ALU.subtract).then_inc(g.w_lo, 1)

            def add_products(gc, u, i0=0, i1=PTAPS):
                m, j = gc * CT + u, turn[u]
                for i in range(max(i0, 1) if u < 2 else i0, i1):
                    pool.wait_ge(prod_ready, m * PTAPS + i + 1)
                    if u < 2 and i == 1:
                        after(pool, c_out, gc * CT * 16)
                        pool.tensor_tensor(csum[:, j], prod[:, 0], prod[:, 1], ALU.add).then_inc(prod_added, 2)
                        continue
                    if i == 0:
                        pool.wait_ge(conv_step, taps_done(gc, 0, DTAPS - 1, j))
                    else:
                        pool.wait_ge(prod_added, m * PTAPS + i)
                    pool.tensor_tensor(csum[:, j], prod[:, i % RING], csum[:, j], ALU.add).then_inc(prod_added, 1)

            rms(0, 0, 0)
            for s in range(2):
                B = s * ALL
                for q in range(CHUNK):
                    rms(B + q + 1, q + 1, (B + q + 1) % 2)
                    if s:
                        add_products(NCHUNK - 1, q)

                def chunk(c):
                    for q in range(CHUNK):
                        tn = c * CHUNK + q + 1
                        rms(B + tn, tn, (B + q + 1) % 2)
                        add_products(s * NCHUNK + c - 1, q)

                chunk(1)
                with pool.Fori(2, NCHUNK - 1) as c:
                    chunk(c)
                chunk(NCHUNK - 1)
                if s == 0:
                    rms(ALL, 0, ALL % 2)
            add_products(2 * NCHUNK - 1, 0)
            for u in range(1, CT):
                for b in range(PTAPS // 2):
                    add_products(2 * NCHUNK - 1, u, 2 * b, 2 * b + 2)
                    out_lo((u - 1) * (PTAPS // 2) + b)

        def scale_x(act, T, t, p):
            n = rows_of(t)
            act.wait_ge(x_in[p], 16 * (T // 2 + 1) if isinstance(T, int) else p_uses(T, p))
            after(act, xt_done, T)
            act.activation(xs[0:n], x[0:n, p], ACT.Square, scale=D ** -0.5, accum_out=ss[0:n, p:p + 1]).then_inc(ss_ready, 1)
            act.wait_ge(rstd_ready, T + 1)
            act.activation(xs[0:n], x[0:n, p], ACT.Copy, scale=rstd[0:n, p:p + 1]).then_inc(xs_ready, 1)

        def p_uses(T, p):
            return T * 8 + (16 if p == 0 else 8)

        def cut_hi(act, T, t, p):
            n = rows_of(t)
            act.wait_ge(xt_done, T + 1)
            after(act, z_mm, T - 1)
            act.activation(xt[p][:, 0, :, 0:n], ps_t[:, :, 0:n], ACT.Copy).then_inc(hi_ready, 1)

        @block.scalar
        def _(act):
            act.wait_ge(cols_t, 1)
            act.activation(g.taps[:, :], ps_g[:, 0:TAPS * KT], ACT.Copy).then_inc(cols_ready, 1)
            act.activation(g.cols[:, :], ps_g[:, 256:256 + VECS * KT], ACT.Copy).then_inc(cols_ready, 1)
            for h in range(2):
                act.wait_ge(st_t, h + 1)
                dst = vdec[:, :, h * DB // 2:(h + 1) * DB // 2, 0:HIST]
                src = ps_t[:, :, 0:DB * HIST // 2].rearrange("p k (b w) -> p k b w", w=HIST)
                for j in range(KT):
                    last = act.activation(dst[:, j], src[:, j], ACT.Copy)
                last.then_inc(st_copied, 1)
            scale_x(act, 0, 0, 0)
            cut_hi(act, 0, 0, 0)

            def products(work, i0, i1):
                if work is None:
                    return
                gc, c, cs, u = work
                m, j = gc * CT + u, turn[u]
                for i in range(i0, i1):
                    after(act, prod_added, m * PTAPS + i - RING + 1)
                    at = c * CTOK + DTAPS + i
                    win = vbuf[:, j, at:at + CTOK] if isinstance(c, int) else vbuf[:, j, bass.ds(at, CTOK)]
                    act.activation(prod[:, i % RING], win, ACT.Identity, scale=wcol(DTAPS + i, cs * CT + j),
                                   bias=bcol(cs * CT + j) if i == 0 and u < 2 else 0.0).then_inc(prod_ready, 1)

            def body(T, t, p, s, work=None):
                last = isinstance(T, int) and T == 2 * ALL - 1
                n = rows_of(t)
                if work is not None:
                    act.wait_ge(vt_copied, T)
                if not last:
                    tn = (t + 1) % ALL if isinstance(t, int) else t + 1
                    scale_x(act, T + 1, tn, 1 - p)
                products(work, 0, 3)
                act.wait_ge(g_mm, T + 1)
                after(act, v_ready, T)
                act.activation(sig[0:n], ps_g[0:n], ACT.Sigmoid).then_inc(sig_ready, 1)
                products(work, 3, 6)
                if not last:
                    cut_hi(act, T + 1, tn, 1 - p)
                products(work, 6, 10)
                act.wait_ge(z_mm, T + 1)
                if not (isinstance(T, int) and T < 2):
                    act.wait_ge(z_out[p], p_uses(T - 2, p) if not isinstance(T, int) else 16 * (T // 2))
                act.activation(zo[0:n, p], ps_z[0:n], ACT.Copy).then_inc(z_copied, 1)
                act.wait_ge(vt_done, T + 1)
                if n == DEC:
                    for j in range(CT):
                        ins = act.activation(vdec[:, s * CT + j, :, HIST:], ps_v[:, j, 0:DEC].rearrange("p (b w) -> p b w", w=DS), ACT.Copy)
                else:
                    if s:
                        done = NCHUNK - 1 if isinstance(t, int) and t < CHUNK else NCHUNK
                        act.wait_ge(conv_step, done * DTAPS * CT)
                    dst = vbuf[:, :, HIST + t * P:HIST + (t + 1) * P] if isinstance(t, int) else vbuf[:, :, bass.ds(t * P + HIST, P)]
                    ins = act.activation(dst, ps_v[:, :, :], ACT.Copy)
                ins.then_inc(vt_copied, 1)
                products(work, 10, PTAPS)

            for s in range(2):
                B = s * ALL
                for m in range(3):
                    split_weights_hi(act, m, na, g, 3 * s + m, free=((g_mm, a_mm, z_mm)[m], ALL) if s else None)
                for t in range(CHUNK):
                    body(B + t, t, (B + t) % 2, s, (NCHUNK - 1, NCHUNK - 1, 0, t) if s else None)

                def chunk(c):
                    for q in range(CHUNK):
                        body(B + c * CHUNK + q, c * CHUNK + q, (B + q) % 2, s, (s * NCHUNK + c - 1, c - 1, s, q))

                chunk(1)
                with act.Fori(2, NCHUNK) as c:
                    chunk(c)
                body(B + TILES, TILES, (B + TILES) % 2, s, (2 * NCHUNK - 1, NCHUNK - 1, 1, 0) if s else None)
            act.wait_ge(z_mm, 2 * ALL)
            for u in range(1, CT):
                for b in range(PTAPS // 2):
                    products((2 * NCHUNK - 1, NCHUNK - 1, 1, u), 2 * b, 2 * b + 2)
                    m, k = divmod((u - 1) * (PTAPS // 2) + b, KT)
                    if m < 2:
                        split_weights_hi(act, m, 1.0, g, 6 + m, k0=k, k1=k + 1)

        @block.vector
        def _(dve):
            dve.wait_ge(cols_ready, 2)

            def cut_lo(T, t, p):
                n = rows_of(t)
                dve.wait_ge(hi_ready, T + 1)
                dve.tensor_tensor(xt[p][:, 1, :, 0:n], ps_t[:, :, 0:n], f32(xt[p][:, 0, :, 0:n]), ALU.subtract).then_inc(lo_ready, 1)

            def gate(T, t, p):
                n = rows_of(t)
                dve.wait_ge(sig_ready, T + 1)
                dve.wait_ge(a_mm, T + 1)
                after(dve, vt_done, T - 1)
                if isinstance(T, int) and T % ALL < 2 and T >= ALL:
                    dve.wait_ge(v_out[0], 16 * DB)
                    dve.wait_ge(v_out[1], 16)
                dve.tensor_tensor(v[0:n, p], ps_a[0:n], sig[0:n], ALU.mult).then_inc(v_ready, 1)

            def conv(gc, c, s, pair, k0, k1):
                for k in range(k0, k1):
                    for i in range(2):
                        j = 2 * pair + i
                        win = vbuf[:, j, c * CTOK + k:c * CTOK + k + CTOK] if isinstance(c, int) else vbuf[:, j, bass.ds(c * CTOK + k, CTOK)]
                        if k == 0 and pair == 0:
                            after(dve, conv_step, taps_done(gc - 1, 1, DTAPS - 1, i))
                            dve.tensor_scalar(acc[:, i], win, wcol(k, s * CT + j), bcol(s * CT + j), ALU.mult, ALU.add).then_inc(conv_step, 1)
                            continue
                        if k == 0:
                            dve.wait_ge(conv_step, taps_done(gc, 0, DTAPS - 1, i))
                            dve.wait_ge(prod_added, (gc * CT + i + 1) * PTAPS)
                        else:
                            dve.wait_ge(conv_step, taps_done(gc, pair, k - 1, i))
                        if k == DTAPS - 1:
                            after(dve, c_out, gc * CT * 16)
                        dve.scalar_tensor_tensor(csum[:, j] if k == DTAPS - 1 else acc[:, i], win, wcol(k, s * CT + j),
                                                 csum[:, j] if k == 0 else acc[:, i], ALU.mult, ALU.add).then_inc(conv_step, 1)

            def dec_conv(s, k0, k1):
                for k in range(k0, k1):
                    for j in range(CT):
                        win = vdec[:, s * CT + j, :, k:k + DS]
                        out = dacc[:, j].rearrange("p (b w) -> p b w", w=DS)
                        if k == 0:
                            after(dve, d_out, 16 * s * CT)
                            dve.tensor_scalar(out, win, wcol(k, s * CT + j), bcol(s * CT + j), ALU.mult, ALU.add).then_inc(dec_step, 1)
                        else:
                            dve.wait_ge(dec_step, (s * TAPS + k - 1) * CT + j + 1)
                            dve.scalar_tensor_tensor(out, win, wcol(k, s * CT + j), out, ALU.mult, ALU.add).then_inc(dec_step, 1)

            cut_lo(0, 0, 0)
            for s in range(2):
                B = s * ALL
                for m in range(3):
                    split_weights_lo(dve, m, na, g, 3 * s + m)

                def step(T, t, p, q, gc, c, cs, dec=False):
                    part = lambda i: i * DTAPS // CHUNK
                    pair, i = q // 2, 2 * (q % 2)
                    gate(T, t, p)
                    if gc is not None:
                        conv(gc, c, cs, pair, part(i), part(i + 1))
                    cut_lo(T + 1, (t + 1) % ALL if isinstance(t, int) else t + 1, 1 - p)
                    if gc is not None:
                        conv(gc, c, cs, pair, part(i + 1), part(i + 2))
                        if dec:
                            dec_conv(0, 8 * q, min(8 * q + 8, TAPS))

                if s:
                    dve.wait_ge(vt_copied, ALL)
                else:
                    dve.wait_ge(hist_zero, 1)
                for q in range(CHUNK):
                    if s:
                        step(B + q, q, (B + q) % 2, q, NCHUNK - 1, NCHUNK - 1, 0, dec=True)
                    else:
                        step(B + q, q, (B + q) % 2, q, None, None, None)

                def chunk(c):
                    dve.wait_ge(vt_copied, B + c * CHUNK)
                    for q in range(CHUNK):
                        step(B + c * CHUNK + q, c * CHUNK + q, (B + q) % 2, q, s * NCHUNK + c - 1, c - 1, s)

                chunk(1)
                with dve.Fori(2, NCHUNK) as c:
                    chunk(c)
                if s:
                    dve.wait_ge(vt_copied, B + TILES)
                    conv(2 * NCHUNK - 1, NCHUNK - 1, 1, 0, 0, DTAPS // 2)
                gate(B + TILES, TILES, (B + TILES) % 2)
                if s == 0:
                    cut_lo(ALL, 0, ALL % 2)
            dve.wait_ge(vt_copied, 2 * ALL)
            conv(2 * NCHUNK - 1, NCHUNK - 1, 1, 0, DTAPS // 2, DTAPS)
            conv(2 * NCHUNK - 1, NCHUNK - 1, 1, 1, 0, DTAPS)
            dec_conv(1, 0, TAPS)

        @block.tensor
        def _(pe):
            pe.wait_ge(ident_made, 3)
            pe.wait_ge(raw_in, 16 * (2 + VECS + 2))
            pe.transpose(ps_g[:, 0:P], raw[:, 0], g.ident[:, :])
            pe.transpose(ps_g[:, P:TAPS * KT], raw[0:TAPS * KT - P, 1], g.ident[0:TAPS * KT - P, 0:TAPS * KT - P])
            pe.transpose(ps_g[:, 256:256 + VECS * KT], raw[0:VECS * KT, 2], g.ident[0:VECS * KT, 0:VECS * KT]).then_inc(cols_t, 1)
            pe.wait_ge(st_in, 32)
            n = DB * HIST // 2
            for h in range(2):
                after(pe, st_copied, h)
                for k in range(KT):
                    last = pe.transpose(ps_t[:, k, 0:n], x[0:n, h, k * P:(k + 1) * P], g.ident[0:n, 0:n])
                last.then_inc(st_t, 1)
            pe.wait_ge(st_copied, 2)

            def turn_x(T, t, p):
                n = rows_of(t)
                pe.wait_ge(xs_ready, T + 1)
                after(pe, lo_ready, T)
                for k in range(KT):
                    last = pe.transpose(ps_t[:, k, 0:n], xs[0:n, k * P:(k + 1) * P], g.ident[0:n, 0:n])
                last.then_inc(xt_done, 1)

            def body(T, t, p, s):
                n = rows_of(t)
                first = isinstance(t, int) and t == 0
                gate_of = lambda m: (g.w_lo, KT * (3 * s + m)) if first else None
                pe.wait_ge(lo_ready, T + 1)
                after(pe, sig_ready, T)
                if isinstance(T, int) and T == 0:
                    pe.wait_ge(cols_ready, 2)
                project(pe, ps_g[0:n], xt[p], g.wslot[GATE], n, gate_of(GATE)).then_inc(g_mm, 1)
                after(pe, v_ready, T)
                project(pe, ps_a[0:n], xt[p], g.wslot[VALUE], n, gate_of(VALUE)).then_inc(a_mm, 1)
                if not (isinstance(T, int) and T == 2 * ALL - 1):
                    turn_x(T + 1, (t + 1) % ALL if isinstance(t, int) else t + 1, 1 - p)
                after(pe, z_copied, T)
                project(pe, ps_z[0:n], xt[p], g.wslot[ZGATE], n, gate_of(ZGATE)).then_inc(z_mm, 1)
                pe.wait_ge(v_ready, T + 1)
                after(pe, vt_copied, T)
                for j in range(CT):
                    last = pe.transpose(ps_v[:, j, 0:n], v[0:n, p, j * P:(j + 1) * P], g.ident[0:n, 0:n])
                last.then_inc(vt_done, 1)

            turn_x(0, 0, 0)
            for s in range(2):
                B = s * ALL
                for t in range(2):
                    body(B + t, t, (B + t) % 2, s)
                with pe.Fori(1, TILES // 2 - 1) as i:
                    for q in range(2):
                        body(B + i * 2 + q, i * 2 + q, (B + q) % 2, s)
                for t in range(TILES - 2, ALL):
                    body(B + t, t, (B + t) % 2, s)


def phase_b(nc, io, g):
    with ExitStack() as ctx:
        sb = lambda name, shape, dt=F32: ctx.enter_context(nc.sbuf_tensor(name, shape, dt))
        pb = lambda name, shape: ctx.enter_context(nc.psum_tensor(name, shape, F32))
        sem = lambda name: ctx.enter_context(nc.semaphore(name))

        OUT0, OUT1, KVS, Q0, Q1 = range(5)
        g.wslot = g.shared_slots + [sb(f"b_w{m}", [P, 2, KT, HALF], F32R) for m in range(2, 5)]
        x = sb("b_x", [P, D])
        y = sb("b_y", [P, D])
        yc = y[:, :].rearrange("p (k n) -> p k n", k=KT)
        yt = sb("b_yt", [P, 2, KT, P], F32R)
        ht = sb("b_ht", [P, 2, KT, P], F32R)
        hq = sb("b_hq", [P, 2 * D])
        early_stage = hq[:, :].rearrange("p (s n) -> p s n", s=STAGES)
        cz = sb("b_cz", [P, 2 * D])
        gate_stage = cz[:, :].rearrange("p (s n) -> p s n", s=STAGES)
        g.stage = early_stage
        c = cz[:, 0:D].rearrange("p (k n) -> p k n", k=KT)
        z = cz[:, D:2 * D]
        gains = {KVS: g.cols[:, KT:2 * KT], Q0: g.cols[:, 2 * KT:3 * KT], Q1: g.cols[:, 2 * KT:3 * KT]}
        h, qo = hq[:, 0:D], hq[:, D:2 * D]
        kvo = sb("b_kvo", [P, 2 * KV])
        kgain = sb("b_kgain", [P, HD])
        stats = sb("b_stats", [P, 2, 6])
        mv = sb("b_mv", [P, 2])
        pause = sb("b_pause", [P, 1])
        lms = sb("b_lms", [P, 1])
        lrs = sb("b_lrs", [P, 1])
        ss = sb("b_ss", [P, 1])
        ms = sb("b_ms", [P, 1])
        hss = sb("b_hss", [P, HEADS + KVH])
        hms = sb("b_hms", [P, HEADS + KVH])
        hrs = sb("b_hrs", [P, HEADS + KVH])

        ps_c = pb("b_psc", [P, D])
        ps_cc = ps_c[:, :].rearrange("p (k n) -> p k n", k=KT)
        ps_t = pb("b_pst", [P, KT, P])
        ps_o = pb("b_pso", [P, D])
        ps_q = pb("b_psq", [P, D])

        g.w_in = [sem(f"b_w_in{b}") for b in range(STAGES)]
        g.w_hi, g.w_lo = sem("b_w_hi"), sem("b_w_lo")
        (kg_in, c_in, z_in, x_in, x1_out, q_out, kv_out, copy_out, tc_done, tz_done, ty_done, th_done, out_mm, kv_mm,
         q_mm, stat_step, lms_ready, lrs_ready, yn_ready, sz_ready, y2_ready, prod_ready, yhi_ready, ylo_ready,
         x1_ready, ss_ready, ms_ready, rstd_ready, h_ready, hhi_ready, hlo_ready, ksq_ready, qsq_ready, v_ready,
         kss_ready, qss_ready, kms_ready, qms_ready, krs_ready, qrs_ready, kn_ready, k_ready, q_ready) = (
             sem("b_" + s) for s in (
                 "kg_in c_in z_in x_in x1_out q_out kv_out copy_out tc_done tz_done ty_done th_done out_mm kv_mm "
                 "q_mm stat_step lms_ready lrs_ready yn_ready sz_ready y2_ready prod_ready yhi_ready ylo_ready "
                 "x1_ready ss_ready ms_ready rstd_ready h_ready hhi_ready hlo_ready ksq_ready qsq_ready v_ready "
                 "kss_ready qss_ready kms_ready qms_ready krs_ready qrs_ready kn_ready k_ready q_ready").split())
        heads = lambda ap, m: ap.rearrange("p (h d) -> p h d", h=m)
        block = ctx.enter_context(nc.Block())

        def steady(eng, body):
            body(0)
            body(1)
            with eng.Fori(1, TILES // 2 - 1) as i:
                for q in range(2):
                    body(i * 2 + q)
            for t in range(TILES - 2, ALL):
                body(t)

        @block.sync
        def _(sp):
            sp.dma_start(kgain[:, :], io.k_norm.rearrange("(a d) -> a d", a=1).broadcast_to([P, HD])).then_inc(kg_in, 16)
            sp.dma_start(io.k_s[:, 0:P - DS, :], io.cache_k[:, DS:P, :]).then_inc(copy_out, 16)
            sp.dma_start(io.v_s[:, 0:P - DS, :], io.cache_v[:, DS:P, :]).then_inc(copy_out, 16)

            def load_c(t):
                after(sp, tc_done, t)
                n = rows_of(t)
                cols = slice(t * P, t * P + n) if isinstance(t, int) else bass.ds(t * P, P)
                sp.dma_start(c[:, :, 0:n], g.c_d.rearrange("(k p) n -> p k n", p=P)[:, :, cols]).then_inc(c_in, 16)

            def load_z(t):
                after(sp, tz_done, t)
                n = rows_of(t)
                sp.dma_start(z[0:n], token_rows(g.z_d, t, n)).then_inc(z_in, 16)

            def load_x(t):
                after(sp, x1_out, 16 * t)
                after(sp, h_ready, t)
                n = rows_of(t)
                sp.dma_start(x[0:n], io.x_sample if n == DEC else token_rows(io.x_prompt, t, n)).then_inc(x_in, 16)

            def store_x1(t):
                n = rows_of(t)
                sp.wait_ge(x1_ready, t + 1)
                sp.dma_start(token_rows(g.x1_d, t, n), x[0:n]).then_inc(x1_out, 16)

            def store_qkv(t):
                n = rows_of(t)
                sp.wait_ge(k_ready, t + 1)
                sp.wait_ge(v_ready, t + 1)
                sp.dma_start(token_rows(g.kv_d, t, n), kvo[0:n]).then_inc(kv_out, 16)
                if isinstance(t, int) and t == TILES - 1:
                    sp.dma_start(io.k_p, kvo[:, 0:KV]).then_inc(copy_out, 16)
                    sp.dma_start(io.v_p, kvo[:, KV:2 * KV]).then_inc(copy_out, 16)
                if n == DEC:
                    for b in range(DB):
                        rows = slice(b * DS, (b + 1) * DS)
                        sp.dma_start(io.k_s[b, P - DS:P, :], kvo[rows, 0:KV]).then_inc(copy_out, 16)
                        sp.dma_start(io.v_s[b, P - DS:P, :], kvo[rows, KV:2 * KV]).then_inc(copy_out, 16)
                sp.wait_ge(q_ready, t + 1)
                sp.dma_start(token_rows(g.q_d, t, n), qo[0:n]).then_inc(q_out, 16)

            load_c(0)
            load_z(0)
            load_x(0)
            for n, w in enumerate((io.w_kv, io.w_in_b[:, 0:HALF], io.w_in_b[:, HALF:D])):
                split_weights_dma(sp, w, g, n)
                if n == 0:
                    load_c(1)
                    load_z(1)

            def body(t):
                store_x1(t)
                if not isinstance(t, int) or t + 1 < ALL:
                    load_x(t + 1)
                if not isinstance(t, int) or t + 2 < ALL:
                    load_c(t + 2)
                    load_z(t + 2)
                if not (isinstance(t, int) and t == 0):
                    store_qkv(t - 1)
            steady(sp, body)
            sp.wait_ge(tc_done, ALL)
            sp.wait_ge(tz_done, ALL)
            g.stage = gate_stage
            for b in range(2):
                split_weights_dma(sp, io.w_in_b[:, D + b * HALF:D + (b + 1) * HALF], g, 3 + b)
            store_qkv(ALL - 1)
            sp.wait_ge(x1_out, 16 * ALL)
            sp.wait_ge(q_out, 16 * ALL)
            sp.wait_ge(kv_out, 16 * ALL)
            sp.wait_ge(copy_out, 16 * (2 + 2 + 2 * DB))

        @block.gpsimd
        def _(pool):
            def power(out, mid, src, n, eps, mid_ready, ready, t):
                after(pool, ready, t)
                pool.tensor_tensor(mid[0:n], src[0:n], eps[0:n, 0:out.shape[1]], ALU.add).then_inc(mid_ready, 1)
                pool.wait_ge(mid_ready, t + 1)
                pool.tensor_tensor(out[0:n], mid[0:n], g.half[0:n, 0:out.shape[1]], ALU.pow).then_inc(ready, 1)

            def layer(t):
                pool.wait_ge(stat_step, 3 * t + 3)
                after(pool, yn_ready, t)
                power(lrs[:, :], lms[:, :], mv[:, 1:2], rows_of(t), g.ln_eps, lms_ready, lrs_ready, t)

            def body(t):
                if not isinstance(t, int) or t + 1 < ALL:
                    layer(t + 1)
                pool.wait_ge(ss_ready, t + 1)
                after(pool, h_ready, t)
                power(g.rstd_b[:, t:t + 1] if isinstance(t, int) else g.rstd_b[:, bass.ds(t, 1)], ms[:, :], ss[:, :], rows_of(t), g.rms_eps,
                      ms_ready, rstd_ready, t)
                if isinstance(t, int) and t == 0:
                    return
                qk(t - 1)

            def qk(t):
                pool.wait_ge(kss_ready, t + 1)
                after(pool, k_ready, t)
                power(hrs[:, HEADS:], hms[:, HEADS:], hss[:, HEADS:], rows_of(t), g.rms_eps, kms_ready, krs_ready, t)
                pool.wait_ge(qss_ready, t + 1)
                after(pool, q_ready, t)
                power(hrs[:, 0:HEADS], hms[:, 0:HEADS], hss[:, 0:HEADS], rows_of(t), g.rms_eps, qms_ready, qrs_ready, t)

            layer(0)
            steady(pool, body)
            qk(ALL - 1)

        lng = g.cols[:, 4 * KT:5 * KT]
        lnb = g.cols[:, 5 * KT:6 * KT]

        @block.scalar
        def _(act):
            def silu_z(t):
                n = rows_of(t)
                act.wait_ge(z_in, 16 * (t + 1))
                act.activation(z[0:n], z[0:n], ACT.Silu).then_inc(sz_ready, 1)

            def silu_y(t):
                n = rows_of(t)
                act.wait_ge(ty_done, t + 1)
                for k in range(KT):
                    ins = act.activation(yc[:, k, 0:n], ps_t[:, k, 0:n], ACT.Silu, scale=lng[:, k:k + 1], bias=lnb[:, k:k + 1])
                ins.then_inc(y2_ready, 1)

            def cut_y(t):
                n = rows_of(t)
                act.wait_ge(prod_ready, t + 1)
                after(act, out_mm, t)
                act.activation(yt[:, 0, :, 0:n], yc[:, :, 0:n], ACT.Copy).then_inc(yhi_ready, 1)

            def square_x1(t):
                n = rows_of(t)
                act.wait_ge(x1_ready, t + 1)
                after(act, th_done, t)
                act.activation(h[0:n], x[0:n], ACT.Square, scale=D ** -0.5, accum_out=ss[0:n]).then_inc(ss_ready, 1)

            def scale_h(t):
                n = rows_of(t)
                act.wait_ge(rstd_ready, t + 1)
                rs = g.rstd_b[0:n, t:t + 1] if isinstance(t, int) else g.rstd_b[0:n, bass.ds(t, 1)]
                act.activation(h[0:n], x[0:n], ACT.Copy, scale=rs).then_inc(h_ready, 1)

            def cut_h(t):
                n = rows_of(t)
                act.wait_ge(th_done, t + 1)
                after(act, q_mm, t)
                act.activation(ht[:, 0, :, 0:n], ps_t[:, :, 0:n], ACT.Copy).then_inc(hhi_ready, 1)

            def qkv(t):
                n = rows_of(t)
                act.wait_ge(kv_mm, t + 1)
                after(act, kv_out, 16 * t)
                if isinstance(t, int) and t == TILES:
                    act.wait_ge(copy_out, 16 * 4)
                act.activation(kvo[0:n, 0:KV], ps_o[0:n, 0:KV], ACT.Square, scale=HD ** -0.5).then_inc(ksq_ready, 1)
                act.activation(kvo[0:n, KV:], ps_o[0:n, KV:2 * KV], ACT.Copy).then_inc(v_ready, 1)
                act.wait_ge(q_mm, t + 1)
                after(act, q_out, 16 * t)
                act.activation(qo[0:n], ps_q[0:n], ACT.Square, scale=HD ** -0.5).then_inc(qsq_ready, 1)

            def body(t):
                if not (isinstance(t, int) and t == 0):
                    cut_h(t - 1)
                more = not isinstance(t, int) or t + 1 < ALL
                if more:
                    silu_z(t + 1)
                square_x1(t)
                if more:
                    silu_y(t + 1)
                scale_h(t)
                if more:
                    cut_y(t + 1)
                if not (isinstance(t, int) and t == 0):
                    qkv(t - 1)

            silu_z(0)
            silu_y(0)
            cut_y(0)
            g.stage = early_stage
            for m in (KVS, Q0, Q1):
                split_weights_hi(act, m, gains[m], g, m - KVS)
            act.wait_ge(g.w_lo, 3 * KT)
            steady(act, body)
            g.stage = gate_stage
            split_weights_hi(act, 0, gains[Q0], g, 3, free=(out_mm, ALL), k1=STAGES)
            cut_h(ALL - 1)
            split_weights_hi(act, 0, gains[Q0], g, 3, k0=STAGES)
            split_weights_hi(act, 1, gains[Q0], g, 4)
            qkv(ALL - 1)

        @block.vector
        def _(dve):
            dve.wait_ge(kg_in, 16)

            def normalize(t):
                n = rows_of(t)
                dve.wait_ge(tc_done, t + 1)
                after(dve, lms_ready, t)
                for b in range(2):
                    dve.bn_stats(stats[0:n, b], ps_c[0:n, b * HALF:(b + 1) * HALF]).then_inc(stat_step, 1)
                dve.wait_ge(stat_step, 3 * t + 2)
                dve.memset(pause[:, :], 0.0)
                dve.bn_aggr(mv[0:n], stats[0:n].rearrange("p a b -> p (a b)")).then_inc(stat_step, 1)
                dve.wait_ge(stat_step, 3 * t + 3)
                dve.wait_ge(lrs_ready, t + 1)
                after(dve, ylo_ready, t)
                dve.tensor_scalar(y[0:n], ps_c[0:n], mv[0:n, 0:1], lrs[0:n, 0:1], ALU.subtract, ALU.mult).then_inc(yn_ready, 1)

            def gate(t):
                n = rows_of(t)
                dve.wait_ge(y2_ready, t + 1)
                dve.wait_ge(tz_done, t + 1)
                dve.tensor_tensor(yc[:, :, 0:n], yc[:, :, 0:n], ps_cc[:, :, 0:n], ALU.mult).then_inc(prod_ready, 1)
                dve.wait_ge(yhi_ready, t + 1)
                dve.tensor_tensor(yt[:, 1, :, 0:n], yc[:, :, 0:n], f32(yt[:, 0, :, 0:n]), ALU.subtract).then_inc(ylo_ready, 1)

            def residual(t):
                n = rows_of(t)
                dve.wait_ge(out_mm, t + 1)
                dve.wait_ge(x_in, 16 * (t + 1))
                dve.tensor_tensor(x[0:n], ps_o[0:n], x[0:n], ALU.add).then_inc(x1_ready, 1)

            def cut_h(t):
                n = rows_of(t)
                dve.wait_ge(hhi_ready, t + 1)
                dve.tensor_tensor(ht[:, 1, :, 0:n], ps_t[:, :, 0:n], f32(ht[:, 0, :, 0:n]), ALU.subtract).then_inc(hlo_ready, 1)

            def keys(t):
                n = rows_of(t)
                dve.wait_ge(ksq_ready, t + 1)
                after(dve, kms_ready, t)
                dve.tensor_reduce(hss[0:n, HEADS:], heads(kvo[0:n, 0:KV], KVH), AX_X, ALU.add).then_inc(kss_ready, 1)
                dve.wait_ge(krs_ready, t + 1)
                dve.wait_ge(v_ready, t + 1)
                rs = hrs[0:n, HEADS:].rearrange("p (h a) -> p h a", a=1).broadcast_to([n, KVH, HD])
                dve.tensor_tensor(heads(kvo[0:n, 0:KV], KVH), heads(ps_o[0:n, 0:KV], KVH), rs, ALU.mult).then_inc(kn_ready, 1)
                dve.wait_ge(kn_ready, t + 1)
                kg = kgain[0:n, :].rearrange("p (a d) -> p a d", a=1).broadcast_to([n, KVH, HD])
                dve.tensor_tensor(heads(kvo[0:n, 0:KV], KVH), heads(kvo[0:n, 0:KV], KVH), kg, ALU.mult).then_inc(k_ready, 1)

            def query_sums(t):
                n = rows_of(t)
                dve.wait_ge(qsq_ready, t + 1)
                after(dve, qms_ready, t)
                dve.tensor_reduce(hss[0:n, 0:HEADS], heads(qo[0:n], HEADS), AX_X, ALU.add).then_inc(qss_ready, 1)

            def queries(t):
                n = rows_of(t)
                dve.wait_ge(qrs_ready, t + 1)
                rs = hrs[0:n, 0:HEADS].rearrange("p (h a) -> p h a", a=1).broadcast_to([n, HEADS, HD])
                dve.tensor_tensor(heads(qo[0:n], HEADS), heads(ps_q[0:n], HEADS), rs, ALU.mult).then_inc(q_ready, 1)

            def body(t):
                if not (isinstance(t, int) and t == 0):
                    cut_h(t - 1)
                if not (isinstance(t, int) and t < 2):
                    queries(t - 2)
                more = not isinstance(t, int) or t + 1 < ALL
                if more:
                    normalize(t + 1)
                residual(t)
                if more:
                    gate(t + 1)
                if not (isinstance(t, int) and t == 0):
                    keys(t - 1)
                    query_sums(t - 1)

            normalize(0)
            gate(0)
            g.stage = early_stage
            for m in (KVS, Q0, Q1):
                split_weights_lo(dve, m, gains[m], g, m - KVS)
            steady(dve, body)
            queries(ALL - 2)
            g.stage = gate_stage
            split_weights_lo(dve, 0, gains[Q0], g, 3, k1=STAGES)
            cut_h(ALL - 1)
            split_weights_lo(dve, 0, gains[Q0], g, 3, k0=STAGES)
            split_weights_lo(dve, 1, gains[Q0], g, 4)
            keys(ALL - 1)
            query_sums(ALL - 1)
            queries(ALL - 1)

        @block.tensor
        def _(pe):
            def turn_c(t):
                n = rows_of(t)
                pe.wait_ge(c_in, 16 * (t + 1))
                after(pe, prod_ready, t)
                for k in range(KT):
                    ins = pe.transpose(ps_c[0:n, k * P:(k + 1) * P], c[:, k, 0:n], g.ident[:, :])
                ins.then_inc(tc_done, 1)

            def turn(out, src, t, done):
                n = rows_of(t)
                for k in range(KT):
                    ins = pe.transpose(out[:, k, 0:n], src[0:n, k * P:(k + 1) * P], g.ident[0:n, 0:n])
                ins.then_inc(done, 1)

            def turn_y(t):
                pe.wait_ge(yn_ready, t + 1)
                after(pe, hlo_ready, t - 1)
                turn(ps_t, y, t, ty_done)

            def turn_z(t):
                pe.wait_ge(sz_ready, t + 1)
                turn(ps_cc, z, t, tz_done)

            def turn_h(t):
                pe.wait_ge(h_ready, t + 1)
                after(pe, y2_ready, t + 2 if not isinstance(t, int) else min(t + 2, ALL))
                turn(ps_t, h, t, th_done)

            def out(t):
                n = rows_of(t)
                pe.wait_ge(ylo_ready, t + 1)
                after(pe, k_ready, t - 1)
                after(pe, v_ready, t - 1)
                for b in range(2):
                    ins = project(pe, ps_o[0:n, b * HALF:(b + 1) * HALF], yt, g.wslot[OUT0 + b], n)
                ins.then_inc(out_mm, 1)

            def qkv(t, gate=False):
                n = rows_of(t)
                pe.wait_ge(hlo_ready, t + 1)
                after(pe, x1_ready, t + 2 if not isinstance(t, int) else min(t + 2, ALL))
                project(pe, ps_o[0:n, 0:HALF], ht, g.wslot[KVS], n, (g.w_lo, 0) if gate else None).then_inc(kv_mm, 1)
                after(pe, q_ready, t)
                for b in range(2):
                    ins = project(pe, ps_q[0:n, b * HALF:(b + 1) * HALF], ht, g.wslot[Q0 + b], n,
                                  (g.w_lo, KT * (1 + b)) if gate else None)
                ins.then_inc(q_mm, 1)

            def body(t):
                more = not isinstance(t, int) or t + 1 < ALL
                if more:
                    turn_c(t + 1)
                out(t)
                if more:
                    turn_y(t + 1)
                    turn_z(t + 1)
                if not (isinstance(t, int) and t == 0):
                    qkv(t - 1, gate=isinstance(t, int) and t == 1)
                turn_h(t)

            turn_c(0)
            turn_y(0)
            turn_z(0)
            steady(pe, body)
            qkv(ALL - 1)


def phase_c(nc, io, g):
    with ExitStack() as ctx:
        sb = lambda name, shape, dt=F32: ctx.enter_context(nc.sbuf_tensor(name, shape, dt))
        pb = lambda name, shape: ctx.enter_context(nc.psum_tensor(name, shape, F32))
        sem = lambda name: ctx.enter_context(nc.semaphore(name))

        Z0, Z1, OUT0, OUT1 = range(4)
        g.wslot = g.shared_slots + [sb(f"c_w{m}", [P, 2, KT, HALF], F32R) for m in range(2, 4)]
        hx = sb("c_hx", [P, D])
        xr = sb("c_xr", [P, D])
        ht = sb("c_ht", [P, 2, KT, P], F32R)
        ot = sb("c_ot", [P, 2, KT, P], F32R)
        q = sb("c_q", [P, D])
        qt = sb("c_qt", [P, KT, P])
        kd = sb("c_kd", [P, 2, KVH, 2, HD])
        kt = sb("c_kt", [P, 2, KVH, P])
        v = sb("c_v", [P, 2, KV])
        bias = sb("c_bias", [P, HEADS, 2 * P])
        s = sb("c_s", [P, 2, GROUP, 2 * P])
        g.stages = 2
        g.stage = xr[:, :].rearrange("p (s n) -> p s n", s=2)
        pt = sb("c_pt", [P, 2, GROUP, P])
        sz = sb("c_sz", [P, D])
        sink0 = sb("c_sink0", [P, HEADS])
        sink = sb("c_sink", [P, HEADS])
        nsink = sb("c_nsink", [P, HEADS])
        sinkd = sb("c_sinkd", [P, 2])
        nm = sb("c_nm", [P, 2, GROUP])
        es = sb("c_es", [P, 2, GROUP])
        den = sb("c_den", [P, 2, GROUP])
        rden = sb("c_rden", [P, 2, GROUP])
        dist = pt[:, 0, 0:2].rearrange("p a b -> p (a b)")
        ddist = sb("c_ddist", [P, P + DS + 1])
        vn = sb("c_vn", [DS, 2, KV])

        acc = pb("c_acc", [P, HALF])
        ps_t = pb("c_pst", [P, KT, P])
        ps_s = pb("c_pss", [P, GROUP, 2 * P])
        ps_p = pb("c_psp", [P, 2, GROUP, P])
        ps_o = pb("c_pso", [P, HALF])

        g.w_in = [sem(f"c_w_in{b}") for b in range(g.stages)]
        g.w_hi, g.w_lo = sem("c_w_hi"), sem("c_w_lo")
        k_in = [sem("c_k_in0"), sem("c_k_in1")]
        kn_in = [sem("c_kn_in0"), sem("c_kn_in1")]
        v_in = [sem("c_v_in0"), sem("c_v_in1")]
        (tab_in, hx_in, xr_in, q_in, y_out, bias_made, nsink_made, h_ready, th_done, hhi_ready, hlo_ready,
         tq_done, qt_ready, tk_done, kt_ready, z_mm, ztanh_ready, zg_done, qk_done, s_read, m_ready, nm_ready,
         es_in, es_ready, p_ready, den_ready, rden_ready, pn_ready, tp_done, pt_ready, pv_done, o_done, to_done,
         ohi_ready, olo_ready, out_mm, res_done, szt_done, szt_ready, od_ready) = (sem("c_" + x) for x in (
             "tab_in hx_in xr_in q_in y_out bias_made nsink_made h_ready th_done hhi_ready hlo_ready "
             "tq_done qt_ready tk_done kt_ready z_mm ztanh_ready zg_done qk_done s_read m_ready nm_ready "
             "es_in es_ready p_ready den_ready rden_ready pn_ready tp_done pt_ready pv_done o_done to_done "
             "ohi_ready olo_ready out_mm res_done szt_done szt_ready od_ready").split())
        WAVES = DB // GROUP
        GD = TILES * KVH
        DK = P + DS
        slope = [2.0 ** (-8.0 * (h + 1) / HEADS) for h in range(HEADS)]
        SCALE = HD ** -0.5
        place = lambda j: 2 * (j % 2) + j // 2
        szc = sz[:, :].rearrange("p (k n) -> p k n", k=KT)
        qc = q[:, :].rearrange("p (k n) -> p k n", k=KT)
        qd = qt[0:HD, :, :].rearrange("p a b -> p (a b)")
        knt = bias[:, 0:4, 0:DEC]
        block = ctx.enter_context(nc.Block())

        def loop(eng, body):
            body(0, 0)
            body(1, 1)
            with eng.Fori(1, TILES // 2 - 1) as i:
                for r in range(2):
                    body(i * 2 + r, r)
            body(TILES - 2, 0)
            body(TILES - 1, 1)

        halves = lambda t: (1,) if isinstance(t, int) and t == 0 else (0, 1)
        keys_of = lambda t: slice(P, 2 * P) if isinstance(t, int) and t == 0 else slice(0, 2 * P)

        @block.sync
        def _(sp):
            def load_h(t):
                after(sp, th_done, t)
                n = rows_of(t)
                sp.dma_start(hx[0:n], token_rows(g.x1_d, t, n)).then_inc(hx_in, 16)

            def load_q(t):
                after(sp, tq_done, t)
                n = rows_of(t)
                sp.dma_start(q[0:n], token_rows(g.q_d, t, n)).then_inc(q_in, 16)

            def load_k(t, p, src=None):
                after(sp, tk_done, t - 1)
                n = P if src is not None else rows_of(t)
                src = token_rows(g.kv_d, t, n)[:, 0:KV] if src is None else src
                for e in range(2):
                    sp.dma_start(kd[0:n, p, :, e], src.rearrange("n (h d) -> n h d", h=KVH)).then_inc(k_in[p], 16)

            def load_v(t, r):
                if not (isinstance(t, int) and t < 2):
                    sp.wait_ge(pv_done, t * KVH)
                sp.dma_start(v[:, r], token_rows(g.kv_d, t, P)[:, KV:2 * KV]).then_inc(v_in[r], 16)

            def load_res(t):
                after(sp, y_out, 16 * t)
                n = rows_of(t)
                sp.dma_start(xr[0:n], token_rows(g.x1_d, t, n)).then_inc(xr_in, 16)

            def store_y(t):
                n = rows_of(t)
                sp.wait_ge(res_done, 2 * t + 2)
                sp.dma_start(io.y_s if n == DEC else token_rows(io.y_p, t, n), xr[0:n]).then_inc(y_out, 16)

            sp.dma_start(dist[:, :], io.distance).then_inc(tab_in, 16)
            sp.dma_start(ddist[:, :], io.decode_distance).then_inc(tab_in, 16)
            sp.dma_start(sink0[:, :], io.sinks.broadcast_to([P, HEADS])).then_inc(tab_in, 16)
            for h in range(HEADS):
                sp.dma_start(sinkd[h * DS:(h + 1) * DS, 0:1], io.sinks[:, h:h + 1].broadcast_to([DS, 1])).then_inc(tab_in, 16)
            load_h(0)
            load_q(0)
            load_k(0, 0)
            load_v(0, 0)
            split_weights_dma(sp, io.w_out_b[:, 0:HALF], g, 0, k1=g.stages)

            def body(t, r):
                first = isinstance(t, int) and t == 0
                load_h(t + 1)
                if not first:
                    load_res(t - 1)
                load_q(t + 1)
                load_k(t + 1, 1 - r)
                if not first:
                    store_y(t - 1)
                if not (isinstance(t, int) and t == TILES - 1):
                    load_v(t + 1, 1 - r)
                if first:
                    split_weights_dma(sp, io.w_out_b[:, 0:HALF], g, 0, k0=g.stages)
                    split_weights_dma(sp, io.w_out_b[:, HALF:D], g, 1)
                    sp.wait_ge(g.w_lo, 2 * KT)
            loop(sp, body)
            load_res(TILES - 1)

            def load_cache(b):
                after(sp, pv_done, max(GD, GD + b - 1))
                sp.dma_start(v[:, b % 2], io.cache_v[b]).then_inc(v_in[b % 2], 16)
                sp.dma_start(vn[:, b % 2], g.kv_d[SEQ + b * DS:SEQ + (b + 1) * DS, KV:2 * KV]).then_inc(kn_in[b % 2], 16)
            load_cache(0)
            load_cache(1)
            for b in range(DB):
                load_k(ALL + b, (ALL + b) % 2, io.cache_k[b])
            store_y(TILES - 1)
            load_res(TILES)
            for b in range(2, DB):
                load_cache(b)
            store_y(TILES)
            sp.wait_ge(y_out, 16 * ALL)

        @block.scalar
        def _(act):
            def scale_h(t):
                n = rows_of(t)
                act.wait_ge(hx_in, 16 * (t + 1))
                rs = g.rstd_b[0:n, t:t + 1] if isinstance(t, int) else g.rstd_b[0:n, bass.ds(t, 1)]
                act.activation(hx[0:n], hx[0:n], ACT.Copy, scale=rs).then_inc(h_ready, 1)

            def cut_h(t):
                n = rows_of(t)
                act.wait_ge(th_done, t + 1)
                after(act, z_mm, 2 * t)
                act.activation(ht[:, 0, :, 0:n], ps_t[:, :, 0:n], ACT.Copy).then_inc(hhi_ready, 1)

            def cut_o(t):
                n = rows_of(t)
                if n == DEC:
                    act.wait_ge(od_ready, 1)
                    src = szc[:, :, 0:n]
                else:
                    act.wait_ge(to_done, t + 1)
                    src = ps_t[:, :, 0:n]
                after(act, out_mm, 2 * t)
                act.activation(ot[:, 0, :, 0:n], src, ACT.Copy).then_inc(ohi_ready, 1)

            def queries(t):
                act.wait_ge(tq_done, t + 1)
                if isinstance(t, int) and t == TILES:
                    after(act, qk_done, GD)
                    act.activation(qd.rearrange("p (b h i) -> p b h i", b=DB, h=HEADS),
                                   ps_t[0:HD, :, :].rearrange("p a c -> p (a c)").rearrange("p (h b i) -> p b h i", h=HEADS, b=DB), ACT.Copy, scale=g.qgain[0:HD]).then_inc(qt_ready, 1)
                else:
                    after(act, qk_done, KVH * t)
                    act.activation(qt[:, :, :], ps_t[:, :, :], ACT.Copy, scale=g.qgain[:, :]).then_inc(qt_ready, 1)

            def keys(t, r):
                act.wait_ge(tk_done, t + 1)
                if isinstance(t, int) and t == TILES:
                    act.activation(knt[:, :, :], acc[:, :].rearrange("p (h k) -> p h k", h=KVH)[:, :, 0:DEC], ACT.Copy).then_inc(kt_ready, 1)
                    return
                act.activation(kt[:, r], acc[:, :].rearrange("p (h k) -> p h k", h=KVH), ACT.Copy).then_inc(kt_ready, 1)

            def gate_tanh(t, b):
                n = rows_of(t)
                act.wait_ge(z_mm, 2 * t + b + 1)
                after(act, to_done, t)
                part = sz[0:n, b * HALF:(b + 1) * HALF]
                act.activation(part, acc[0:n], ACT.Tanh, scale=0.5).then_inc(ztanh_ready, 1)

            def exps(G, b, ks):
                act.wait_ge(nm_ready, G + 1)
                after(act, rden_ready, G - 1)
                act.wait_ge(es_in, G + 1)
                act.activation(es[:, b], es[:, b], ACT.Exp).then_inc(es_ready, 1)
                for j in range(GROUP):
                    ins = act.activation(s[:, b, j, ks], s[:, b, j, ks], ACT.Exp, bias=nm[:, b, j:j + 1], accum_out=den[:, b, j:j + 1])
                ins.then_inc(p_ready, 1)

            def turn_out(G, ks):
                act.wait_ge(tp_done, G + 1)
                after(act, pv_done, G)
                act.activation(pt[:, ks], ps_p[:, ks], ACT.Copy).then_inc(pt_ready, 1)

            scale_h(0)
            cut_h(0)
            queries(0)
            keys(0, 0)

            def body(t, r):
                hs = slice(1, 2) if isinstance(t, int) and t == 0 else slice(0, 2)
                ks = keys_of(t)
                first = isinstance(t, int) and t == 0
                split = lambda k: split_weights_hi(act, OUT0 + k // KT, 0.5, g, k // KT, k0=k % KT, k1=k % KT + 2) if first else None
                scale_h(t + 1)
                split(0)
                exps(t * KVH, 0, ks)
                gate_tanh(t, 0)
                if not first:
                    cut_o(t - 1)
                split(2)
                turn_out(t * KVH, hs)
                split(4)
                exps(t * KVH + 1, 1, ks)
                gate_tanh(t, 1)
                split(6)
                turn_out(t * KVH + 1, hs)
                split(8)
                exps(t * KVH + 2, 0, ks)
                cut_h(t + 1)
                split(10)
                turn_out(t * KVH + 2, hs)
                exps(t * KVH + 3, 1, ks)
                split(12)
                split(14)
                turn_out(t * KVH + 3, hs)
                queries(t + 1)
                keys(t + 1, 1 - r)
            loop(act, body)

            gate_tanh(TILES, 0)
            cut_o(TILES - 1)
            for b in range(DB):
                if b == GROUP:
                    gate_tanh(TILES, 1)
                keys(ALL + b, b % 2)
            for w in range(WAVES):
                exps(GD + w, w % 2, slice(0, DK))
            for b in range(DB):
                act.wait_ge(tp_done, GD + b + 1)
                act.wait_ge(pv_done, GD + max(b - 1, 0))
                act.activation(pt[:, b % 2, 0], ps_p[:, b % 2, 0], ACT.Copy)
                act.activation(pt[0:DS, b % 2, 1], ps_p[0:DS, b % 2, 1], ACT.Copy).then_inc(pt_ready, 1)
            act.wait_ge(szt_done, 1)
            act.activation(qc[:, :, 0:DEC], ps_t[:, :, 0:DEC], ACT.Copy).then_inc(szt_ready, 1)
            cut_o(TILES)

        @block.vector
        def _(dve):
            dve.wait_ge(tab_in, 16 * (3 + HEADS))
            for h in range(HEADS):
                ins = dve.tensor_scalar(bias[:, h - h % GROUP + place(h % GROUP)], dist[:, :], -slope[h], None, ALU.mult)
            ins.then_inc(bias_made, 1)
            ordered = lambda ap: ap.rearrange("p (g b a) -> p g b a", b=2, a=2)
            given = sink0[:, :].rearrange("p (g a b) -> p g b a", b=2, a=2)
            dve.tensor_scalar(ordered(sink[:, :]), given, 1.0, None, ALU.mult).then_inc(nsink_made, 1)
            dve.tensor_scalar(ordered(nsink[:, :]), given, -1.0, None, ALU.mult).then_inc(nsink_made, 1)
            dve.tensor_scalar(sinkd[:, 1:2], sinkd[:, 0:1], -1.0, None, ALU.mult).then_inc(nsink_made, 1)
            dve.tensor_scalar(ddist[:, 0:DK], ddist[:, 0:DK], ddist[:, DK:DK + 1], None, ALU.mult).then_inc(nsink_made, 1)

            def cut_h(t):
                n = rows_of(t)
                dve.wait_ge(hhi_ready, t + 1)
                dve.tensor_tensor(ht[:, 1, :, 0:n], ps_t[:, :, 0:n], f32(ht[:, 0, :, 0:n]), ALU.subtract).then_inc(hlo_ready, 1)

            def cut_o(t):
                n = rows_of(t)
                dve.wait_ge(ohi_ready, t + 1)
                src = szc if n == DEC else ps_t
                dve.tensor_tensor(ot[:, 1, :, 0:n], src[:, :, 0:n], f32(ot[:, 0, :, 0:n]), ALU.subtract).then_inc(olo_ready, 1)

            def gate(t, b):
                n = rows_of(t)
                k = 2 * t + b
                part = sz[0:n, b * HALF:(b + 1) * HALF]
                dve.wait_ge(ztanh_ready, k + 1)
                dve.scalar_tensor_tensor(part, part, 1.0, acc[0:n], ALU.add, ALU.mult).then_inc(zg_done, 1)

            def scores(G, t, kv, b):
                ks = keys_of(t)
                dve.wait_ge(qk_done, G + 1)
                after(dve, tp_done, G - 1)
                dve.scalar_tensor_tensor(s[:, b, :, ks], ps_s[:, :, ks], SCALE, bias[:, kv * GROUP:(kv + 1) * GROUP, ks],
                                         ALU.mult, ALU.add).then_inc(s_read, 1)
                dve.wait_ge(s_read, G + 1)
                dve.tensor_reduce(nm[:, b], s[:, b, :, ks], AX_X, ALU.max, negate=True).then_inc(m_ready, 1)
                sinks(G, b, nsink[:, kv * GROUP:(kv + 1) * GROUP], sink[:, kv * GROUP:(kv + 1) * GROUP])

            def sinks(G, b, minus, plus):
                dve.wait_ge(m_ready, G + 1)
                dve.tensor_tensor(nm[:, b], nm[:, b], minus, ALU.min).then_inc(nm_ready, 1)
                dve.wait_ge(nm_ready, G + 1)
                dve.tensor_tensor(es[:, b], plus, nm[:, b], ALU.add).then_inc(es_in, 1)

            def sums(G, b):
                dve.wait_ge(p_ready, G + 1)
                dve.wait_ge(es_ready, G + 1)
                dve.tensor_tensor(den[:, b], den[:, b], es[:, b], ALU.add).then_inc(den_ready, 1)
                dve.wait_ge(den_ready, G + 1)
                dve.reciprocal(rden[:, b], den[:, b]).then_inc(rden_ready, 1)

            def gated(G, kv, b):
                dve.wait_ge(pv_done, G + 1)
                dve.wait_ge(rden_ready, G + 1)
                for j in range(GROUP):
                    part = sz[:, (kv * GROUP + j) * HD:(kv * GROUP + j + 1) * HD]
                    ins = dve.scalar_tensor_tensor(part, ps_o[:, j * HD:(j + 1) * HD], rden[:, b, place(j):place(j) + 1], part, ALU.mult, ALU.mult)
                ins.then_inc(o_done, 1)

            def residual(t, b):
                n = rows_of(t)
                part = xr[0:n, b * HALF:(b + 1) * HALF]
                dve.wait_ge(out_mm, 2 * t + b + 1)
                dve.wait_ge(xr_in, 16 * (t + 1))
                dve.tensor_tensor(part, acc[0:n], part, ALU.add).then_inc(res_done, 1)

            cut_h(0)
            dve.wait_ge(bias_made, 1)
            dve.wait_ge(nsink_made, 4)

            def body(t, r):
                first = isinstance(t, int) and t == 0
                split = lambda k: split_weights_lo(dve, OUT0 + k // KT, 0.5, g, k // KT, k0=k % KT, k1=k % KT + 2) if first else None
                G = t * KVH
                split(0)
                scores(G, t, 0, 0)
                gate(t, 0)
                scores(G + 1, t, 1, 1)
                sums(G, 0)
                if not first:
                    cut_o(t - 1)
                split(2)
                sums(G + 1, 1)
                split(4)
                gate(t, 1)
                gated(G, 0, 0)
                split(6)
                scores(G + 2, t, 2, 0)
                split(8)
                gated(G + 1, 1, 1)
                sums(G + 2, 0)
                cut_h(t + 1)
                split(10)
                if not first:
                    residual(t - 1, 0)
                scores(G + 3, t, 3, 1)
                sums(G + 3, 1)
                if not first:
                    residual(t - 1, 1)
                gated(G + 2, 2, 0)
                split(12)
                split(14)
                gated(G + 3, 3, 1)
            loop(dve, body)

            gate(TILES, 0)
            cut_o(TILES - 1)
            dd = ddist[:, 0:DK].rearrange("p (a k) -> p a k", a=1).broadcast_to([P, GROUP, DK])
            for w in range(WAVES):
                G, b = GD + w, w % 2
                dve.wait_ge(qk_done, G + 1)
                dve.wait_ge(tp_done, G - 1)
                dve.scalar_tensor_tensor(s[:, b, :, 0:DK], ps_s[:, :, 0:DK], SCALE, dd, ALU.mult, ALU.add).then_inc(s_read, 1)
                dve.wait_ge(s_read, G + 1)
                dve.tensor_reduce(nm[:, b], s[:, b, :, 0:DK], AX_X, ALU.max, negate=True).then_inc(m_ready, 1)
                sinks(G, b, sinkd[:, 1:2].broadcast_to([P, GROUP]), sinkd[:, 0:1].broadcast_to([P, GROUP]))
                if w == 0:
                    gate(TILES, 1)
            for w in range(WAVES):
                G, b = GD + w, w % 2
                sums(G, b)
                dve.wait_ge(rden_ready, G + 1)
                for j in range(GROUP):
                    ins = dve.tensor_scalar(s[:, b, j, 0:DK], s[:, b, j, 0:DK], rden[:, b, j:j + 1], None, ALU.mult)
                ins.then_inc(pn_ready, 1)
                residual(TILES - 1, w)
            dve.wait_ge(pv_done, GD + DB)
            dve.wait_ge(szt_ready, 1)
            dve.tensor_tensor(szc[:, :, 0:DEC], ps_o[:, :].rearrange("p (k n) -> p k n", k=KT), qc[:, :, 0:DEC], ALU.mult).then_inc(od_ready, 1)
            dve.wait_ge(od_ready, 1)
            cut_o(TILES)
            residual(TILES, 0)
            residual(TILES, 1)

        @block.tensor
        def _(pe):
            def turn_h(t):
                n = rows_of(t)
                pe.wait_ge(h_ready, t + 1)
                if isinstance(t, int) and t <= 1:
                    after(pe, qt_ready, t)
                else:
                    pe.wait_ge(olo_ready, t - 1)
                for k in range(KT):
                    ins = pe.transpose(ps_t[:, k, 0:n], hx[0:n, k * P:(k + 1) * P], g.ident[0:n, 0:n])
                ins.then_inc(th_done, 1)

            def turn_q(t):
                pe.wait_ge(q_in, 16 * (t + 1))
                pe.wait_ge(hlo_ready, t + 1)
                if isinstance(t, int) and t == TILES:
                    flat = ps_t[0:HD, :, :].rearrange("p a b -> p (a b)")
                    for h in range(HEADS):
                        ins = pe.transpose(flat[:, h * DEC:(h + 1) * DEC], q[0:DEC, h * HD:(h + 1) * HD], g.ident[0:DEC, 0:DEC])
                else:
                    for k in range(KT):
                        ins = pe.transpose(ps_t[:, k], q[:, k * P:(k + 1) * P], g.ident[:, :])
                ins.then_inc(tq_done, 1)

            def turn_k(t, p):
                n = P if isinstance(t, int) and t >= ALL else rows_of(t)
                pe.wait_ge(k_in[p], 32 * (t // 2 + 1) if isinstance(t, int) else t * 16 + (32 if p == 0 else 16))
                for h in range(KVH):
                    ins = pe.transpose(acc[:, h * P:h * P + n], kd[0:n, p, h].rearrange("p e d -> p (e d)"), g.ident[0:n, 0:n])
                ins.then_inc(tk_done, 1)

            def qk(t, kv, r):
                G = t * KVH + kv
                pe.wait_ge(qt_ready, t + 1)
                pe.wait_ge(kt_ready, t + 1)
                after(pe, s_read, G)
                for j in range(GROUP):
                    h = kv * GROUP + j
                    e = h % 2
                    for half in halves(t):
                        ins = pe.matmul(ps_s[:, place(j), half * P:(half + 1) * P], qt[e * HD:(e + 1) * HD, h // 2],
                                        kt[e * HD:(e + 1) * HD, r if half else 1 - r, kv], start=True, stop=True)
                ins.then_inc(qk_done, 1)

            def turn_p(t, kv, b):
                G = t * KVH + kv
                pe.wait_ge(p_ready, G + 1)
                after(pe, pt_ready, G)
                for j in range(GROUP):
                    for half in halves(t):
                        ins = pe.transpose(ps_p[:, half, j], s[:, b, j, half * P:(half + 1) * P], g.ident[:, :])
                ins.then_inc(tp_done, 1)

            def pv(t, kv, r, loads):
                G = t * KVH + kv
                pe.wait_ge(pt_ready, G + 1)
                after(pe, o_done, G)
                if kv == 0:
                    pe.wait_ge(v_in[r], loads)
                for j in range(GROUP):
                    hv = halves(t)
                    for half in hv:
                        ins = pe.matmul(ps_o[:, j * HD:(j + 1) * HD], pt[:, half, place(j)], v[:, r if half else 1 - r, kv * HD:(kv + 1) * HD],
                                        start=(half == hv[0]), stop=(half == 1))
                ins.then_inc(pv_done, 1)

            def z(t, b):
                n = rows_of(t)
                pe.wait_ge(hlo_ready, t + 1)
                if b == 0:
                    pe.wait_ge(kt_ready, t + 1)
                else:
                    pe.wait_ge(zg_done, 2 * t + 1)
                project(pe, acc[0:n], ht, g.wslot[Z0 + b], n).then_inc(z_mm, 1)

            def turn_o(t):
                pe.wait_ge(o_done, KVH * (t + 1))
                pe.wait_ge(qt_ready, t + 2)
                for k in range(KT):
                    ins = pe.transpose(ps_t[:, k], sz[:, k * P:(k + 1) * P], g.ident[:, :])
                ins.then_inc(to_done, 1)

            def out(t, b, gate=False):
                n = rows_of(t)
                pe.wait_ge(olo_ready, t + 1)
                if b == 0:
                    pe.wait_ge(zg_done, 2 * t + 4 if n == P else 2 * ALL)
                else:
                    pe.wait_ge(res_done, 2 * t + 1)
                project(pe, acc[0:n], ot, g.wslot[OUT0 + b], n, (g.w_lo, KT * b) if gate else None).then_inc(out_mm, 1)

            turn_h(0)
            turn_q(0)
            turn_k(0, 0)

            def body(t, r):
                first = isinstance(t, int) and t == 0
                loads = 16 * (t // 2 + 1) if isinstance(t, int) else (t * 8 + (16 if r == 0 else 8))
                qk(t, 0, r)
                z(t, 0)
                if not first:
                    turn_o(t - 1)
                qk(t, 1, r)
                turn_p(t, 0, 0)
                z(t, 1)
                pv(t, 0, r, loads)
                qk(t, 2, r)
                turn_p(t, 1, 1)
                turn_h(t + 1)
                pv(t, 1, r, loads)
                if not first:
                    out(t - 1, 0, isinstance(t, int) and t == 1)
                qk(t, 3, r)
                turn_p(t, 2, 0)
                if not first:
                    out(t - 1, 1, isinstance(t, int) and t == 1)
                pv(t, 2, r, loads)
                turn_p(t, 3, 1)
                turn_q(t + 1)
                if first:
                    pe.wait_ge(zg_done, 2)
                else:
                    pe.wait_ge(res_done, t * 2)
                turn_k(t + 1, 1 - r)
                pv(t, 3, r, loads)
            loop(pe, body)

            z(TILES, 0)
            turn_o(TILES - 1)
            for w in range(WAVES):
                for j in range(GROUP):
                    b = GROUP * w + j
                    if j == 0:
                        pe.wait_ge(zg_done, 2 * TILES + 1 + w)
                        turn_k(ALL + b, (ALL + b) % 2)
                    pe.wait_ge(kt_ready, ALL + b + 1)
                    if j + 1 < GROUP:
                        turn_k(ALL + b + 1, (ALL + b + 1) % 2)
                    if j == 0:
                        after(pe, s_read, GD + w)
                    for kv in range(KVH):
                        rows = slice(kv * GROUP * DS, (kv + 1) * GROUP * DS)
                        qh = qd[:, b * P + kv * GROUP * DS:b * P + (kv + 1) * GROUP * DS]
                        pe.matmul(ps_s[rows, j, 0:P], qh, kt[0:HD, b % 2, kv], start=True, stop=True)
                        ins = pe.matmul(ps_s[rows, j, P:DK], qh, knt[0:HD, kv, b * DS:(b + 1) * DS], start=True, stop=True)
                ins.then_inc(qk_done, 1)
                if w == 0:
                    z(TILES, 1)
            pe.wait_ge(kt_ready, ALL + DB)
            out(TILES - 1, 0)
            out(TILES - 1, 1)
            pe.wait_ge(zg_done, 2 * ALL)
            pe.wait_ge(olo_ready, TILES)
            for k in range(KT):
                ins = pe.transpose(ps_t[:, k, 0:DEC], sz[0:DEC, k * P:(k + 1) * P], g.ident[0:DEC, 0:DEC])
            ins.then_inc(szt_done, 1)

            def turn_batch(b):
                w, j = divmod(b, GROUP)
                pe.wait_ge(pn_ready, w + 1)
                pe.wait_ge(pt_ready, GD + max(b - 1, 0))
                pe.transpose(ps_p[:, b % 2, 0], s[:, w % 2, j, 0:P], g.ident[:, :])
                pe.transpose(ps_p[0:DS, b % 2, 1], s[:, w % 2, j, P:DK], g.ident[:, :]).then_inc(tp_done, 1)

            turn_batch(0)
            for b in range(DB):
                if b + 1 < DB:
                    turn_batch(b + 1)
                pe.wait_ge(pt_ready, GD + b + 1)
                pe.wait_ge(v_in[b % 2], 16 * (TILES // 2 + b // 2 + 1))
                pe.wait_ge(kn_in[b % 2], 16 * (b // 2 + 1))
                if b == 0:
                    pe.wait_ge(o_done, GD)
                for kv in range(KVH):
                    for e in range(2):
                        to = ps_o[e * HD:(e + 1) * HD, :].rearrange("p (k n) -> p k n", k=KT)[:, 2 * kv:2 * kv + 2, b * DS:(b + 1) * DS]
                        col = lambda half, n: pt[0:n, b % 2, half, kv * 32:(kv + 1) * 32].rearrange("p (j i) -> p j i", i=DS)[:, e::2]
                        pe.matmul(to, v[:, b % 2, kv * HD:(kv + 1) * HD], col(0, P), start=True, stop=False)
                        ins = pe.matmul(to, vn[:, b % 2, kv * HD:(kv + 1) * HD], col(1, DS), start=False, stop=True)
                ins.then_inc(pv_done, 1)
            out(TILES, 0)
            out(TILES, 1)


def program(nc, io):
    g = Names()
    with ExitStack() as ctx:
        sb = lambda name, shape: ctx.enter_context(nc.sbuf_tensor(name, shape, F32))
        g.ident = sb("ident", [P, P])
        g.half = sb("minus_half", [P, HEADS + KVH])
        g.rms_eps = sb("rms_eps", [P, HEADS + KVH])
        g.ln_eps = sb("ln_eps", [P, 1])
        g.taps = sb("taps", [P, TAPS * KT])
        g.cols = sb("cols", [P, VECS * KT])
        g.qgain = sb("qgain", [P, 1])
        g.rstd_b = sb("rstd_b", [P, ALL])
        g.shared_slots = [ctx.enter_context(nc.sbuf_tensor(f"w{m}", [P, 2, KT, HALF], F32R)) for m in range(2)]
        scratch = lambda name, *shape: nc.dram_tensor(name, shape, F32, kind=SCRATCH).ap()
        g.c_d = scratch("c_d", D, TOK)
        g.z_d = scratch("z_d", TOK, D)
        g.x1_d = scratch("x1_d", TOK, D)
        g.q_d = scratch("q_d", TOK, D)
        g.kv_d = scratch("kv_d", TOK, 2 * KV)
        phase_a(nc, io, g)
        phase_b(nc, io, g)
        phase_c(nc, io, g)


SCRATCH = "Internal"
INPUTS = ("x_prompt", "x_sample", "state_conv", "cache_k", "cache_v", "norm_a", "w_in_a", "w_dw_a", "b_dw_a", "ln_g_a",
          "ln_b_a", "w_out_a", "norm_kv", "w_kv", "k_norm", "norm_b", "w_in_b", "q_norm", "sinks_b", "w_out_b")
OUTPUTS = (("y_p", (1, SEQ, D)), ("y_s", (DB, DS, D)), ("conv_p", (1, 1, HIST, D)), ("conv_s", (1, DB, HIST, D)),
           ("k_p", (1, P, KVH, HD)), ("v_p", (1, P, KVH, HD)), ("k_s", (DB, P, KVH, HD)), ("v_s", (DB, P, KVH, HD)))


def constants():
    far = 1e30
    i, j = np.arange(P)[:, None], np.arange(2 * P)[None, :]
    dist = (i + P - j).astype(np.float64)
    distance = np.where((dist >= 0) & (dist < P), dist, far).astype(np.float32)
    i, j = (np.arange(P) % DS)[:, None], np.arange(P + DS)[None, :]
    dist = (i + P - j).astype(np.float64)
    decode = np.where((dist >= 0) & (dist < P), dist, far)
    slope = -(2.0 ** (-8.0 * (np.arange(P) // DS + 1) / HEADS))[:, None]
    return {"distance": distance, "decode_distance": np.concatenate([decode, slope], 1).astype(np.float32)}


def build(nc, shapes):
    dram = lambda name, shape, kind: nc.dram_tensor(name, shape, F32, kind=kind).ap()
    a = {name: dram("in_" + name, shape, "ExternalInput") for name, shape in shapes.items()}
    o = {name: dram("out_" + name, shape, "ExternalOutput") for name, shape in OUTPUTS}
    flat = lambda ap: ap.rearrange("b w h d -> b w (h d)")
    io = Names()
    io.x_prompt = a["x_prompt"][0]
    io.x_sample = a["x_sample"].rearrange("b s d -> (b s) d")
    io.state = a["state_conv"][0]
    io.cache_k = flat(a["cache_k"])
    io.cache_v = flat(a["cache_v"])
    io.k_norm = a["k_norm"]
    io.norm_kv = a["norm_kv"]
    io.w_kv = a["w_kv"]
    io.norm_a = a["norm_a"][0]
    io.w_in_a = a["w_in_a"][0]
    io.w_dw_a = a["w_dw_a"][0]
    io.b_dw_a = a["b_dw_a"][0]
    io.ln_g_a = a["ln_g_a"][0]
    io.ln_b_a = a["ln_b_a"][0]
    io.w_out_a = a["w_out_a"][0]
    io.norm_b = a["norm_b"][0]
    io.w_in_b = a["w_in_b"][0]
    io.q_norm = a["q_norm"][0]
    io.sinks = a["sinks_b"]
    io.w_out_b = a["w_out_b"][0]
    io.distance = a["distance"]
    io.decode_distance = a["decode_distance"]
    io.y_p = o["y_p"][0]
    io.y_s = o["y_s"].rearrange("b s d -> (b s) d")
    io.conv_p = o["conv_p"][0, 0]
    io.conv_s = o["conv_s"][0]
    io.k_p = flat(o["k_p"])[0]
    io.v_p = flat(o["v_p"])[0]
    io.k_s = flat(o["k_s"])
    io.v_s = flat(o["v_s"])
    program(nc, io)


def kernel(**inputs):
    import concourse.bacc as bacc
    from concourse.bass_utils import run_bass_kernel_spmd

    nc = bacc.Bacc("TRN2", target_bir_lowering=False, num_devices=1)
    arrays = {name: np.ascontiguousarray(inputs[name]) for name in INPUTS}
    arrays.update(constants())
    build(nc, {name: array.shape for name, array in arrays.items()})
    r = run_bass_kernel_spmd(nc, [{"in_" + name: array for name, array in arrays.items()}], core_ids=[0])
    return tuple(r.results[0]["out_" + name] for name, _ in OUTPUTS)
```

```python
from contextlib import ExitStack

import numpy as np

import concourse.bass as bass
from concourse import mybir

F32 = mybir.dt.float32
F32R = mybir.dt.float32r
ALU = mybir.AluOpType
ACT = mybir.ActivationFunctionType
AX_X = mybir.AxisListType.X

P = 128
D = 1024
KT = D // P
SEQ = 2048
TILES = SEQ // P
DB, DS = 8, 8
DEC = DB * DS
TOK = SEQ + DEC
ALL = TILES + 1
TAPS = 31
VECS = 6
HIST = TAPS - 1
HALF = 512
CT = HALF // P
CHUNK = 4
CTOK = CHUNK * P
NCHUNK = TILES // CHUNK
HEADS, KVH, HD = 16, 4, 64
GROUP = HEADS // KVH
KV = KVH * HD
RMS_EPS = 1e-6
LN_EPS = 1e-5


class Names:
    pass


def after(eng, sem, count):
    if isinstance(count, int) and count <= 0:
        return
    eng.wait_ge(sem, count)


def rows_of(tile):
    return DEC if isinstance(tile, int) and tile % ALL == TILES else P


def f32(ap):
    return ap.bitcast(F32)


def token_rows(dram, t, n):
    return dram[bass.ds(t * P, n), :] if not isinstance(t, int) else dram[t * P:t * P + n, :]


STAGES = 4
PTAPS = 12
DTAPS = TAPS - PTAPS
RING = 4


def split_weights_dma(sp, weights, g, n0, k0=0, k1=KT):
    for k in range(k0, k1):
        piece = KT * n0 + k
        after(sp, g.w_lo, piece - g.stages + 1)
        sp.dma_start(g.stage[:, piece % g.stages], weights[k * P:(k + 1) * P, :]).then_inc(g.w_in[piece % g.stages], 16)


def gain_of(gain, k):
    return gain if isinstance(gain, float) else gain[:, k:k + 1]


def split_weights_hi(act, m, gain, g, n0, free=None, k0=0, k1=KT):
    if free is not None:
        act.wait_ge(*free)
    for k in range(k0, k1):
        piece = KT * n0 + k
        act.wait_ge(g.w_in[piece % g.stages], 16 * (piece // g.stages + 1))
        act.activation(g.wslot[m][:, 0, k], g.stage[:, piece % g.stages], ACT.Copy, scale=gain_of(gain, k)).then_inc(g.w_hi, 1)


def split_weights_lo(dve, m, gain, g, n0, k0=0, k1=KT):
    for k in range(k0, k1):
        piece = KT * n0 + k
        dve.wait_ge(g.w_hi, piece + 1)
        dve.scalar_tensor_tensor(g.wslot[m][:, 1, k], g.stage[:, piece % g.stages],
                                 gain_of(gain, k), f32(g.wslot[m][:, 0, k]),
                                 ALU.mult, ALU.subtract).then_inc(g.w_lo, 1)


def project(pe, out, xt, w, n, lo_gate=None):
    for k in range(KT):
        if lo_gate is not None:
            pe.wait_ge(lo_gate[0], lo_gate[1] + k + 1)
        for a, b in ((0, 0), (1, 0), (0, 1)):
            last = pe.matmul(out, xt[:, a, k, 0:n], w[:, b, k], start=(k == 0 and a == 0 and b == 0),
                             stop=(k == KT - 1 and b == 1))
    return last


def phase_a(nc, io, g):
    with ExitStack() as ctx:
        sb = lambda name, shape, dt=F32: ctx.enter_context(nc.sbuf_tensor(name, shape, dt))
        pb = lambda name, shape: ctx.enter_context(nc.psum_tensor(name, shape, F32))
        sem = lambda name: ctx.enter_context(nc.semaphore(name))

        g.wslot = g.shared_slots + [sb("a_w2", [P, 2, KT, HALF], F32R)]
        g.stages = STAGES
        g.stage = sb("a_stage", [P, STAGES, HALF])
        x = sb("a_x", [P, 2, D])
        xs = sb("a_xs", [P, D])
        xt = [sb(f"a_xt{p}", [P, 2, KT, P], F32R) for p in range(2)]
        sig = sb("a_sig", [P, HALF])
        v = sb("a_v", [P, 2, HALF])
        zo = sb("a_zo", [P, 2, HALF])
        vbuf = sb("a_vbuf", [P, CT, HIST + SEQ])
        vdec = sb("a_vdec", [P, KT, DB, HIST + DS])
        csum = sb("a_csum", [P, CT, CTOK])
        prod = sb("a_prod", [P, RING, CTOK])
        dacc = sb("a_dacc", [P, CT, DEC])
        raw = sb("a_raw", [P, 3, P])
        ss = sb("a_ss", [P, 2])
        ms = sb("a_ms", [P, 2])
        rstd = sb("a_rstd", [P, 2])

        ps_t = pb("a_pst", [P, KT, P])
        ps_g, ps_a, ps_z = (pb(f"a_ps{n}", [P, HALF]) for n in "gaz")
        ps_v = pb("a_psv", [P, CT, P])
        acc = pb("a_acc", [P, 2, CTOK])

        g.w_in = [sem(f"a_w_in{b}") for b in range(STAGES)]
        g.w_hi, g.w_lo = sem("a_w_hi"), sem("a_w_lo")
        x_in = [sem("a_x_in0"), sem("a_x_in1")]
        v_out = [sem("a_v_out0"), sem("a_v_out1")]
        z_out = [sem("a_z_out0"), sem("a_z_out1")]
        (raw_in, st_in, eps_made, ident_made, cols_t, cols_ready, hist_zero, st_t, st_copied, ss_ready, ms_ready, rstd_ready,
         xs_ready, xt_done, hi_ready, lo_ready, g_mm, a_mm, z_mm, sig_ready, v_ready, z_copied, vt_done, vt_copied,
         conv_step, prod_ready, prod_added, dec_step, c_out, d_out, copy_out, left_out) = (sem("a_" + s) for s in (
             "raw_in st_in eps_made ident_made cols_t cols_ready hist_zero st_t st_copied ss_ready ms_ready rstd_ready "
             "xs_ready xt_done hi_ready lo_ready g_mm a_mm z_mm sig_ready v_ready z_copied vt_done vt_copied "
             "conv_step prod_ready prod_added dec_step c_out d_out copy_out left_out").split())

        w_in = io.w_in_a
        GATE, VALUE, ZGATE = 0, 1, 2
        col = lambda s, m: ((D, 0, 2 * D)[m]) + s * HALF
        na = g.cols[:, 0:KT]
        wcol = lambda k, ch: g.taps[:, k * KT + ch:k * KT + ch + 1]
        taps_done = lambda gc, pair, k, j: ((gc * 2 + pair) * DTAPS + k) * 2 + j + 1
        turn = (2, 3, 0, 1)
        bcol = lambda ch: g.cols[:, 3 * KT + ch:3 * KT + ch + 1]
        block = ctx.enter_context(nc.Block())

        @block.sync
        def _(sp):
            taps = io.w_dw_a.rearrange("w (j p) -> (w j) p", p=P)
            sp.dma_start(raw[:, 0], taps[0:P, :]).then_inc(raw_in, 16)
            sp.dma_start(raw[0:TAPS * KT - P, 1], taps[P:TAPS * KT, :]).then_inc(raw_in, 16)
            for n, vec in enumerate((io.norm_a, io.norm_kv, io.norm_b, io.b_dw_a, io.ln_g_a, io.ln_b_a)):
                sp.dma_start(raw[n * KT:(n + 1) * KT, 2], vec.rearrange("(j p) -> j p", p=P)).then_inc(raw_in, 16)
            for h in range(2):
                sp.dma_start(g.qgain[h * HD:(h + 1) * HD, :], io.q_norm.rearrange("(p a) -> p a", a=1)).then_inc(raw_in, 16)
            state = io.state.rearrange("b w c -> (b w) c")
            for h in range(2):
                sp.dma_start(x[0:DB * HIST // 2, h], state[h * DB * HIST // 2:(h + 1) * DB * HIST // 2, :]).then_inc(st_in, 16)
            sp.dma_start(io.conv_s[:, 0:HIST - DS, :], io.state[:, DS:HIST, :]).then_inc(copy_out, 16)

            def load_x(T, t, p):
                if isinstance(T, int) and T < 2:
                    sp.wait_ge(st_t, T + 1)
                after(sp, xs_ready, T - 1)
                n = rows_of(t)
                src = io.x_sample if n == DEC else token_rows(io.x_prompt, t, n)
                sp.dma_start(x[0:n, p], src).then_inc(x_in[p], 16)

            def store(T, t, p, s):
                n = rows_of(t)
                sp.wait_ge(z_copied, T + 1)
                sp.dma_start(token_rows(g.z_d, t, n)[:, s * HALF:(s + 1) * HALF], zo[0:n, p]).then_inc(z_out[p], 16)

            def store_state(T, t, p, s):
                sp.wait_ge(v_ready, T + 1)
                cols = slice(s * HALF, (s + 1) * HALF)
                if t == TILES:
                    for b in range(DB):
                        sp.dma_start(io.conv_s[b, HIST - DS:HIST, cols], v[b * DS:(b + 1) * DS, p]).then_inc(v_out[p], 16)
                else:
                    sp.dma_start(io.conv_p[:, cols], v[P - HIST:P, p]).then_inc(v_out[p], 16)

            def store_c(gc, c, s):
                for j in range(CT):
                    if j < 2:
                        sp.wait_ge(prod_added, (gc * CT + j + 3) * PTAPS)
                    else:
                        sp.wait_ge(conv_step, taps_done(gc, 1, DTAPS - 1, j - 2))
                    dst = g.c_d[(s * CT + j) * P:(s * CT + j + 1) * P, :]
                    dst = dst[:, bass.ds(c * CTOK, CTOK)] if not isinstance(c, int) else dst[:, c * CTOK:(c + 1) * CTOK]
                    sp.dma_start(dst, csum[:, j]).then_inc(c_out, 16)

            def store_dec():
                for j in range(CT):
                    sp.wait_ge(dec_step, (TAPS - 1) * CT + j + 1)
                    sp.dma_start(g.c_d[j * P:(j + 1) * P, SEQ:TOK], dacc[:, j]).then_inc(d_out, 16)

            def leave_v(n0, n1):
                first = (NCHUNK - 1) * CTOK
                sp.dma_start(g.v_left.rearrange("(j p) n -> p j n", p=P)[:, :, n0 - first:n1 - first], vbuf[:, :, n0:n1]).then_inc(left_out, 16)

            load_x(0, 0, 0)
            load_x(1, 1, 1)
            for s in range(2):
                for m in range(3):
                    if s == 0 or m == ZGATE:
                        split_weights_dma(sp, w_in[:, col(s, m):col(s, m) + HALF], g, 3 * s + m)
                B = s * ALL
                for t in range(CHUNK):
                    load_x(B + t + 2, t + 2, (B + t) % 2)
                    store(B + t, t, (B + t) % 2, s)
                if s:
                    store_c(NCHUNK - 1, NCHUNK - 1, 0)
                    store_dec()
                with sp.Fori(1, NCHUNK - 1) as c:
                    for q in range(CHUNK):
                        load_x(B + c * CHUNK + q + 2, c * CHUNK + q + 2, (B + q) % 2)
                        store(B + c * CHUNK + q, c * CHUNK + q, (B + q) % 2, s)
                    store_c(s * NCHUNK + c - 1, c - 1, s)
                for t in range(TILES - CHUNK, TILES):
                    if B + t + 2 < 2 * ALL:
                        load_x(B + t + 2, (t + 2) % ALL, (B + t) % 2)
                    if s and t == TILES - 1:
                        sp.wait_ge(vt_copied, 2 * ALL - 2)
                        leave_v((NCHUNK - 1) * CTOK, (TILES - 1) * P + HIST)
                    store(B + t, t, (B + t) % 2, s)
                store_state(B + TILES - 1, TILES - 1, (B + TILES - 1) % 2, s)
                if s == 0:
                    load_x(ALL + 1, 1, (ALL + 1) % 2)
                    split_weights_dma(sp, w_in[:, col(1, GATE):col(1, GATE) + HALF], g, 3 + GATE)
                    store_c(NCHUNK - 2, NCHUNK - 2, 0)
                    split_weights_dma(sp, w_in[:, col(1, VALUE):col(1, VALUE) + HALF], g, 3 + VALUE)
                else:
                    split_weights_dma(sp, io.w_out_a[:, 0:HALF], g, 6)
                    sp.wait_ge(vt_copied, 2 * ALL - 1)
                    leave_v((TILES - 1) * P + HIST, SEQ + HIST)
                    store_c(2 * NCHUNK - 2, NCHUNK - 2, 1)
                    split_weights_dma(sp, io.w_out_a[:, HALF:D], g, 7, k1=STAGES)
                store(B + TILES, TILES, (B + TILES) % 2, s)
                store_state(B + TILES, TILES, (B + TILES) % 2, s)
            sp.wait_ge(vt_copied, 2 * ALL)
            sp.dma_start(g.vdec_left.rearrange("(j p) n -> p j n", p=P), vdec[:, CT:].rearrange("p j b w -> p j (b w)")).then_inc(left_out, 16)
            split_weights_dma(sp, io.w_out_a[:, HALF:D], g, 7, k0=STAGES)
            sp.wait_ge(c_out, 16 * (2 * NCHUNK - 1) * CT)
            sp.wait_ge(d_out, 16 * CT)
            sp.wait_ge(left_out, 16 * 3)
            for p in range(2):
                sp.wait_ge(z_out[p], 16 * ALL)
                sp.wait_ge(v_out[p], 16 * (1 + DB))
            sp.wait_ge(copy_out, 16)

        @block.gpsimd
        def _(pool):
            pool.memset(g.half[:, :], -0.5).then_inc(ident_made, 1)
            pool.memset(g.rms_eps[:, :], RMS_EPS)
            pool.memset(g.ln_eps[:, :], LN_EPS).then_inc(eps_made, 1)
            pool.wait_ge(eps_made, 1)
            pool.memset(g.ident[:, :], 0.0).then_inc(ident_made, 1)
            pool.wait_ge(ident_made, 2)
            pool.affine_select(out=g.ident[:, :], in_=g.ident[:, :], compare_op=ALU.not_equal, fill=1.0, base=0,
                               pattern=[[-1, P]], channel_multiplier=1).then_inc(ident_made, 1)
            pool.memset(vbuf[:, :, 0:HIST], 0.0).then_inc(hist_zero, 1)

            def rms(T, t, p):
                n = rows_of(t)
                pool.wait_ge(ss_ready, T + 1)
                after(pool, xs_ready, T - 1)
                pool.tensor_tensor(ms[0:n, p:p + 1], ss[0:n, p:p + 1], g.rms_eps[0:n, 0:1], ALU.add).then_inc(ms_ready, 1)
                pool.wait_ge(ms_ready, T + 1)
                pool.tensor_tensor(rstd[0:n, p:p + 1], ms[0:n, p:p + 1], g.half[0:n, 0:1], ALU.pow).then_inc(rstd_ready, 1)

            def add_products(gc, u):
                m, j = gc * CT + u, turn[u]
                for i in range(1 if u < 2 else 0, PTAPS):
                    pool.wait_ge(prod_ready, m * PTAPS + i + 1)
                    if u < 2 and i == 1:
                        after(pool, c_out, gc * CT * 16)
                        pool.tensor_tensor(csum[:, j], prod[:, 0], prod[:, 1], ALU.add).then_inc(prod_added, 2)
                        continue
                    if i == 0:
                        pool.wait_ge(conv_step, taps_done(gc, 0, DTAPS - 1, j))
                    else:
                        pool.wait_ge(prod_added, m * PTAPS + i)
                    pool.tensor_tensor(csum[:, j], prod[:, i % RING], csum[:, j], ALU.add).then_inc(prod_added, 1)

            rms(0, 0, 0)
            for s in range(2):
                B = s * ALL
                for q in range(CHUNK):
                    rms(B + q + 1, q + 1, (B + q + 1) % 2)
                    if s:
                        add_products(NCHUNK - 1, q)

                def chunk(c):
                    for q in range(CHUNK):
                        tn = c * CHUNK + q + 1
                        rms(B + tn, tn, (B + q + 1) % 2)
                        add_products(s * NCHUNK + c - 1, q)

                chunk(1)
                with pool.Fori(2, NCHUNK - 1) as c:
                    chunk(c)
                chunk(NCHUNK - 1)
                if s == 0:
                    rms(ALL, 0, ALL % 2)

        def square_x(act, T, t, p):
            n = rows_of(t)
            act.wait_ge(x_in[p], 16 * (T // 2 + 1) if isinstance(T, int) else p_uses(T, p))
            after(act, xt_done, T)
            act.activation(xs[0:n], x[0:n, p], ACT.Square, scale=D ** -0.5, accum_out=ss[0:n, p:p + 1]).then_inc(ss_ready, 1)

        def scale_x(act, T, t, p):
            n = rows_of(t)
            act.wait_ge(rstd_ready, T + 1)
            act.activation(xs[0:n], x[0:n, p], ACT.Copy, scale=rstd[0:n, p:p + 1]).then_inc(xs_ready, 1)

        def p_uses(T, p):
            return T * 8 + (16 if p == 0 else 8)

        def cut_hi(act, T, t, p):
            n = rows_of(t)
            act.wait_ge(xt_done, T + 1)
            after(act, z_mm, T - 1)
            act.activation(xt[p][:, 0, :, 0:n], ps_t[:, :, 0:n], ACT.Copy).then_inc(hi_ready, 1)

        @block.scalar
        def _(act):
            act.wait_ge(cols_t, 1)
            act.activation(g.taps[:, :], ps_g[:, 0:TAPS * KT], ACT.Copy).then_inc(cols_ready, 1)
            act.activation(g.cols[:, :], ps_g[:, 256:256 + VECS * KT], ACT.Copy).then_inc(cols_ready, 1)
            for h in range(2):
                act.wait_ge(st_t, h + 1)
                dst = vdec[:, :, h * DB // 2:(h + 1) * DB // 2, 0:HIST]
                src = ps_t[:, :, 0:DB * HIST // 2].rearrange("p k (b w) -> p k b w", w=HIST)
                for j in range(KT):
                    last = act.activation(dst[:, j], src[:, j], ACT.Copy)
                last.then_inc(st_copied, 1)
            square_x(act, 0, 0, 0)
            scale_x(act, 0, 0, 0)
            cut_hi(act, 0, 0, 0)

            def products(work, i0, i1):
                if work is None:
                    return
                gc, c, cs, u = work
                m, j = gc * CT + u, turn[u]
                for i in range(i0, i1):
                    after(act, prod_added, m * PTAPS + i - RING + 1)
                    at = c * CTOK + DTAPS + i
                    win = vbuf[:, j, at:at + CTOK] if isinstance(c, int) else vbuf[:, j, bass.ds(at, CTOK)]
                    act.activation(prod[:, i % RING], win, ACT.Identity, scale=wcol(DTAPS + i, cs * CT + j),
                                   bias=bcol(cs * CT + j) if i == 0 and u < 2 else 0.0).then_inc(prod_ready, 1)

            def body(T, t, p, s, work=None):
                last = isinstance(T, int) and T == 2 * ALL - 1
                n = rows_of(t)
                if work is not None:
                    act.wait_ge(vt_copied, T)
                if not last:
                    tn = (t + 1) % ALL if isinstance(t, int) else t + 1
                    square_x(act, T + 1, tn, 1 - p)
                products(work, 0, 3)
                act.wait_ge(g_mm, T + 1)
                after(act, v_ready, T)
                act.activation(sig[0:n], ps_g[0:n], ACT.Sigmoid).then_inc(sig_ready, 1)
                if not last:
                    scale_x(act, T + 1, tn, 1 - p)
                if isinstance(t, int) and t == 0:
                    split_weights_hi(act, ZGATE, na, g, 3 * s + ZGATE, free=(z_mm, ALL) if s else None)
                products(work, 3, 6)
                turning = isinstance(T, int) and T == ALL - 1
                if turning:
                    split_weights_hi(act, GATE, na, g, 3 + GATE, free=(g_mm, ALL), k1=STAGES)
                if last:
                    split_weights_hi(act, 0, 1.0, g, 6, free=(g_mm, 2 * ALL))
                else:
                    cut_hi(act, T + 1, tn, 1 - p)
                products(work, 6, 10)
                if turning:
                    split_weights_hi(act, GATE, na, g, 3 + GATE, k0=STAGES)
                    split_weights_hi(act, VALUE, na, g, 3 + VALUE, free=(a_mm, ALL), k1=STAGES)
                act.wait_ge(z_mm, T + 1)
                if not (isinstance(T, int) and T < 2):
                    act.wait_ge(z_out[p], p_uses(T - 2, p) if not isinstance(T, int) else 16 * (T // 2))
                act.activation(zo[0:n, p], ps_z[0:n], ACT.Copy).then_inc(z_copied, 1)
                act.wait_ge(vt_done, T + 1)
                if n == DEC:
                    for j in range(CT):
                        ins = act.activation(vdec[:, s * CT + j, :, HIST:], ps_v[:, j, 0:DEC].rearrange("p (b w) -> p b w", w=DS), ACT.Copy)
                else:
                    if s:
                        done = NCHUNK - 1 if isinstance(t, int) and t < CHUNK else NCHUNK
                        act.wait_ge(conv_step, done * DTAPS * CT)
                    dst = vbuf[:, :, HIST + t * P:HIST + (t + 1) * P] if isinstance(t, int) else vbuf[:, :, bass.ds(t * P + HIST, P)]
                    ins = act.activation(dst, ps_v[:, :, :], ACT.Copy)
                ins.then_inc(vt_copied, 1)
                products(work, 10, PTAPS)

            for s in range(2):
                B = s * ALL
                if s:
                    split_weights_hi(act, VALUE, na, g, 3 + VALUE, k0=STAGES)
                else:
                    split_weights_hi(act, GATE, na, g, GATE)
                    split_weights_hi(act, VALUE, na, g, VALUE)
                for t in range(CHUNK):
                    body(B + t, t, (B + t) % 2, s, (NCHUNK - 1, NCHUNK - 1, 0, t) if s else None)

                def chunk(c):
                    for q in range(CHUNK):
                        body(B + c * CHUNK + q, c * CHUNK + q, (B + q) % 2, s, (s * NCHUNK + c - 1, c - 1, s, q))

                chunk(1)
                with act.Fori(2, NCHUNK) as c:
                    chunk(c)
                body(B + TILES, TILES, (B + TILES) % 2, s)
            split_weights_hi(act, 1, 1.0, g, 7, free=(a_mm, 2 * ALL))

        @block.vector
        def _(dve):
            dve.wait_ge(cols_ready, 2)

            def cut_lo(T, t, p):
                n = rows_of(t)
                dve.wait_ge(hi_ready, T + 1)
                dve.tensor_tensor(xt[p][:, 1, :, 0:n], ps_t[:, :, 0:n], f32(xt[p][:, 0, :, 0:n]), ALU.subtract).then_inc(lo_ready, 1)

            def gate(T, t, p):
                n = rows_of(t)
                dve.wait_ge(sig_ready, T + 1)
                dve.wait_ge(a_mm, T + 1)
                after(dve, vt_done, T - 1)
                if isinstance(T, int) and T % ALL < 2 and T >= ALL:
                    dve.wait_ge(v_out[0], 16 * DB)
                    dve.wait_ge(v_out[1], 16)
                dve.tensor_tensor(v[0:n, p], ps_a[0:n], sig[0:n], ALU.mult).then_inc(v_ready, 1)

            def conv(gc, c, s, pair, k0, k1):
                for k in range(k0, k1):
                    for i in range(2):
                        j = 2 * pair + i
                        win = vbuf[:, j, c * CTOK + k:c * CTOK + k + CTOK] if isinstance(c, int) else vbuf[:, j, bass.ds(c * CTOK + k, CTOK)]
                        if k == 0 and pair == 0:
                            after(dve, conv_step, taps_done(gc - 1, 1, DTAPS - 1, i))
                            dve.tensor_scalar(acc[:, i], win, wcol(k, s * CT + j), bcol(s * CT + j), ALU.mult, ALU.add).then_inc(conv_step, 1)
                            continue
                        if k == 0:
                            dve.wait_ge(conv_step, taps_done(gc, 0, DTAPS - 1, i))
                            dve.wait_ge(prod_added, (gc * CT + i + 1) * PTAPS)
                        else:
                            dve.wait_ge(conv_step, taps_done(gc, pair, k - 1, i))
                        if k == DTAPS - 1:
                            after(dve, c_out, gc * CT * 16)
                        dve.scalar_tensor_tensor(csum[:, j] if k == DTAPS - 1 else acc[:, i], win, wcol(k, s * CT + j),
                                                 csum[:, j] if k == 0 else acc[:, i], ALU.mult, ALU.add).then_inc(conv_step, 1)

            def dec_conv(k0, k1):
                for k in range(k0, k1):
                    for j in range(CT):
                        win = vdec[:, j, :, k:k + DS]
                        out = dacc[:, j].rearrange("p (b w) -> p b w", w=DS)
                        if k == 0:
                            dve.tensor_scalar(out, win, wcol(k, j), bcol(j), ALU.mult, ALU.add).then_inc(dec_step, 1)
                        else:
                            dve.wait_ge(dec_step, (k - 1) * CT + j + 1)
                            dve.scalar_tensor_tensor(out, win, wcol(k, j), out, ALU.mult, ALU.add).then_inc(dec_step, 1)

            cut_lo(0, 0, 0)
            for s in range(2):
                B = s * ALL

                def split_late(m):
                    for k in range(KT):
                        split_weights_lo(dve, m, na, g, 3 * s + m, k0=k, k1=k + 1)
                        if s:
                            if m == VALUE and k == 0:
                                dve.wait_ge(vt_copied, ALL)
                            dec_conv((m - VALUE) * KT + k, (m - VALUE) * KT + k + 1)

                if s == 0:
                    split_weights_lo(dve, GATE, na, g, GATE)
                split_late(VALUE)

                def step(T, t, p, q, gc, c, cs, dec=False):
                    pair = q // 2
                    k0, k2 = ((0, DTAPS // 2), (DTAPS // 2, DTAPS))[q % 2]
                    k1 = k0 + 2
                    gate(T, t, p)
                    if isinstance(t, int) and t == 0:
                        split_late(ZGATE)
                    if gc is not None:
                        conv(gc, c, cs, pair, k0, k1)
                    cut_lo(T + 1, (t + 1) % ALL if isinstance(t, int) else t + 1, 1 - p)
                    if gc is not None:
                        conv(gc, c, cs, pair, k1, k2)
                        if dec:
                            dec_conv(2 * KT + 4 * q, min(2 * KT + 4 * q + 4, TAPS))

                if s:
                    dve.wait_ge(vt_copied, ALL)
                else:
                    dve.wait_ge(hist_zero, 1)
                for q in range(CHUNK):
                    if s:
                        step(B + q, q, (B + q) % 2, q, NCHUNK - 1, NCHUNK - 1, 0, dec=True)
                    else:
                        step(B + q, q, (B + q) % 2, q, None, None, None)

                def chunk(c):
                    dve.wait_ge(vt_copied, B + c * CHUNK)
                    for q in range(CHUNK):
                        step(B + c * CHUNK + q, c * CHUNK + q, (B + q) % 2, q, s * NCHUNK + c - 1, c - 1, s)

                chunk(1)
                with dve.Fori(2, NCHUNK) as c:
                    chunk(c)
                gate(B + TILES, TILES, (B + TILES) % 2)
                if s == 0:
                    split_weights_lo(dve, GATE, na, g, 3 + GATE, k1=STAGES)
                    cut_lo(ALL, 0, ALL % 2)
                    split_weights_lo(dve, GATE, na, g, 3 + GATE, k0=STAGES)
            for m in range(2):
                split_weights_lo(dve, m, 1.0, g, 6 + m)

        @block.tensor
        def _(pe):
            pe.wait_ge(ident_made, 3)
            pe.wait_ge(raw_in, 16 * (2 + VECS + 2))
            pe.transpose(ps_g[:, 0:P], raw[:, 0], g.ident[:, :])
            pe.transpose(ps_g[:, P:TAPS * KT], raw[0:TAPS * KT - P, 1], g.ident[0:TAPS * KT - P, 0:TAPS * KT - P])
            pe.transpose(ps_g[:, 256:256 + VECS * KT], raw[0:VECS * KT, 2], g.ident[0:VECS * KT, 0:VECS * KT]).then_inc(cols_t, 1)
            pe.wait_ge(st_in, 32)
            n = DB * HIST // 2
            for h in range(2):
                after(pe, st_copied, h)
                for k in range(KT):
                    last = pe.transpose(ps_t[:, k, 0:n], x[0:n, h, k * P:(k + 1) * P], g.ident[0:n, 0:n])
                last.then_inc(st_t, 1)
            pe.wait_ge(st_copied, 2)

            def turn_x(T, t, p):
                n = rows_of(t)
                pe.wait_ge(xs_ready, T + 1)
                after(pe, lo_ready, T)
                for k in range(KT):
                    last = pe.transpose(ps_t[:, k, 0:n], xs[0:n, k * P:(k + 1) * P], g.ident[0:n, 0:n])
                last.then_inc(xt_done, 1)

            def body(T, t, p, s):
                n = rows_of(t)
                first = isinstance(t, int) and t == 0
                gate_of = lambda m: (g.w_lo, KT * (3 * s + m)) if first else None
                pe.wait_ge(lo_ready, T + 1)
                after(pe, sig_ready, T)
                if isinstance(T, int) and T == 0:
                    pe.wait_ge(cols_ready, 2)
                project(pe, ps_g[0:n], xt[p], g.wslot[GATE], n, gate_of(GATE)).then_inc(g_mm, 1)
                after(pe, v_ready, T)
                project(pe, ps_a[0:n], xt[p], g.wslot[VALUE], n, gate_of(VALUE)).then_inc(a_mm, 1)
                if not (isinstance(T, int) and T == 2 * ALL - 1):
                    turn_x(T + 1, (t + 1) % ALL if isinstance(t, int) else t + 1, 1 - p)
                after(pe, z_copied, T)
                project(pe, ps_z[0:n], xt[p], g.wslot[ZGATE], n, gate_of(ZGATE)).then_inc(z_mm, 1)
                pe.wait_ge(v_ready, T + 1)
                after(pe, vt_copied, T)
                for j in range(CT):
                    last = pe.transpose(ps_v[:, j, 0:n], v[0:n, p, j * P:(j + 1) * P], g.ident[0:n, 0:n])
                last.then_inc(vt_done, 1)

            turn_x(0, 0, 0)
            for s in range(2):
                B = s * ALL
                for t in range(2):
                    body(B + t, t, (B + t) % 2, s)
                with pe.Fori(1, TILES // 2 - 1) as i:
                    for q in range(2):
                        body(B + i * 2 + q, i * 2 + q, (B + q) % 2, s)
                for t in range(TILES - 2, ALL):
                    body(B + t, t, (B + t) % 2, s)


def phase_b(nc, io, g):
    with ExitStack() as ctx:
        sb = lambda name, shape, dt=F32: ctx.enter_context(nc.sbuf_tensor(name, shape, dt))
        pb = lambda name, shape: ctx.enter_context(nc.psum_tensor(name, shape, F32))
        sem = lambda name: ctx.enter_context(nc.semaphore(name))

        OUT0, OUT1, KVS, Q0, Q1 = range(5)
        g.wslot = g.shared_slots + [sb(f"b_w{m}", [P, 2, KT, HALF], F32R) for m in range(2, 5)]
        x = sb("b_x", [P, D])
        y = sb("b_y", [P, D])
        yc = y[:, :].rearrange("p (k n) -> p k n", k=KT)
        yt = sb("b_yt", [P, 2, KT, P], F32R)
        ht = sb("b_ht", [P, 2, KT, P], F32R)
        h = y
        qo = sb("b_qo", [P, D])
        g.stages = 3
        three = sb("b_three", [P, g.stages, HIST + CTOK])
        early_stage = three[:, :, 0:HALF]
        vw, cw, kvo = three[:, 0], three[:, 1, 0:CTOK], three[:, 2, 0:2 * KV]
        cz = sb("b_cz", [P, 2 * D])
        gate_stage = cz[:, 0:g.stages * HALF].rearrange("p (s n) -> p s n", s=g.stages)
        g.stage = early_stage
        c = cz[:, 0:D].rearrange("p (k n) -> p k n", k=KT)
        z = cz[:, D:2 * D]
        vd = sb("b_vd", [P, DB, HIST + DS])
        cd = sb("b_cd", [P, DEC])
        gains = {KVS: g.cols[:, KT:2 * KT], Q0: g.cols[:, 2 * KT:3 * KT], Q1: g.cols[:, 2 * KT:3 * KT]}
        kgain = sb("b_kgain", [P, HD])
        stats = sb("b_stats", [P, 2, 6])
        mv = sb("b_mv", [P, 2])
        pause = sb("b_pause", [P, 1])
        lms = sb("b_lms", [P, 1])
        lrs = sb("b_lrs", [P, 1])
        ss = sb("b_ss", [P, 1])
        ms = sb("b_ms", [P, 1])
        hss = sb("b_hss", [P, HEADS + KVH])
        hms = sb("b_hms", [P, HEADS + KVH])
        hrs = sb("b_hrs", [P, HEADS + KVH])

        ps_c = pb("b_psc", [P, D])
        ps_cc = ps_c[:, :].rearrange("p (k n) -> p k n", k=KT)
        ps_t = pb("b_pst", [P, KT, P])
        ps_o = pb("b_pso", [P, D])
        ps_q = pb("b_psq", [P, D])

        g.w_in = [sem(f"b_w_in{b}") for b in range(g.stages)]
        g.w_hi, g.w_lo = sem("b_w_hi"), sem("b_w_lo")
        (kg_in, c_in, z_in, x_in, x1_out, q_out, kv_out, copy_out, tc_done, tz_done, ty_done, th_done, out_mm, kv_mm,
         q_mm, stat_step, lms_ready, lrs_ready, yn_ready, sz_ready, y2_ready, prod_ready, yhi_ready, ylo_ready,
         x1_ready, ss_ready, ms_ready, rstd_ready, h_ready, hhi_ready, hlo_ready, ksq_ready, qsq_ready, v_ready,
         kss_ready, qss_ready, kms_ready, qms_ready, krs_ready, qrs_ready, kn_ready, k_ready, q_ready) = (
             sem("b_" + s) for s in (
                 "kg_in c_in z_in x_in x1_out q_out kv_out copy_out tc_done tz_done ty_done th_done out_mm kv_mm "
                 "q_mm stat_step lms_ready lrs_ready yn_ready sz_ready y2_ready prod_ready yhi_ready ylo_ready "
                 "x1_ready ss_ready ms_ready rstd_ready h_ready hhi_ready hlo_ready ksq_ready qsq_ready v_ready "
                 "kss_ready qss_ready kms_ready qms_ready krs_ready qrs_ready kn_ready k_ready q_ready").split())
        left_in, left_step, left_out = sem("b_left_in"), sem("b_left_step"), sem("b_left_out")
        heads = lambda ap, m: ap.rearrange("p (h d) -> p h d", h=m)
        block = ctx.enter_context(nc.Block())

        def steady(eng, body, between=None):
            body(0)
            body(1)
            body(2, 0, 0)
            body(3, 0, 1)
            with eng.Fori(2, CT + 1) as i:
                for q in range(2):
                    body(i * 2 + q, i - 1, q)
            if between is not None:
                between()
            with eng.Fori(CT + 1, TILES // 2 - 1) as i:
                for q in range(2):
                    body(i * 2 + q)
            for t in range(TILES - 2, ALL):
                body(t)

        @block.sync
        def _(sp):
            def load_c(t):
                after(sp, tc_done, t)
                n = rows_of(t)
                cols = slice(t * P, t * P + n) if isinstance(t, int) else bass.ds(t * P, P)
                sp.dma_start(c[:, :, 0:n], g.c_d.rearrange("(k p) n -> p k n", p=P)[:, :, cols]).then_inc(c_in, 16)

            def load_z(t):
                after(sp, tz_done, t)
                n = rows_of(t)
                sp.dma_start(z[0:n], token_rows(g.z_d, t, n)).then_inc(z_in, 16)

            def load_x(t):
                after(sp, x1_out, 16 * t)
                after(sp, h_ready, t)
                n = rows_of(t)
                sp.dma_start(x[0:n], io.x_sample if n == DEC else token_rows(io.x_prompt, t, n)).then_inc(x_in, 16)

            def store_x1(t):
                n = rows_of(t)
                sp.wait_ge(x1_ready, t + 1)
                sp.dma_start(token_rows(g.x1_d, t, n), x[0:n]).then_inc(x1_out, 16)

            def store_qkv(t):
                n = rows_of(t)
                sp.wait_ge(k_ready, t + 1)
                sp.wait_ge(v_ready, t + 1)
                sp.dma_start(token_rows(g.kv_d, t, n), kvo[0:n]).then_inc(kv_out, 16)
                if isinstance(t, int) and t == TILES - 1:
                    sp.dma_start(io.k_p, kvo[:, 0:KV]).then_inc(copy_out, 16)
                    sp.dma_start(io.v_p, kvo[:, KV:2 * KV]).then_inc(copy_out, 16)
                if n == DEC:
                    for b in range(DB):
                        rows = slice(b * DS, (b + 1) * DS)
                        sp.dma_start(io.k_s[b, P - DS:P, :], kvo[rows, 0:KV]).then_inc(copy_out, 16)
                        sp.dma_start(io.v_s[b, P - DS:P, :], kvo[rows, KV:2 * KV]).then_inc(copy_out, 16)
                sp.wait_ge(q_ready, t + 1)
                sp.dma_start(token_rows(g.q_d, t, n), qo[0:n]).then_inc(q_out, 16)

            def load_left(j):
                after(sp, left_step, 2 * TAPS * j)
                sp.dma_start(vw, g.v_left[bass.ds(j * P, P), :] if not isinstance(j, int) else g.v_left[j * P:(j + 1) * P, :]).then_inc(left_in, 16)
                sp.dma_start(vd[:, :, :].rearrange("p b w -> p (b w)"),
                             g.vdec_left[bass.ds(j * P, P), :] if not isinstance(j, int) else g.vdec_left[j * P:(j + 1) * P, :]).then_inc(left_in, 16)

            def store_left(j):
                sp.wait_ge(left_step, 2 * TAPS * (j + 1))
                rows = g.c_d[bass.ds(j * P + D // 2, P), :] if not isinstance(j, int) else g.c_d[D // 2 + j * P:D // 2 + (j + 1) * P, :]
                sp.dma_start(rows[:, SEQ - CTOK:SEQ], cw).then_inc(left_out, 16)
                sp.dma_start(rows[:, SEQ:TOK], cd[:, :]).then_inc(left_out, 16)

            load_c(0)
            load_z(0)
            load_c(1)
            load_x(0)
            load_z(1)
            split_weights_dma(sp, io.w_kv, g, 0)
            load_c(2)
            split_weights_dma(sp, io.w_in_b[:, 0:HALF], g, 1)

            def body(t, left=None, part=0):
                if left is not None and part == 0:
                    if isinstance(left, int):
                        sp.wait_ge(g.w_lo, 3 * KT)
                    else:
                        store_left(left - 1)
                    load_left(left)
                store_x1(t)
                if isinstance(t, int) and t == 0:
                    load_z(2)
                    load_x(1)
                    split_weights_dma(sp, io.w_in_b[:, HALF:D], g, 2, k1=g.stages)
                    load_c(3)
                    split_weights_dma(sp, io.w_in_b[:, HALF:D], g, 2, k0=g.stages)
                    sp.dma_start(kgain[:, :], io.k_norm.rearrange("(a d) -> a d", a=1).broadcast_to([P, HD])).then_inc(kg_in, 16)
                    sp.dma_start(io.k_s[:, 0:P - DS, :], io.cache_k[:, DS:P, :]).then_inc(copy_out, 16)
                    sp.dma_start(io.v_s[:, 0:P - DS, :], io.cache_v[:, DS:P, :]).then_inc(copy_out, 16)
                    return
                if not isinstance(t, int) or t + 1 < ALL:
                    load_x(t + 1)
                if not isinstance(t, int) or t + 2 < ALL:
                    if not (isinstance(t, int) and t == 1):
                        load_c(t + 2)
                    load_z(t + 2)
                if isinstance(t, int) and t == TILES:
                    sp.wait_ge(tc_done, ALL)
                    sp.wait_ge(tz_done, ALL)
                    g.stage = gate_stage
                    split_weights_dma(sp, io.w_in_b[:, D:D + HALF], g, 3)
                if not (isinstance(t, int) and t == 0):
                    store_qkv(t - 1)
            def all_convolved():
                store_left(CT - 1)
                sp.wait_ge(left_out, 32 * CT)
            steady(sp, body, all_convolved)
            split_weights_dma(sp, io.w_in_b[:, D + HALF:2 * D], g, 4)
            store_qkv(ALL - 1)
            sp.wait_ge(x1_out, 16 * ALL)
            sp.wait_ge(q_out, 16 * ALL)
            sp.wait_ge(kv_out, 16 * ALL)
            sp.wait_ge(copy_out, 16 * (2 + 2 + 2 * DB))

        @block.gpsimd
        def _(pool):
            def power(out, mid, src, n, eps, mid_ready, ready, t):
                after(pool, ready, t)
                pool.tensor_tensor(mid[0:n], src[0:n], eps[0:n, 0:out.shape[1]], ALU.add).then_inc(mid_ready, 1)
                pool.wait_ge(mid_ready, t + 1)
                pool.tensor_tensor(out[0:n], mid[0:n], g.half[0:n, 0:out.shape[1]], ALU.pow).then_inc(ready, 1)

            def layer(t):
                pool.wait_ge(stat_step, 3 * t + 3)
                after(pool, yn_ready, t)
                power(lrs[:, :], lms[:, :], mv[:, 1:2], rows_of(t), g.ln_eps, lms_ready, lrs_ready, t)

            def body(t, left=None, part=0):
                if not isinstance(t, int) or t + 1 < ALL:
                    layer(t + 1)
                pool.wait_ge(ss_ready, t + 1)
                after(pool, h_ready, t)
                power(g.rstd_b[:, t:t + 1] if isinstance(t, int) else g.rstd_b[:, bass.ds(t, 1)], ms[:, :], ss[:, :], rows_of(t), g.rms_eps,
                      ms_ready, rstd_ready, t)
                if isinstance(t, int) and t == 0:
                    return
                qk(t - 1)

            def qk(t):
                pool.wait_ge(kss_ready, t + 1)
                after(pool, k_ready, t)
                power(hrs[:, HEADS:], hms[:, HEADS:], hss[:, HEADS:], rows_of(t), g.rms_eps, kms_ready, krs_ready, t)
                pool.wait_ge(qss_ready, t + 1)
                after(pool, q_ready, t)
                power(hrs[:, 0:HEADS], hms[:, 0:HEADS], hss[:, 0:HEADS], rows_of(t), g.rms_eps, qms_ready, qrs_ready, t)

            layer(0)
            steady(pool, body)
            qk(ALL - 1)

        lng = g.cols[:, 4 * KT:5 * KT]
        lnb = g.cols[:, 5 * KT:6 * KT]

        @block.scalar
        def _(act):
            def silu_z(t):
                n = rows_of(t)
                act.wait_ge(z_in, 16 * (t + 1))
                act.activation(z[0:n], z[0:n], ACT.Silu).then_inc(sz_ready, 1)

            def silu_y(t):
                n = rows_of(t)
                act.wait_ge(ty_done, t + 1)
                for k in range(KT):
                    ins = act.activation(yc[:, k, 0:n], ps_t[:, k, 0:n], ACT.Silu, scale=lng[:, k:k + 1], bias=lnb[:, k:k + 1])
                ins.then_inc(y2_ready, 1)

            def cut_y(t):
                n = rows_of(t)
                act.wait_ge(prod_ready, t + 1)
                after(act, out_mm, t)
                act.activation(yt[:, 0, :, 0:n], yc[:, :, 0:n], ACT.Copy).then_inc(yhi_ready, 1)

            def square_x1(t):
                n = rows_of(t)
                act.wait_ge(x1_ready, t + 1)
                after(act, q_out, 16 * (t - 1))
                act.activation(qo[0:n], x[0:n], ACT.Square, scale=D ** -0.5, accum_out=ss[0:n]).then_inc(ss_ready, 1)

            def scale_h(t):
                n = rows_of(t)
                act.wait_ge(rstd_ready, t + 1)
                act.wait_ge(ylo_ready, t + 2 if not isinstance(t, int) else min(t + 2, ALL))
                rs = g.rstd_b[0:n, t:t + 1] if isinstance(t, int) else g.rstd_b[0:n, bass.ds(t, 1)]
                act.activation(h[0:n], x[0:n], ACT.Copy, scale=rs).then_inc(h_ready, 1)

            def cut_h(t):
                n = rows_of(t)
                act.wait_ge(th_done, t + 1)
                after(act, q_mm, t)
                act.activation(ht[:, 0, :, 0:n], ps_t[:, :, 0:n], ACT.Copy).then_inc(hhi_ready, 1)

            def keys_values(t):
                n = rows_of(t)
                act.wait_ge(kv_mm, t + 1)
                after(act, kv_out, 16 * t)
                if isinstance(t, int) and t == TILES:
                    act.wait_ge(copy_out, 16 * 4)
                act.activation(kvo[0:n, 0:KV], ps_o[0:n, 0:KV], ACT.Square, scale=HD ** -0.5).then_inc(ksq_ready, 1)
                act.activation(kvo[0:n, KV:], ps_o[0:n, KV:2 * KV], ACT.Copy).then_inc(v_ready, 1)
                if isinstance(t, int) and t == TILES - 1:
                    g.stage = gate_stage
                    split_weights_hi(act, 0, gains[Q0], g, 3, free=(out_mm, ALL), k1=5)

            def queries(t):
                n = rows_of(t)
                act.wait_ge(q_mm, t + 1)
                after(act, q_out, 16 * t)
                act.activation(qo[0:n], ps_q[0:n], ACT.Square, scale=HD ** -0.5).then_inc(qsq_ready, 1)

            def body(t, left=None, part=0):
                if not (isinstance(t, int) and t == 0):
                    cut_h(t - 1)
                more = not isinstance(t, int) or t + 1 < ALL
                if more:
                    silu_z(t + 1)
                start = isinstance(t, int) and t == 0
                if not start:
                    square_x1(t)
                if more:
                    silu_y(t + 1)
                if start:
                    square_x1(t)
                if more:
                    cut_y(t + 1)
                else:
                    scale_h(t)
                if isinstance(t, int) and t == 1:
                    split_weights_hi(act, Q1, gains[Q1], g, 2)
                    act.wait_ge(g.w_lo, 3 * KT)
                if not (isinstance(t, int) and t == 0):
                    keys_values(t - 1)
                if more:
                    scale_h(t)
                if start:
                    split_weights_hi(act, Q0, gains[Q0], g, 1)
                if not (isinstance(t, int) and t == 0):
                    queries(t - 1)

            silu_z(0)
            g.stage = early_stage
            silu_y(0)
            cut_y(0)
            split_weights_hi(act, KVS, gains[KVS], g, 0)
            steady(act, body)
            cut_h(ALL - 1)
            split_weights_hi(act, 0, gains[Q0], g, 3, k0=5)
            split_weights_hi(act, 1, gains[Q0], g, 4, k1=g.stages)
            keys_values(ALL - 1)
            split_weights_hi(act, 1, gains[Q0], g, 4, k0=g.stages)
            queries(ALL - 1)

        @block.vector
        def _(dve):
            def normalize(t, fill=None):
                n = rows_of(t)
                dve.wait_ge(tc_done, t + 1)
                after(dve, lms_ready, t)
                for b in range(2):
                    dve.bn_stats(stats[0:n, b], ps_c[0:n, b * HALF:(b + 1) * HALF]).then_inc(stat_step, 1)
                dve.wait_ge(stat_step, 3 * t + 2)
                dve.memset(pause[:, :], 0.0)
                dve.bn_aggr(mv[0:n], stats[0:n].rearrange("p a b -> p (a b)")).then_inc(stat_step, 1)
                dve.wait_ge(stat_step, 3 * t + 3)
                if fill is not None:
                    fill(1)
                dve.wait_ge(lrs_ready, t + 1)
                after(dve, ylo_ready, t)
                after(dve, th_done, t - 1)
                dve.tensor_scalar(y[0:n], ps_c[0:n], mv[0:n, 0:1], lrs[0:n, 0:1], ALU.subtract, ALU.mult).then_inc(yn_ready, 1)

            def gate(t, fill=None):
                n = rows_of(t)
                dve.wait_ge(y2_ready, t + 1)
                dve.wait_ge(tz_done, t + 1)
                dve.tensor_tensor(yc[:, :, 0:n], yc[:, :, 0:n], ps_cc[:, :, 0:n], ALU.mult).then_inc(prod_ready, 1)
                if fill is not None:
                    fill(1)
                dve.wait_ge(yhi_ready, t + 1)
                dve.tensor_tensor(yt[:, 1, :, 0:n], yc[:, :, 0:n], f32(yt[:, 0, :, 0:n]), ALU.subtract).then_inc(ylo_ready, 1)

            def residual(t):
                n = rows_of(t)
                dve.wait_ge(out_mm, t + 1)
                dve.wait_ge(x_in, 16 * (t + 1))
                dve.tensor_tensor(x[0:n], ps_o[0:n], x[0:n], ALU.add).then_inc(x1_ready, 1)

            def cut_h(t):
                n = rows_of(t)
                dve.wait_ge(hhi_ready, t + 1)
                dve.tensor_tensor(ht[:, 1, :, 0:n], ps_t[:, :, 0:n], f32(ht[:, 0, :, 0:n]), ALU.subtract).then_inc(hlo_ready, 1)

            def keys(t, fill=None):
                n = rows_of(t)
                dve.wait_ge(ksq_ready, t + 1)
                after(dve, kms_ready, t)
                dve.tensor_reduce(hss[0:n, HEADS:], heads(kvo[0:n, 0:KV], KVH), AX_X, ALU.add).then_inc(kss_ready, 1)
                if fill is not None:
                    fill(1)
                dve.wait_ge(krs_ready, t + 1)
                dve.wait_ge(v_ready, t + 1)
                rs = hrs[0:n, HEADS:].rearrange("p (h a) -> p h a", a=1).broadcast_to([n, KVH, HD])
                dve.tensor_tensor(heads(kvo[0:n, 0:KV], KVH), heads(ps_o[0:n, 0:KV], KVH), rs, ALU.mult).then_inc(kn_ready, 1)
                dve.wait_ge(kn_ready, t + 1)
                if isinstance(t, int) and t == 0:
                    dve.wait_ge(kg_in, 16)
                kg = kgain[0:n, :].rearrange("p (a d) -> p a d", a=1).broadcast_to([n, KVH, HD])
                dve.tensor_tensor(heads(kvo[0:n, 0:KV], KVH), heads(kvo[0:n, 0:KV], KVH), kg, ALU.mult).then_inc(k_ready, 1)

            def query_sums(t):
                n = rows_of(t)
                dve.wait_ge(qsq_ready, t + 1)
                after(dve, qms_ready, t)
                dve.tensor_reduce(hss[0:n, 0:HEADS], heads(qo[0:n], HEADS), AX_X, ALU.add).then_inc(qss_ready, 1)

            def queries(t):
                n = rows_of(t)
                dve.wait_ge(qrs_ready, t + 1)
                rs = hrs[0:n, 0:HEADS].rearrange("p (h a) -> p h a", a=1).broadcast_to([n, HEADS, HD])
                dve.tensor_tensor(heads(qo[0:n], HEADS), heads(ps_q[0:n], HEADS), rs, ALU.mult).then_inc(q_ready, 1)

            def convolve(j, k0, k1):
                if j is None:
                    return
                scalar = lambda ap, base: ap[:, base + j:base + j + 1] if isinstance(j, int) else ap[:, bass.ds(j + base, 1)]
                for k in range(k0, k1):
                    for e, (win, out) in enumerate(((vw[:, k:k + CTOK], cw),
                                                    (vd[:, :, k:k + DS], cd[:, :].rearrange("p (b w) -> p b w", w=DS)))):
                        w = scalar(g.taps, k * KT + CT)
                        if k == 0:
                            if e == 0:
                                dve.wait_ge(left_in, 32 * (j + 1))
                                after(dve, left_out, 32 * j)
                            dve.tensor_scalar(out, win, w, scalar(g.cols, 3 * KT + CT), ALU.mult, ALU.add).then_inc(left_step, 1)
                        else:
                            dve.wait_ge(left_step, 2 * TAPS * j + 2 * (k - 1) + e + 1)
                            dve.scalar_tensor_tensor(out, win, w, out, ALU.mult, ALU.add).then_inc(left_step, 1)

            def body(t, left=None, part=0):
                at = [(0, 14)[part]]

                def fill(n):
                    end = min(at[0] + n, (14, TAPS)[part])
                    convolve(left, at[0], end)
                    at[0] = end

                if not (isinstance(t, int) and t == 0):
                    cut_h(t - 1)
                if part:
                    fill(2)
                if not (isinstance(t, int) and t < 2):
                    queries(t - 2)
                more = not isinstance(t, int) or t + 1 < ALL
                if more:
                    normalize(t + 1, fill if part else None)
                start = isinstance(t, int) and t == 0
                if start:
                    split_weights_lo(dve, KVS, gains[KVS], g, 0, k0=KT // 2)
                residual(t)
                fill(3)
                if more:
                    gate(t + 1, fill)
                if start:
                    split_weights_lo(dve, Q0, gains[Q0], g, 1)
                else:
                    if isinstance(t, int) and t == 1:
                        split_weights_lo(dve, Q1, gains[Q1], g, 2)
                    keys(t - 1, fill)
                    fill(TAPS)
                    if isinstance(t, int) and t == TILES:
                        g.stage = gate_stage
                        split_weights_lo(dve, 0, gains[Q0], g, 3, k1=5)
                    query_sums(t - 1)

            normalize(0)
            g.stage = early_stage
            gate(0)
            split_weights_lo(dve, KVS, gains[KVS], g, 0, k1=KT // 2)
            steady(dve, body)
            cut_h(ALL - 1)
            queries(ALL - 2)
            split_weights_lo(dve, 0, gains[Q0], g, 3, k0=5)
            split_weights_lo(dve, 1, gains[Q0], g, 4, k1=g.stages)
            keys(ALL - 1)
            split_weights_lo(dve, 1, gains[Q0], g, 4, k0=g.stages)
            query_sums(ALL - 1)
            queries(ALL - 1)

        @block.tensor
        def _(pe):
            def turn_c(t):
                n = rows_of(t)
                pe.wait_ge(c_in, 16 * (t + 1))
                after(pe, prod_ready, t)
                for k in range(KT):
                    ins = pe.transpose(ps_c[0:n, k * P:(k + 1) * P], c[:, k, 0:n], g.ident[:, :])
                ins.then_inc(tc_done, 1)

            def turn(out, src, t, done):
                n = rows_of(t)
                for k in range(KT):
                    ins = pe.transpose(out[:, k, 0:n], src[0:n, k * P:(k + 1) * P], g.ident[0:n, 0:n])
                ins.then_inc(done, 1)

            def turn_y(t):
                pe.wait_ge(yn_ready, t + 1)
                after(pe, hlo_ready, t - 1)
                turn(ps_t, y, t, ty_done)

            def turn_z(t):
                pe.wait_ge(sz_ready, t + 1)
                turn(ps_cc, z, t, tz_done)

            def turn_h(t):
                pe.wait_ge(h_ready, t + 1)
                after(pe, y2_ready, t + 2 if not isinstance(t, int) else min(t + 2, ALL))
                turn(ps_t, h, t, th_done)

            def out(t):
                n = rows_of(t)
                pe.wait_ge(ylo_ready, t + 1)
                after(pe, k_ready, t - 1)
                after(pe, v_ready, t - 1)
                for b in range(2):
                    ins = project(pe, ps_o[0:n, b * HALF:(b + 1) * HALF], yt, g.wslot[OUT0 + b], n)
                ins.then_inc(out_mm, 1)

            def qkv(t, gate=False):
                n = rows_of(t)
                pe.wait_ge(hlo_ready, t + 1)
                after(pe, x1_ready, t + 2 if not isinstance(t, int) else min(t + 2, ALL))
                project(pe, ps_o[0:n, 0:HALF], ht, g.wslot[KVS], n, (g.w_lo, 0) if gate else None).then_inc(kv_mm, 1)
                after(pe, q_ready, t)
                for b in range(2):
                    ins = project(pe, ps_q[0:n, b * HALF:(b + 1) * HALF], ht, g.wslot[Q0 + b], n,
                                  (g.w_lo, KT * (1 + b)) if gate else None)
                ins.then_inc(q_mm, 1)

            def body(t, left=None, part=0):
                more = not isinstance(t, int) or t + 1 < ALL
                if more:
                    turn_c(t + 1)
                out(t)
                if more:
                    turn_y(t + 1)
                    turn_z(t + 1)
                if not (isinstance(t, int) and t == 0):
                    qkv(t - 1, gate=isinstance(t, int) and t == 1)
                turn_h(t)

            turn_c(0)
            turn_y(0)
            turn_z(0)
            steady(pe, body)
            qkv(ALL - 1)


def phase_c(nc, io, g):
    with ExitStack() as ctx:
        sb = lambda name, shape, dt=F32: ctx.enter_context(nc.sbuf_tensor(name, shape, dt))
        pb = lambda name, shape: ctx.enter_context(nc.psum_tensor(name, shape, F32))
        sem = lambda name: ctx.enter_context(nc.semaphore(name))

        Z0, Z1, OUT0, OUT1 = range(4)
        g.wslot = g.shared_slots + [sb(f"c_w{m}", [P, 2, KT, HALF], F32R) for m in range(2, 4)]
        hx = sb("c_hx", [P, D])
        xr = sb("c_xr", [P, D])
        ht = sb("c_ht", [P, 2, KT, P], F32R)
        ot = sb("c_ot", [P, 2, KT, P], F32R)
        q = sb("c_q", [P, D])
        qt = sb("c_qt", [P, KT, P])
        kd = sb("c_kd", [P, 2, KVH, 2, HD])
        kt = sb("c_kt", [P, 2, KVH, P])
        v = sb("c_v", [P, 2, KV])
        bias = sb("c_bias", [P, HEADS, 2 * P])
        s = sb("c_s", [P, 2, GROUP, 2 * P])
        g.stages = 2
        g.stage = xr[:, :].rearrange("p (s n) -> p s n", s=2)
        pt = sb("c_pt", [P, 2, GROUP, P])
        sz = sb("c_sz", [P, D])
        sink0 = sb("c_sink0", [P, HEADS])
        sink = sb("c_sink", [P, HEADS])
        nsink = sb("c_nsink", [P, HEADS])
        sinkd = sb("c_sinkd", [P, 2])
        nm = sb("c_nm", [P, 2, GROUP])
        es = sb("c_es", [P, 2, GROUP])
        den = sb("c_den", [P, 2, GROUP])
        rden = sb("c_rden", [P, 2, GROUP])
        dist = pt[:, 0, 0:2].rearrange("p a b -> p (a b)")
        ddist = sb("c_ddist", [P, P + DS + 1])
        vn = sb("c_vn", [DS, 2, KV])

        acc = pb("c_acc", [P, HALF])
        ps_t = pb("c_pst", [P, KT, P])
        ps_s = pb("c_pss", [P, GROUP, 2 * P])
        ps_p = pb("c_psp", [P, 2, GROUP, P])
        ps_o = pb("c_pso", [P, HALF])

        g.w_in = [sem(f"c_w_in{b}") for b in range(g.stages)]
        g.w_hi, g.w_lo = sem("c_w_hi"), sem("c_w_lo")
        k_in = [sem("c_k_in0"), sem("c_k_in1")]
        kn_in = [sem("c_kn_in0"), sem("c_kn_in1")]
        v_in = [sem("c_v_in0"), sem("c_v_in1")]
        (tab_in, sinkd_in, hx_in, xr_in, q_in, y_out, bias_made, nsink_made, h_ready, th_done, hhi_ready, hlo_ready,
         tq_done, qt_ready, tk_done, kt_ready, z_mm, ztanh_ready, zg_done, qk_done, s_read, m_ready, nm_ready,
         es_in, es_ready, p_ready, den_ready, rden_ready, pn_ready, tp_done, pt_ready, sn_ready, pv_done, snt_ready, o_done,
         ohi_ready, olo_ready, out_mm, res_done, szt_done, szt_ready, od_ready) = (sem("c_" + x) for x in (
             "tab_in sinkd_in hx_in xr_in q_in y_out bias_made nsink_made h_ready th_done hhi_ready hlo_ready "
             "tq_done qt_ready tk_done kt_ready z_mm ztanh_ready zg_done qk_done s_read m_ready nm_ready "
             "es_in es_ready p_ready den_ready rden_ready pn_ready tp_done pt_ready sn_ready pv_done snt_ready o_done "
             "ohi_ready olo_ready out_mm res_done szt_done szt_ready od_ready").split())
        WAVES = DB // GROUP
        GD = TILES * KVH
        DK = P + DS
        slope = [2.0 ** (-8.0 * (h + 1) / HEADS) for h in range(HEADS)]
        SCALE = HD ** -0.5
        place = lambda j: 2 * (j % 2) + j // 2
        szc = sz[:, :].rearrange("p (k n) -> p k n", k=KT)
        qc = q[:, :].rearrange("p (k n) -> p k n", k=KT)
        qd = qt[0:HD, :, :].rearrange("p a b -> p (a b)")
        knt = bias[:, 0:4, 0:DEC]
        block = ctx.enter_context(nc.Block())

        def loop(eng, body):
            body(0, 0)
            body(1, 1)
            with eng.Fori(1, TILES // 2 - 1) as i:
                for r in range(2):
                    body(i * 2 + r, r)
            body(TILES - 2, 0)
            body(TILES - 1, 1)

        halves = lambda t: (1,) if isinstance(t, int) and t == 0 else (0, 1)
        keys_of = lambda t: slice(P, 2 * P) if isinstance(t, int) and t == 0 else slice(0, 2 * P)

        @block.sync
        def _(sp):
            def load_h(t):
                after(sp, th_done, t)
                n = rows_of(t)
                sp.dma_start(hx[0:n], token_rows(g.x1_d, t, n)).then_inc(hx_in, 16)

            def load_q(t):
                after(sp, tq_done, t)
                n = rows_of(t)
                sp.dma_start(q[0:n], token_rows(g.q_d, t, n)).then_inc(q_in, 16)

            def load_k(t, p, src=None):
                after(sp, tk_done, t - 1)
                n = P if src is not None else rows_of(t)
                src = token_rows(g.kv_d, t, n)[:, 0:KV] if src is None else src
                for e in range(2):
                    sp.dma_start(kd[0:n, p, :, e], src.rearrange("n (h d) -> n h d", h=KVH)).then_inc(k_in[p], 16)

            def load_v(t, r):
                if not (isinstance(t, int) and t < 2):
                    sp.wait_ge(pv_done, t * KVH)
                sp.dma_start(v[:, r], token_rows(g.kv_d, t, P)[:, KV:2 * KV]).then_inc(v_in[r], 16)

            def load_res(t):
                after(sp, y_out, 16 * t)
                n = rows_of(t)
                sp.dma_start(xr[0:n], token_rows(g.x1_d, t, n)).then_inc(xr_in, 16)

            def store_y(t):
                n = rows_of(t)
                sp.wait_ge(res_done, 2 * t + 2)
                sp.dma_start(io.y_s if n == DEC else token_rows(io.y_p, t, n), xr[0:n]).then_inc(y_out, 16)

            load_h(0)
            load_q(0)
            load_k(0, 0)
            sp.dma_start(dist[:, :], io.distance).then_inc(tab_in, 16)
            load_v(0, 0)
            sp.dma_start(ddist[:, :], io.decode_distance).then_inc(tab_in, 16)
            sp.dma_start(sink0[:, :], io.sinks.broadcast_to([P, HEADS])).then_inc(tab_in, 16)
            for h in range(HEADS):
                sp.dma_start(sinkd[h * DS:(h + 1) * DS, 0:1], io.sinks[:, h:h + 1].broadcast_to([DS, 1])).then_inc(sinkd_in, 16)
            split_weights_dma(sp, io.w_out_b[:, 0:HALF], g, 0, k1=g.stages)

            def body(t, r):
                first = isinstance(t, int) and t == 0
                load_h(t + 1)
                if not first:
                    load_res(t - 1)
                load_q(t + 1)
                load_k(t + 1, 1 - r)
                if not first:
                    store_y(t - 1)
                if not (isinstance(t, int) and t == TILES - 1):
                    load_v(t + 1, 1 - r)
                if first:
                    split_weights_dma(sp, io.w_out_b[:, 0:HALF], g, 0, k0=g.stages)
                    split_weights_dma(sp, io.w_out_b[:, HALF:D], g, 1)
                    sp.wait_ge(g.w_lo, 2 * KT)
            loop(sp, body)
            load_res(TILES - 1)

            def load_cache(b):
                after(sp, pv_done, max(GD, GD + b - 1))
                sp.dma_start(v[:, b % 2], io.cache_v[b]).then_inc(v_in[b % 2], 16)
                sp.dma_start(vn[:, b % 2], g.kv_d[SEQ + b * DS:SEQ + (b + 1) * DS, KV:2 * KV]).then_inc(kn_in[b % 2], 16)
            load_cache(0)
            load_cache(1)
            for b in range(DB):
                load_k(ALL + b, (ALL + b) % 2, io.cache_k[b])
            store_y(TILES - 1)
            load_res(TILES)
            for b in range(2, DB):
                load_cache(b)
            store_y(TILES)
            sp.wait_ge(y_out, 16 * ALL)

        @block.scalar
        def _(act):
            def scale_h(t):
                n = rows_of(t)
                act.wait_ge(hx_in, 16 * (t + 1))
                rs = g.rstd_b[0:n, t:t + 1] if isinstance(t, int) else g.rstd_b[0:n, bass.ds(t, 1)]
                act.activation(hx[0:n], hx[0:n], ACT.Copy, scale=rs).then_inc(h_ready, 1)

            def cut_h(t):
                n = rows_of(t)
                act.wait_ge(th_done, t + 1)
                after(act, z_mm, 2 * t)
                act.activation(ht[:, 0, :, 0:n], ps_t[:, :, 0:n], ACT.Copy).then_inc(hhi_ready, 1)

            def cut_o(t):
                n = rows_of(t)
                if n == DEC:
                    act.wait_ge(od_ready, 1)
                else:
                    act.wait_ge(o_done, KVH * (t + 1))
                after(act, out_mm, 2 * t)
                act.activation(ot[:, 0, :, 0:n], szc[:, :, 0:n], ACT.Copy).then_inc(ohi_ready, 1)

            def queries(t):
                act.wait_ge(tq_done, t + 1)
                if isinstance(t, int) and t == TILES:
                    after(act, qk_done, GD)
                    act.activation(qd.rearrange("p (b h i) -> p b h i", b=DB, h=HEADS),
                                   ps_t[0:HD, :, :].rearrange("p a c -> p (a c)").rearrange("p (h b i) -> p b h i", h=HEADS, b=DB), ACT.Copy, scale=g.qgain[0:HD]).then_inc(qt_ready, 1)
                else:
                    after(act, qk_done, KVH * t)
                    act.activation(qt[:, :, :], ps_t[:, :, :], ACT.Copy, scale=g.qgain[:, :]).then_inc(qt_ready, 1)

            def keys(t, r):
                act.wait_ge(tk_done, t + 1)
                if isinstance(t, int) and t == TILES:
                    act.activation(knt[:, :, :], acc[:, :].rearrange("p (h k) -> p h k", h=KVH)[:, :, 0:DEC], ACT.Copy).then_inc(kt_ready, 1)
                    return
                act.activation(kt[:, r], acc[:, :].rearrange("p (h k) -> p h k", h=KVH), ACT.Copy).then_inc(kt_ready, 1)

            def gate_tanh(t, b):
                n = rows_of(t)
                act.wait_ge(z_mm, 2 * t + b + 1)
                after(act, olo_ready, t)
                part = sz[0:n, b * HALF:(b + 1) * HALF]
                act.activation(part, acc[0:n], ACT.Tanh, scale=0.5).then_inc(ztanh_ready, 1)

            def exps(G, b, ks):
                act.wait_ge(nm_ready, G + 1)
                after(act, rden_ready, G - 1)
                act.wait_ge(es_in, G + 1)
                act.activation(es[:, b], es[:, b], ACT.Exp).then_inc(es_ready, 1)
                for j in range(GROUP):
                    ins = act.activation(s[:, b, j, ks], s[:, b, j, ks], ACT.Exp, bias=nm[:, b, j:j + 1], accum_out=den[:, b, j:j + 1])
                ins.then_inc(p_ready, 1)

            def turn_out(G, ks):
                act.wait_ge(tp_done, G + 1)
                after(act, pv_done, G)
                act.activation(pt[:, ks], ps_p[:, ks], ACT.Copy).then_inc(pt_ready, 1)

            def copy_gate(G, kv):
                act.wait_ge(pv_done, G + 1)
                act.activation(szc[:, 2 * kv:2 * kv + 2, :], ps_o[:, 2 * P:4 * P].rearrange("p (k n) -> p k n", k=2), ACT.Copy).then_inc(snt_ready, 1)

            scale_h(0)
            cut_h(0)
            queries(0)
            keys(0, 0)

            def body(t, r):
                hs = slice(1, 2) if isinstance(t, int) and t == 0 else slice(0, 2)
                ks = keys_of(t)
                first = isinstance(t, int) and t == 0
                split = lambda k: split_weights_hi(act, OUT0 + k // KT, 0.5, g, k // KT, k0=k % KT, k1=k % KT + 2) if first else None
                if not first:
                    cut_o(t - 1)
                scale_h(t + 1)
                split(0)
                exps(t * KVH, 0, ks)
                gate_tanh(t, 0)
                split(2)
                turn_out(t * KVH, hs)
                split(4)
                exps(t * KVH + 1, 1, ks)
                gate_tanh(t, 1)
                copy_gate(t * KVH, 0)
                split(6)
                turn_out(t * KVH + 1, hs)
                split(8)
                exps(t * KVH + 2, 0, ks)
                cut_h(t + 1)
                copy_gate(t * KVH + 1, 1)
                split(10)
                turn_out(t * KVH + 2, hs)
                exps(t * KVH + 3, 1, ks)
                copy_gate(t * KVH + 2, 2)
                split(12)
                split(14)
                turn_out(t * KVH + 3, hs)
                queries(t + 1)
                keys(t + 1, 1 - r)
                copy_gate(t * KVH + 3, 3)
            loop(act, body)

            cut_o(TILES - 1)
            gate_tanh(TILES, 0)
            for b in range(DB):
                if b == GROUP:
                    gate_tanh(TILES, 1)
                keys(ALL + b, b % 2)
            for w in range(WAVES):
                exps(GD + w, w % 2, slice(0, DK))
            for b in range(DB):
                act.wait_ge(tp_done, GD + b + 1)
                act.wait_ge(pv_done, GD + max(b - 1, 0))
                act.activation(pt[:, b % 2, 0], ps_p[:, b % 2, 0], ACT.Copy)
                act.activation(pt[0:DS, b % 2, 1], ps_p[0:DS, b % 2, 1], ACT.Copy).then_inc(pt_ready, 1)
            act.wait_ge(szt_done, 1)
            act.activation(qc[:, :, 0:DEC], ps_t[:, :, 0:DEC], ACT.Copy).then_inc(szt_ready, 1)
            cut_o(TILES)

        @block.vector
        def _(dve):
            def cut_h(t):
                n = rows_of(t)
                dve.wait_ge(hhi_ready, t + 1)
                dve.tensor_tensor(ht[:, 1, :, 0:n], ps_t[:, :, 0:n], f32(ht[:, 0, :, 0:n]), ALU.subtract).then_inc(hlo_ready, 1)

            def cut_o(t):
                n = rows_of(t)
                dve.wait_ge(ohi_ready, t + 1)
                dve.tensor_tensor(ot[:, 1, :, 0:n], szc[:, :, 0:n], f32(ot[:, 0, :, 0:n]), ALU.subtract).then_inc(olo_ready, 1)

            def gate(t, b):
                n = rows_of(t)
                k = 2 * t + b
                part = sz[0:n, b * HALF:(b + 1) * HALF]
                dve.wait_ge(ztanh_ready, k + 1)
                dve.scalar_tensor_tensor(part, part, 1.0, acc[0:n], ALU.add, ALU.mult).then_inc(zg_done, 1)

            def scores(G, t, kv, b):
                ks = keys_of(t)
                dve.wait_ge(qk_done, G + 1)
                after(dve, tp_done, G - 1)
                dve.scalar_tensor_tensor(s[:, b, :, ks], ps_s[:, :, ks], SCALE, bias[:, kv * GROUP:(kv + 1) * GROUP, ks],
                                         ALU.mult, ALU.add).then_inc(s_read, 1)
                dve.wait_ge(s_read, G + 1)
                dve.tensor_reduce(nm[:, b], s[:, b, :, ks], AX_X, ALU.max, negate=True).then_inc(m_ready, 1)
                sinks(G, b, nsink[:, kv * GROUP:(kv + 1) * GROUP], sink[:, kv * GROUP:(kv + 1) * GROUP])

            def sinks(G, b, minus, plus):
                dve.wait_ge(m_ready, G + 1)
                dve.tensor_tensor(nm[:, b], nm[:, b], minus, ALU.min).then_inc(nm_ready, 1)
                dve.wait_ge(nm_ready, G + 1)
                dve.tensor_tensor(es[:, b], plus, nm[:, b], ALU.add).then_inc(es_in, 1)

            def sums(G, b):
                dve.wait_ge(p_ready, G + 1)
                dve.wait_ge(es_ready, G + 1)
                dve.tensor_tensor(den[:, b], den[:, b], es[:, b], ALU.add).then_inc(den_ready, 1)
                dve.wait_ge(den_ready, G + 1)
                dve.reciprocal(rden[:, b], den[:, b]).then_inc(rden_ready, 1)

            def norm(G, t, kv, b):
                dve.wait_ge(rden_ready, G + 1)
                dve.wait_ge(zg_done, 2 * t + kv // 2 + 1)
                part = sz[:, kv * GROUP * HD:(kv + 1) * GROUP * HD].rearrange("p (a e d) -> p a e d", a=2, e=2)
                over = rden[:, b].rearrange("p (e a x) -> p a e x", e=2, x=1).broadcast_to([P, 2, 2, HD])
                dve.tensor_tensor(part, part, over, ALU.mult).then_inc(sn_ready, 1)

            def gated(G, kv):
                dve.wait_ge(snt_ready, G + 1)
                part = szc[:, 2 * kv:2 * kv + 2, :]
                dve.tensor_tensor(part, ps_o[:, 0:2 * P].rearrange("p (k n) -> p k n", k=2), part, ALU.mult).then_inc(o_done, 1)

            def residual(t, b):
                n = rows_of(t)
                part = xr[0:n, b * HALF:(b + 1) * HALF]
                dve.wait_ge(out_mm, 2 * t + b + 1)
                dve.wait_ge(xr_in, 16 * (t + 1))
                dve.tensor_tensor(part, acc[0:n], part, ALU.add).then_inc(res_done, 1)

            cut_h(0)
            dve.wait_ge(tab_in, 16 * 3)
            for h in range(HEADS):
                ins = dve.tensor_scalar(bias[:, h - h % GROUP + place(h % GROUP)], dist[:, :], -slope[h], None, ALU.mult)
            ins.then_inc(bias_made, 1)
            ordered = lambda ap: ap.rearrange("p (g b a) -> p g b a", b=2, a=2)
            given = sink0[:, :].rearrange("p (g a b) -> p g b a", b=2, a=2)
            dve.tensor_scalar(ordered(sink[:, :]), given, 1.0, None, ALU.mult).then_inc(nsink_made, 1)
            dve.tensor_scalar(ordered(nsink[:, :]), given, -1.0, None, ALU.mult).then_inc(nsink_made, 1)
            dve.wait_ge(bias_made, 1)
            dve.wait_ge(nsink_made, 2)

            def body(t, r):
                first = isinstance(t, int) and t == 0
                split = lambda k: split_weights_lo(dve, OUT0 + k // KT, 0.5, g, k // KT, k0=k % KT, k1=k % KT + 2) if first else None
                G = t * KVH
                split(0)
                scores(G, t, 0, 0)
                if not first:
                    cut_o(t - 1)
                gate(t, 0)
                scores(G + 1, t, 1, 1)
                sums(G, 0)
                norm(G, t, 0, 0)
                split(2)
                sums(G + 1, 1)
                norm(G + 1, t, 1, 1)
                split(4)
                gate(t, 1)
                gated(G, 0)
                split(6)
                scores(G + 2, t, 2, 0)
                split(8)
                gated(G + 1, 1)
                sums(G + 2, 0)
                norm(G + 2, t, 2, 0)
                cut_h(t + 1)
                split(10)
                if not first:
                    residual(t - 1, 0)
                scores(G + 3, t, 3, 1)
                sums(G + 3, 1)
                norm(G + 3, t, 3, 1)
                if not first:
                    residual(t - 1, 1)
                gated(G + 2, 2)
                split(12)
                split(14)
                gated(G + 3, 3)
            loop(dve, body)

            cut_o(TILES - 1)
            gate(TILES, 0)
            dve.wait_ge(sinkd_in, 16 * HEADS)
            dve.tensor_scalar(sinkd[:, 1:2], sinkd[:, 0:1], -1.0, None, ALU.mult).then_inc(nsink_made, 1)
            dve.tensor_scalar(ddist[:, 0:DK], ddist[:, 0:DK], ddist[:, DK:DK + 1], None, ALU.mult).then_inc(nsink_made, 1)
            dve.wait_ge(nsink_made, 4)
            dd = ddist[:, 0:DK].rearrange("p (a k) -> p a k", a=1).broadcast_to([P, GROUP, DK])
            for w in range(WAVES):
                G, b = GD + w, w % 2
                dve.wait_ge(qk_done, G + 1)
                dve.wait_ge(tp_done, G - 1)
                dve.scalar_tensor_tensor(s[:, b, :, 0:DK], ps_s[:, :, 0:DK], SCALE, dd, ALU.mult, ALU.add).then_inc(s_read, 1)
                dve.wait_ge(s_read, G + 1)
                dve.tensor_reduce(nm[:, b], s[:, b, :, 0:DK], AX_X, ALU.max, negate=True).then_inc(m_ready, 1)
                sinks(G, b, sinkd[:, 1:2].broadcast_to([P, GROUP]), sinkd[:, 0:1].broadcast_to([P, GROUP]))
                if w == 0:
                    gate(TILES, 1)
            for w in range(WAVES):
                G, b = GD + w, w % 2
                sums(G, b)
                dve.wait_ge(rden_ready, G + 1)
                for j in range(GROUP):
                    ins = dve.tensor_scalar(s[:, b, j, 0:DK], s[:, b, j, 0:DK], rden[:, b, j:j + 1], None, ALU.mult)
                ins.then_inc(pn_ready, 1)
                residual(TILES - 1, w)
            dve.wait_ge(pv_done, GD + DB)
            dve.wait_ge(szt_ready, 1)
            dve.tensor_tensor(szc[:, :, 0:DEC], ps_o[:, :].rearrange("p (k n) -> p k n", k=KT), qc[:, :, 0:DEC], ALU.mult).then_inc(od_ready, 1)
            dve.wait_ge(od_ready, 1)
            cut_o(TILES)
            residual(TILES, 0)
            residual(TILES, 1)

        @block.tensor
        def _(pe):
            def turn_h(t):
                n = rows_of(t)
                pe.wait_ge(h_ready, t + 1)
                after(pe, qt_ready, t)
                for k in range(KT):
                    ins = pe.transpose(ps_t[:, k, 0:n], hx[0:n, k * P:(k + 1) * P], g.ident[0:n, 0:n])
                ins.then_inc(th_done, 1)

            def turn_q(t):
                pe.wait_ge(q_in, 16 * (t + 1))
                pe.wait_ge(hlo_ready, t + 1)
                if isinstance(t, int) and t == TILES:
                    flat = ps_t[0:HD, :, :].rearrange("p a b -> p (a b)")
                    for h in range(HEADS):
                        ins = pe.transpose(flat[:, h * DEC:(h + 1) * DEC], q[0:DEC, h * HD:(h + 1) * HD], g.ident[0:DEC, 0:DEC])
                else:
                    for k in range(KT):
                        ins = pe.transpose(ps_t[:, k], q[:, k * P:(k + 1) * P], g.ident[:, :])
                ins.then_inc(tq_done, 1)

            def turn_k(t, p):
                n = P if isinstance(t, int) and t >= ALL else rows_of(t)
                pe.wait_ge(k_in[p], 32 * (t // 2 + 1) if isinstance(t, int) else t * 16 + (32 if p == 0 else 16))
                for h in range(KVH):
                    ins = pe.transpose(acc[:, h * P:h * P + n], kd[0:n, p, h].rearrange("p e d -> p (e d)"), g.ident[0:n, 0:n])
                ins.then_inc(tk_done, 1)

            def qk(t, kv, r):
                G = t * KVH + kv
                pe.wait_ge(qt_ready, t + 1)
                pe.wait_ge(kt_ready, t + 1)
                after(pe, s_read, G)
                for j in range(GROUP):
                    h = kv * GROUP + j
                    e = h % 2
                    for half in halves(t):
                        ins = pe.matmul(ps_s[:, place(j), half * P:(half + 1) * P], qt[e * HD:(e + 1) * HD, h // 2],
                                        kt[e * HD:(e + 1) * HD, r if half else 1 - r, kv], start=True, stop=True)
                ins.then_inc(qk_done, 1)

            def turn_p(t, kv, b):
                G = t * KVH + kv
                pe.wait_ge(p_ready, G + 1)
                after(pe, pt_ready, G)
                for j in range(GROUP):
                    for half in halves(t):
                        ins = pe.transpose(ps_p[:, half, j], s[:, b, j, half * P:(half + 1) * P], g.ident[:, :])
                ins.then_inc(tp_done, 1)

            def pv(t, kv, r, loads):
                G = t * KVH + kv
                pe.wait_ge(sn_ready, G + 1)
                after(pe, o_done, G)
                for a in range(2):
                    pe.transpose(ps_o[:, (2 + a) * P:(3 + a) * P], sz[:, (2 * kv + a) * P:(2 * kv + a + 1) * P], g.ident[:, :])
                pe.wait_ge(pt_ready, G + 1)
                if kv == 0:
                    pe.wait_ge(v_in[r], loads)
                for half in halves(t):
                    for e in range(2):
                        ins = pe.matmul(ps_o[e * HD:(e + 1) * HD, 0:2 * P], v[:, r if half else 1 - r, kv * HD:(kv + 1) * HD],
                                        pt[:, half, 2 * e:2 * e + 2], start=(half == halves(t)[0]), stop=(half == 1))
                ins.then_inc(pv_done, 1)

            def z(t, b):
                n = rows_of(t)
                pe.wait_ge(hlo_ready, t + 1)
                if b == 0:
                    pe.wait_ge(kt_ready, t + 1)
                else:
                    pe.wait_ge(zg_done, 2 * t + 1)
                project(pe, acc[0:n], ht, g.wslot[Z0 + b], n).then_inc(z_mm, 1)

            def out(t, b, gate=False):
                n = rows_of(t)
                pe.wait_ge(olo_ready, t + 1)
                if b == 0:
                    pe.wait_ge(zg_done, 2 * t + 4 if n == P else 2 * ALL)
                else:
                    pe.wait_ge(res_done, 2 * t + 1)
                project(pe, acc[0:n], ot, g.wslot[OUT0 + b], n, (g.w_lo, KT * b) if gate else None).then_inc(out_mm, 1)

            turn_h(0)
            turn_q(0)
            turn_k(0, 0)

            def body(t, r):
                first = isinstance(t, int) and t == 0
                loads = 16 * (t // 2 + 1) if isinstance(t, int) else (t * 8 + (16 if r == 0 else 8))
                qk(t, 0, r)
                z(t, 0)
                qk(t, 1, r)
                turn_p(t, 0, 0)
                z(t, 1)
                pv(t, 0, r, loads)
                qk(t, 2, r)
                turn_p(t, 1, 1)
                turn_h(t + 1)
                pv(t, 1, r, loads)
                if not first:
                    out(t - 1, 0, isinstance(t, int) and t == 1)
                qk(t, 3, r)
                turn_p(t, 2, 0)
                if not first:
                    out(t - 1, 1, isinstance(t, int) and t == 1)
                pv(t, 2, r, loads)
                turn_p(t, 3, 1)
                turn_q(t + 1)
                if first:
                    pe.wait_ge(zg_done, 2)
                else:
                    pe.wait_ge(res_done, t * 2)
                turn_k(t + 1, 1 - r)
                pv(t, 3, r, loads)
            loop(pe, body)

            z(TILES, 0)
            for w in range(WAVES):
                for j in range(GROUP):
                    b = GROUP * w + j
                    if j == 0:
                        pe.wait_ge(zg_done, 2 * TILES + 1 + w)
                        turn_k(ALL + b, (ALL + b) % 2)
                    pe.wait_ge(kt_ready, ALL + b + 1)
                    if j + 1 < GROUP:
                        turn_k(ALL + b + 1, (ALL + b + 1) % 2)
                    if j == 0:
                        after(pe, s_read, GD + w)
                    for kv in range(KVH):
                        rows = slice(kv * GROUP * DS, (kv + 1) * GROUP * DS)
                        qh = qd[:, b * P + kv * GROUP * DS:b * P + (kv + 1) * GROUP * DS]
                        pe.matmul(ps_s[rows, j, 0:P], qh, kt[0:HD, b % 2, kv], start=True, stop=True)
                        ins = pe.matmul(ps_s[rows, j, P:DK], qh, knt[0:HD, kv, b * DS:(b + 1) * DS], start=True, stop=True)
                ins.then_inc(qk_done, 1)
                if w == 0:
                    z(TILES, 1)
            pe.wait_ge(kt_ready, ALL + DB)
            out(TILES - 1, 0)
            out(TILES - 1, 1)
            pe.wait_ge(zg_done, 2 * ALL)
            pe.wait_ge(qt_ready, ALL)
            for k in range(KT):
                ins = pe.transpose(ps_t[:, k, 0:DEC], sz[0:DEC, k * P:(k + 1) * P], g.ident[0:DEC, 0:DEC])
            ins.then_inc(szt_done, 1)

            def turn_batch(b):
                w, j = divmod(b, GROUP)
                pe.wait_ge(pn_ready, w + 1)
                pe.wait_ge(pt_ready, GD + max(b - 1, 0))
                pe.transpose(ps_p[:, b % 2, 0], s[:, w % 2, j, 0:P], g.ident[:, :])
                pe.transpose(ps_p[0:DS, b % 2, 1], s[:, w % 2, j, P:DK], g.ident[:, :]).then_inc(tp_done, 1)

            turn_batch(0)
            for b in range(DB):
                if b + 1 < DB:
                    turn_batch(b + 1)
                pe.wait_ge(pt_ready, GD + b + 1)
                pe.wait_ge(v_in[b % 2], 16 * (TILES // 2 + b // 2 + 1))
                pe.wait_ge(kn_in[b % 2], 16 * (b // 2 + 1))
                if b == 0:
                    pe.wait_ge(o_done, GD)
                for kv in range(KVH):
                    for e in range(2):
                        to = ps_o[e * HD:(e + 1) * HD, :].rearrange("p (k n) -> p k n", k=KT)[:, 2 * kv:2 * kv + 2, b * DS:(b + 1) * DS]
                        col = lambda half, n: pt[0:n, b % 2, half, kv * 32:(kv + 1) * 32].rearrange("p (j i) -> p j i", i=DS)[:, e::2]
                        pe.matmul(to, v[:, b % 2, kv * HD:(kv + 1) * HD], col(0, P), start=True, stop=False)
                        ins = pe.matmul(to, vn[:, b % 2, kv * HD:(kv + 1) * HD], col(1, DS), start=False, stop=True)
                ins.then_inc(pv_done, 1)
            out(TILES, 0)
            out(TILES, 1)


def program(nc, io):
    g = Names()
    with ExitStack() as ctx:
        sb = lambda name, shape: ctx.enter_context(nc.sbuf_tensor(name, shape, F32))
        g.ident = sb("ident", [P, P])
        g.half = sb("minus_half", [P, HEADS + KVH])
        g.rms_eps = sb("rms_eps", [P, HEADS + KVH])
        g.ln_eps = sb("ln_eps", [P, 1])
        g.taps = sb("taps", [P, TAPS * KT])
        g.cols = sb("cols", [P, VECS * KT])
        g.qgain = sb("qgain", [P, 1])
        g.rstd_b = sb("rstd_b", [P, ALL])
        g.shared_slots = [ctx.enter_context(nc.sbuf_tensor(f"w{m}", [P, 2, KT, HALF], F32R)) for m in range(2)]
        scratch = lambda name, *shape: nc.dram_tensor(name, shape, F32, kind=SCRATCH).ap()
        g.c_d = scratch("c_d", D, TOK)
        g.z_d = scratch("z_d", TOK, D)
        g.v_left = scratch("v_left", D // 2, HIST + CTOK)
        g.vdec_left = scratch("vdec_left", D // 2, DB * (HIST + DS))
        g.x1_d = scratch("x1_d", TOK, D)
        g.q_d = scratch("q_d", TOK, D)
        g.kv_d = scratch("kv_d", TOK, 2 * KV)
        phase_a(nc, io, g)
        phase_b(nc, io, g)
        phase_c(nc, io, g)


SCRATCH = "Internal"
INPUTS = ("x_prompt", "x_sample", "state_conv", "cache_k", "cache_v", "norm_a", "w_in_a", "w_dw_a", "b_dw_a", "ln_g_a",
          "ln_b_a", "w_out_a", "norm_kv", "w_kv", "k_norm", "norm_b", "w_in_b", "q_norm", "sinks_b", "w_out_b")
OUTPUTS = (("y_p", (1, SEQ, D)), ("y_s", (DB, DS, D)), ("conv_p", (1, 1, HIST, D)), ("conv_s", (1, DB, HIST, D)),
           ("k_p", (1, P, KVH, HD)), ("v_p", (1, P, KVH, HD)), ("k_s", (DB, P, KVH, HD)), ("v_s", (DB, P, KVH, HD)))


def constants():
    far = 1e30
    i, j = np.arange(P)[:, None], np.arange(2 * P)[None, :]
    dist = (i + P - j).astype(np.float64)
    distance = np.where((dist >= 0) & (dist < P), dist, far).astype(np.float32)
    i, j = (np.arange(P) % DS)[:, None], np.arange(P + DS)[None, :]
    dist = (i + P - j).astype(np.float64)
    decode = np.where((dist >= 0) & (dist < P), dist, far)
    slope = -(2.0 ** (-8.0 * (np.arange(P) // DS + 1) / HEADS))[:, None]
    return {"distance": distance, "decode_distance": np.concatenate([decode, slope], 1).astype(np.float32)}


def build(nc, shapes):
    dram = lambda name, shape, kind: nc.dram_tensor(name, shape, F32, kind=kind).ap()
    a = {name: dram("in_" + name, shape, "ExternalInput") for name, shape in shapes.items()}
    o = {name: dram("out_" + name, shape, "ExternalOutput") for name, shape in OUTPUTS}
    flat = lambda ap: ap.rearrange("b w h d -> b w (h d)")
    io = Names()
    io.x_prompt = a["x_prompt"][0]
    io.x_sample = a["x_sample"].rearrange("b s d -> (b s) d")
    io.state = a["state_conv"][0]
    io.cache_k = flat(a["cache_k"])
    io.cache_v = flat(a["cache_v"])
    io.k_norm = a["k_norm"]
    io.norm_kv = a["norm_kv"]
    io.w_kv = a["w_kv"]
    io.norm_a = a["norm_a"][0]
    io.w_in_a = a["w_in_a"][0]
    io.w_dw_a = a["w_dw_a"][0]
    io.b_dw_a = a["b_dw_a"][0]
    io.ln_g_a = a["ln_g_a"][0]
    io.ln_b_a = a["ln_b_a"][0]
    io.w_out_a = a["w_out_a"][0]
    io.norm_b = a["norm_b"][0]
    io.w_in_b = a["w_in_b"][0]
    io.q_norm = a["q_norm"][0]
    io.sinks = a["sinks_b"]
    io.w_out_b = a["w_out_b"][0]
    io.distance = a["distance"]
    io.decode_distance = a["decode_distance"]
    io.y_p = o["y_p"][0]
    io.y_s = o["y_s"].rearrange("b s d -> (b s) d")
    io.conv_p = o["conv_p"][0, 0]
    io.conv_s = o["conv_s"][0]
    io.k_p = flat(o["k_p"])[0]
    io.v_p = flat(o["v_p"])[0]
    io.k_s = flat(o["k_s"])
    io.v_s = flat(o["v_s"])
    program(nc, io)


def kernel(**inputs):
    import concourse.bacc as bacc
    from concourse.bass_utils import run_bass_kernel_spmd

    nc = bacc.Bacc("TRN2", target_bir_lowering=False, num_devices=1)
    arrays = {name: np.ascontiguousarray(inputs[name]) for name in INPUTS}
    arrays.update(constants())
    build(nc, {name: array.shape for name, array in arrays.items()})
    r = run_bass_kernel_spmd(nc, [{"in_" + name: array for name, array in arrays.items()}], core_ids=[0])
    return tuple(r.results[0]["out_" + name] for name, _ in OUTPUTS)
```
